# Optimizing a Trainium2 kernel written in Bass

```python
import math
import jax, jax.numpy as jnp
from jax import lax
import numpy as np

D_MODEL = 1024
BATCH = 1
SEQ = 2048
DEPTH = 2

N_A_LAYERS = DEPTH // 2
N_B_LAYERS = DEPTH - N_A_LAYERS
CONV_WIDTH = 3
N_HEADS = 8
HEAD_DIM = 64
ATT_WIDTH = N_HEADS * HEAD_DIM
Q_BLOCK = 128
RMS_EPS = 1e-6


def _rmsnorm(x, g):
    xf = x.astype(jnp.float32)
    y = xf * lax.rsqrt(jnp.mean(xf * xf, axis=-1, keepdims=True) + RMS_EPS)
    return (y * g.astype(jnp.float32)).astype(x.dtype)

def _causal_depthwise_conv(u, w):
    return lax.conv_general_dilated(
        u, w[:, None, :].astype(u.dtype),
        window_strides=(1,),
        padding=[(CONV_WIDTH - 1, 0)],
        dimension_numbers=("NWC", "WIO", "NWC"),
        feature_group_count=u.shape[-1])

def _short_conv_mixer(h, w_in, w_conv, w_out):
    u = h @ w_in
    b_gate, c_gate, xin, g = jnp.split(u, 4, axis=-1)
    y = b_gate * _causal_depthwise_conv(c_gate * xin, w_conv)
    return (y * jax.nn.silu(g)) @ w_out

def _stick_breaking_attention(q, k, v):
    seq = q.shape[2]
    n_blocks = seq // Q_BLOCK
    scale = HEAD_DIM ** -0.5
    qf = q.astype(jnp.float32)
    kf = k.astype(jnp.float32)
    vf = v.astype(jnp.float32)
    outs = []
    for blk in range(n_blocks):
        q0 = blk * Q_BLOCK
        kl = q0 + Q_BLOCK
        qb = qf[:, :, q0:kl]
        z = jnp.einsum("bhqd,bhkd->bhqk", qb, kf[:, :, :kl]) * scale
        q_pos = q0 + jnp.arange(Q_BLOCK)
        mask = jnp.arange(kl)[None, :] < q_pos[:, None]
        log_one_minus = jnp.where(mask, jax.nn.log_sigmoid(-z), 0.0)
        rev = lax.cumsum(log_one_minus, axis=3, reverse=True)
        weights = jnp.exp(jnp.where(mask, z + rev, -jnp.inf))
        outs.append(jnp.einsum("bhqk,bhkd->bhqd", weights, vf[:, :, :kl]))
    o = jnp.concatenate(outs, axis=2)
    return o.astype(q.dtype)

def first_inputs(seed: int = 0) -> dict:
    key = jax.random.key(seed)
    ks = jax.random.split(key, 12)
    D = D_MODEL
    s = D ** -0.5
    f32 = jnp.float32
    return {
        "x": jax.random.normal(ks[0], (BATCH, SEQ, D), f32),
        "norm_a": 1.0 + 0.02 * jax.random.normal(ks[1], (N_A_LAYERS, D), f32),
        "w_in_a": s * jax.random.normal(ks[2], (N_A_LAYERS, D, 4 * D), f32),
        "conv_a": (CONV_WIDTH ** -0.5) * jax.random.normal(ks[3], (N_A_LAYERS, CONV_WIDTH, D), f32),
        "w_out_a": s * jax.random.normal(ks[4], (N_A_LAYERS, D, D), f32),
        "norm_kv": 1.0 + 0.02 * jax.random.normal(ks[5], (D,), f32),
        "w_kv": s * jax.random.normal(ks[6], (D, 2 * ATT_WIDTH), f32),
        "norm_b": 1.0 + 0.02 * jax.random.normal(ks[7], (N_B_LAYERS, D), f32),
        "w_in_b": s * jax.random.normal(ks[8], (N_B_LAYERS, D, 2 * ATT_WIDTH), f32),
        "w_out_b": (ATT_WIDTH ** -0.5) * jax.random.normal(ks[9], (N_B_LAYERS, ATT_WIDTH, D), f32),
        "norm_f": 1.0 + 0.02 * jax.random.normal(ks[10], (D,), f32),
    }

def first_block(x, norm_a, w_in_a, conv_a, w_out_a, norm_kv, w_kv, norm_b, w_in_b, w_out_b, norm_f):
    bsz, seq, _ = x.shape
    k = v = None
    for layer in range(DEPTH):
        if layer < N_A_LAYERS:
            i = layer
            h = _rmsnorm(x, norm_a[i])
            x = x + _short_conv_mixer(h, w_in_a[i], conv_a[i], w_out_a[i])
            if layer == N_A_LAYERS - 1:
                kv = _rmsnorm(x, norm_kv) @ w_kv
                k, v = jnp.split(kv, 2, axis=-1)
                k = k.reshape(bsz, seq, N_HEADS, HEAD_DIM).transpose(0, 2, 1, 3)
                v = v.reshape(bsz, seq, N_HEADS, HEAD_DIM).transpose(0, 2, 1, 3)
        else:
            j = layer - N_A_LAYERS
            h = _rmsnorm(x, norm_b[j])
            q, g = jnp.split(h @ w_in_b[j], 2, axis=-1)
            q = q.reshape(bsz, seq, N_HEADS, HEAD_DIM).transpose(0, 2, 1, 3)
            o = _stick_breaking_attention(q, k, v)
            o = o.transpose(0, 2, 1, 3).reshape(bsz, seq, ATT_WIDTH)
            x = x + (o * jax.nn.silu(g)) @ w_out_b[j]
    return _rmsnorm(x, norm_f)


DEPTH_2 = 1

D_MIX = 1024
POOL_WINDOWS = (2, 4, 8, 16)
POOL_WIDTH = 512
POOL_GROUP = POOL_WIDTH // len(POOL_WINDOWS)
N_KV_HEADS = 2
ATTN_WIDTH = N_HEADS * HEAD_DIM
KV_WIDTH = N_KV_HEADS * HEAD_DIM
N_IDX_HEADS = 8
IDX_DIM = 64
TOPK_MAX = 256
ROPE_THETA = 10000.0
EPS = 1e-6
SPLITS = (POOL_WIDTH, POOL_WIDTH, ATTN_WIDTH, KV_WIDTH, KV_WIDTH, ATTN_WIDTH,
          N_IDX_HEADS * IDX_DIM, IDX_DIM, N_IDX_HEADS)
D_IN_PROJ = 2888


def rms_norm(x, w):
    xf = x.astype(jnp.float32)
    y = xf * lax.rsqrt(jnp.mean(xf * xf, axis=-1, keepdims=True) + EPS)
    return (y * w.astype(jnp.float32)).astype(x.dtype)

def rope(x, pos):
    d = x.shape[-1]
    half = d // 2
    freqs = ROPE_THETA ** (-jnp.arange(half, dtype=jnp.float32) / half)
    ang = pos.astype(jnp.float32)[:, None] * freqs[None, :]
    cos = jnp.cos(ang)[None, :, None, :]
    sin = jnp.sin(ang)[None, :, None, :]
    xf = x.astype(jnp.float32)
    x1, x2 = xf[..., :half], xf[..., half:]
    out = jnp.concatenate([x1 * cos - x2 * sin, x2 * cos + x1 * sin], axis=-1)
    return out.astype(x.dtype)

def pool_mixer(u, w_pool, pool_scale):
    B, S, _ = u.shape
    ug = u.reshape(B, S, len(POOL_WINDOWS), POOL_GROUP).astype(jnp.float32)
    cs = jnp.cumsum(ug, axis=1)
    n_avail = jnp.arange(1, S + 1)
    means = []
    for g, w in enumerate(POOL_WINDOWS):
        csg = cs[:, :, g]
        lag = jnp.pad(csg, ((0, 0), (w, 0), (0, 0)))[:, :S]
        cnt = jnp.minimum(n_avail, w).astype(jnp.float32)[None, :, None]
        means.append((csg - lag) / cnt)
    pooled = jnp.stack(means, axis=2) - ug
    mixed = jnp.einsum('bsgc,gcd->bsgd', pooled, w_pool.astype(jnp.float32))
    mixed = mixed.reshape(B, S, POOL_WIDTH) * pool_scale.astype(jnp.float32)
    return mixed.astype(u.dtype)

def dsa_attention(q, k, v, q_idx, k_idx, w_idx):
    B, S = q.shape[0], q.shape[1]
    nb = S // Q_BLOCK
    k_top = min(TOPK_MAX, S // 4)
    grp = N_HEADS // N_KV_HEADS
    key_pos = jnp.arange(S)
    kf_idx = k_idx.astype(jnp.float32)

    def to_blocks(a):
        return jnp.moveaxis(a.reshape(B, nb, Q_BLOCK, *a.shape[2:]), 1, 0)

    def one_block(args):
        blk, qb, qib, wb = args
        q_pos = blk * Q_BLOCK + jnp.arange(Q_BLOCK)
        logits = jnp.einsum('bqhd,bsd->bqhs', qib.astype(jnp.float32), kf_idx) * (IDX_DIM ** -0.5)
        score = jnp.einsum('bqhs,bqh->bqs', jax.nn.relu(logits),
                           wb.astype(jnp.float32)) * (N_IDX_HEADS ** -0.5)
        causal = key_pos[None, :] <= q_pos[:, None]
        score = jnp.where(causal[None], score, -jnp.inf)
        _, sel = lax.top_k(score, k_top)
        valid = sel <= q_pos[None, :, None]
        k_sel = jax.vmap(lambda kk, ii: kk[ii])(k, sel)
        v_sel = jax.vmap(lambda vv, ii: vv[ii])(v, sel)
        qg = qb.reshape(B, Q_BLOCK, N_KV_HEADS, grp, HEAD_DIM).astype(jnp.float32)
        s = jnp.einsum('bqhgd,bqkhd->bqhgk', qg, k_sel.astype(jnp.float32)) * (HEAD_DIM ** -0.5)
        s = jnp.where(valid[:, :, None, None, :], s, -jnp.inf)
        p = jax.nn.softmax(s, axis=-1)
        o = jnp.einsum('bqhgk,bqkhd->bqhgd', p, v_sel.astype(jnp.float32))
        return o.reshape(B, Q_BLOCK, ATTN_WIDTH).astype(q.dtype)

    out = lax.map(one_block, (jnp.arange(nb), to_blocks(q), to_blocks(q_idx), to_blocks(w_idx)))
    return jnp.moveaxis(out, 0, 1).reshape(B, S, ATTN_WIDTH)

def second_inputs(seed: int = 0) -> dict:
    key = jax.random.key(seed)
    ks = jax.random.split(key, 12)
    f32 = jnp.float32
    x = jax.random.normal(ks[0], (BATCH, SEQ, D_MODEL), f32)
    c = jax.random.normal(ks[1], (BATCH, D_MODEL), f32)
    norm_w = 1.0 + 0.1 * jax.random.normal(ks[2], (DEPTH_2, D_MODEL), f32)
    w_ada = jax.random.normal(ks[3], (DEPTH_2, D_MODEL, 3 * D_MODEL), f32) * D_MODEL ** -0.5
    b_ada = 0.01 * jax.random.normal(ks[4], (DEPTH_2, 3 * D_MODEL), f32)
    w_in = jax.random.normal(ks[5], (DEPTH_2, D_MODEL, D_IN_PROJ), f32) * D_MODEL ** -0.5
    q_norm_w = 1.0 + 0.1 * jax.random.normal(ks[6], (DEPTH_2, HEAD_DIM), f32)
    k_norm_w = 1.0 + 0.1 * jax.random.normal(ks[7], (DEPTH_2, HEAD_DIM), f32)
    w_pool = jax.random.normal(ks[8], (DEPTH_2, len(POOL_WINDOWS), POOL_GROUP, POOL_GROUP), f32) * POOL_GROUP ** -0.5
    pool_scale = 1.0 + 0.1 * jax.random.normal(ks[9], (DEPTH_2, POOL_WIDTH), f32)
    w_out = jax.random.normal(ks[10], (DEPTH_2, D_MIX, D_MODEL), f32) * D_MIX ** -0.5
    return {"x": x, "c": c, "norm_w": norm_w, "w_ada": w_ada, "b_ada": b_ada,
            "w_in": w_in, "q_norm_w": q_norm_w, "k_norm_w": k_norm_w,
            "w_pool": w_pool, "pool_scale": pool_scale, "w_out": w_out}

def second_block(x, c, norm_w, w_ada, b_ada, w_in, q_norm_w, k_norm_w, w_pool, pool_scale, w_out):
    B, S, _ = x.shape
    pos = jnp.arange(S)
    split_points = [int(p) for p in np.cumsum(SPLITS)[:-1]]
    for l in range(DEPTH_2):
        mod = jnp.einsum('bd,de->be', jax.nn.silu(c), w_ada[l]) + b_ada[l]
        shift, scale, gate = jnp.split(mod, 3, axis=-1)
        h = rms_norm(x, norm_w[l]) * (1.0 + scale[:, None, :]) + shift[:, None, :]
        proj = jnp.einsum('bsd,de->bse', h, w_in[l])
        u_pool, g_pool, q, k, v, g_attn, qi, ki, wi = jnp.split(proj, split_points, axis=-1)
        pool_out = pool_mixer(u_pool, w_pool[l], pool_scale[l]) * jax.nn.silu(g_pool)
        q = rope(rms_norm(q.reshape(B, S, N_HEADS, HEAD_DIM), q_norm_w[l]), pos)
        k = rope(rms_norm(k.reshape(B, S, N_KV_HEADS, HEAD_DIM), k_norm_w[l]), pos)
        v = v.reshape(B, S, N_KV_HEADS, HEAD_DIM)
        qi = rope(qi.reshape(B, S, N_IDX_HEADS, IDX_DIM), pos)
        ki = rope(ki[:, :, None, :], pos)[:, :, 0, :]
        attn_out = dsa_attention(q, k, v, qi, ki, wi) * jax.nn.silu(g_attn)
        y = jnp.einsum('bse,ed->bsd', jnp.concatenate([pool_out, attn_out], axis=-1), w_out[l])
        x = x + gate[:, None, :] * y
    return x


def setup_inputs(seed=0):
    out = dict(first_inputs(seed))
    for name, value in second_inputs(seed + 1).items():
        if name != "x":
            out[name + "_2"] = value
    return out


def reference(
    x, norm_a, w_in_a, conv_a, w_out_a, norm_kv, w_kv, norm_b, w_in_b, w_out_b, norm_f, c_2,
    norm_w_2, w_ada_2, b_ada_2, w_in_2, q_norm_w_2, k_norm_w_2, w_pool_2, pool_scale_2, w_out_2,
):
    x = first_block(
        x, norm_a, w_in_a, conv_a, w_out_a, norm_kv, w_kv, norm_b, w_in_b, w_out_b, norm_f,
    )
    return second_block(
        x, c_2, norm_w_2, w_ada_2, b_ada_2, w_in_2, q_norm_w_2, k_norm_w_2, w_pool_2,
        pool_scale_2, w_out_2,
    )


_drawn_inputs = setup_inputs


def setup_inputs(seed=0):
    import zlib

    import numpy as np

    out = dict(_drawn_inputs(seed))
    spreads = {}
    factors = {'norm_kv': 6.591, 'norm_b': 6.823, 'b_ada_2': 5.373, 'q_norm_w_2': 8.0, 'k_norm_w_2': 8.0}
    for name, (base, spread) in spreads.items():
        noise = np.random.default_rng([zlib.crc32(name.encode()), seed]).standard_normal(out[name].shape)
        drawn = base * np.exp(spread * noise) if base else spread * noise
        out[name] = __import__('jax').numpy.asarray(drawn.astype(out[name].dtype))
    for name, factor in factors.items():
        out[name] = (out[name] * factor).astype(out[name].dtype)
    return out
```

```python
import concourse.bass as bass
import numpy as np
from concourse import mybir
from contextlib import ExitStack, contextmanager

F32 = mybir.dt.float32
F32R = mybir.dt.float32r
ALU = mybir.AluOpType
ACT = mybir.ActivationFunctionType

P = 128
SEQ, DM = 2048, 1024
TILES = SEQ // P
KC = DM // P
NT = SEQ // 512
EPS = 1e-6


class Alloc:

    def __init__(self, nc, ctx):
        self.nc, self.ctx = nc, ctx

    def sb(self, name, shape, dt=F32):
        return self.ctx.enter_context(self.nc.sbuf_tensor("s_" + name, shape, dt))

    def ps(self, name, shape, dt=F32):
        return self.ctx.enter_context(self.nc.psum_tensor("p_" + name, shape, dt))


def split_pass_list(w_hi, w_lo, a_hi, a_lo):
    return ((w_hi, a_hi), (w_hi, a_lo), (w_lo, a_hi))


def phase_norm_x(nc, sem, x, norm_a, ident, xt_hi, xt_lo):
    with ExitStack() as ctx:
        al = Alloc(nc, ctx)
        xin = al.sb("nx_xin", [P, 2, DM])
        xn = al.sb("nx_xn", [P, 2, DM])
        junk = al.sb("nx_junk", [P, 2, DM])
        norm_b = al.sb("nx_norm", [P, DM])
        ss = al.sb("nx_ss", [P, 8])
        root = al.sb("nx_root", [P, 8])
        rinv = al.sb("nx_rinv", [P, 8])
        eps = al.sb("nx_eps", [P, 1])
        pt = [al.ps(f"nx_pt{j}", [P, KC, P]) for j in range(2)]
        x_in = [sem(f"nx_x_in{j}") for j in range(2)]
        norm_in, ready = sem("nx_norm_in"), sem("nx_ready")
        squared, rooted, inverted, normed = sem("nx_squared"), sem("nx_rooted"), sem("nx_inverted"), sem("nx_normed")
        transposed, hi_done, lo_done = sem("nx_transposed"), sem("nx_hi_done"), sem("nx_lo_done")
        x_v = x.rearrange("(t p) d -> t p d", p=P)
        block = ctx.enter_context(nc.Block())

        @block.sync
        def _(sp):
            sp.dma_start(norm_b[:], norm_a.partition_broadcast(P)).then_inc(norm_in, 16)
            for j in range(2):
                sp.dma_start(xin[:, j], x_v[j]).then_inc(x_in[j], 16)
            with sp.Fori(1, TILES // 2) as i:
                for j in range(2):
                    sp.wait_ge(normed, i * 2 + (j - 1))
                    sp.dma_start(xin[:, j], x_v[bass.ds(i * 2 + j, 1)].rearrange("a p d -> (a p) d")).then_inc(x_in[j], 16)

        @block.gpsimd
        def _(pool):
            nc.gpsimd.memset(eps[:], EPS).then_inc(ready, 1)
            nc.gpsimd.memset(ident[:], 0.0).then_inc(ready, 1)
            pool.wait_ge(ready, 2)
            nc.gpsimd.affine_select(out=ident[:], in_=ident[:], compare_op=ALU.not_equal, fill=1.0, base=0,
                                    pattern=[[-1, P]], channel_multiplier=1).then_inc(ready, 1)

        @block.scalar
        def _(act):
            act.wait_ge(ready, 3)
            with act.Fori(0, TILES // 2) as i:
                for j in range(2):
                    act.wait_ge(x_in[j], i * 16 + 16)
                    nc.scalar.activation(junk[:, j], xin[:, j], ACT.Square, accum_out=ss[:, 4 * j:4 * j + 1]).then_inc(squared, 1)
                    act.wait_ge(squared, i * 2 + (j + 1))
                    nc.scalar.activation(root[:, 4 * j:4 * j + 1], ss[:, 4 * j:4 * j + 1], ACT.Sqrt, bias=eps[:], scale=1.0 / DM).then_inc(rooted, 1)
                for j in range(2):
                    act.wait_ge(transposed, i * 2 + (j + 1))
                    nc.scalar.activation(xt_hi[:, :, bass.ds((i * 2 + j) * P, P)], pt[j][:], ACT.Copy).then_inc(hi_done, 1)

        @block.vector
        def _(dve):
            dve.wait_ge(norm_in, 16)
            with dve.Fori(0, TILES // 2) as i:
                for j in range(2):
                    dve.wait_ge(rooted, i * 2 + (j + 1))
                    nc.vector.reciprocal(rinv[:, 4 * j:4 * j + 1], root[:, 4 * j:4 * j + 1]).then_inc(inverted, 1)
                    dve.wait_ge(inverted, i * 2 + (j + 1))
                    nc.vector.scalar_tensor_tensor(xn[:, j], xin[:, j], rinv[:, 4 * j:4 * j + 1], norm_b[:],
                                                   ALU.mult, ALU.mult).then_inc(normed, 1)
                for j in range(2):
                    dve.wait_ge(hi_done, i * 2 + (j + 1))
                    nc.vector.tensor_tensor(xt_lo[:, :, bass.ds((i * 2 + j) * P, P)], pt[j][:],
                                            xt_hi[:, :, bass.ds((i * 2 + j) * P, P)].bitcast(F32), ALU.subtract).then_inc(lo_done, 1)

        @block.tensor
        def _(pe):
            pe.wait_ge(ready, 3)
            for j in range(2):
                pe.sem_inc(lo_done, 1)
            with pe.Fori(0, TILES // 2) as i:
                for j in range(2):
                    pe.wait_ge(normed, i * 2 + (j + 1))
                    pe.wait_ge(lo_done, i * 2 + (j + 1))
                    for k in range(KC):
                        ins = nc.tensor.transpose(pt[j][:, k, :], xn[:, j, k * P:(k + 1) * P], ident[:])
                    ins.then_inc(transposed, 1)


def phase_mixer(nc, sem, w_in_a, conv_a, xt_hi, xt_lo, y_t):
    with ExitStack() as ctx:
        al = Alloc(nc, ctx)
        raw = al.sb("mx_raw", [P, 4, KC, P])
        w_hi = al.sb("mx_w_hi", [P, 4, KC, P], F32R)
        w_lo = al.sb("mx_w_lo", [P, 4, KC, P], F32R)
        c_sb = al.sb("mx_c", [P, SEQ])
        u = al.sb("mx_u", [P, SEQ + 2])
        y = al.sb("mx_y", [P, SEQ])
        cw = al.sb("mx_cw", [P, KC, 3])
        ps = [al.ps(f"mx_ps{s}", [P, SEQ]) for s in range(2)]
        ORDER = (1, 2, 3, 0)
        w_in = [sem(f"mx_w_in{j}") for j in range(4)]
        cw_in, hi_done, lo_done, product = sem("mx_cw_in"), sem("mx_hi_done"), sem("mx_lo_done"), sem("mx_product")
        c_ready, g_ready, u_ready = sem("mx_c_ready"), sem("mx_g_ready"), sem("mx_u_ready")
        chain, y_ready, y_out = sem("mx_chain"), sem("mx_y_ready"), sem("mx_y_out")
        w_v = w_in_a.rearrange("(k p) (b e n) -> b e p k n", p=P, b=4, n=P)
        y_v = y_t.rearrange("(e p) t -> e p t", p=P)
        block = ctx.enter_context(nc.Block())

        @block.sync
        def _(sp):
            with nc.allow_non_contiguous_dma(reason="three taps of each channel, once"):
                for tap in range(3):
                    sp.dma_start(cw[:, :, tap], conv_a[tap].rearrange("(e p) -> p e", p=P)).then_inc(cw_in, 16)
            for j in range(4):
                sp.dma_start(raw[:, j], w_v[ORDER[j], 0]).then_inc(w_in[j], 16)
            with sp.Fori(1, KC) as e:
                sp.wait_ge(lo_done, e * 4)
                for j in range(4):
                    sp.dma_start(raw[:, j], w_v[ORDER[j]][bass.ds(e, 1)].rearrange("a p k n -> (a p) k n")).then_inc(w_in[j], 16)
                sp.wait_ge(y_ready, e + 1)
                sp.dma_start(y_v[bass.ds(e - 1, 1)].rearrange("a p t -> (a p) t"), y[:]).then_inc(y_out, 16)
            sp.wait_ge(y_ready, KC + 1)
            sp.dma_start(y_v[KC - 1], y[:]).then_inc(y_out, 16)
            sp.wait_ge(y_out, 16 * KC + 16)

        def split_hi(act, e, j):
            act.wait_ge(w_in[j], e * 16 + 16)
            act.wait_ge(product, e * 4 + (j + 1))
            nc.scalar.activation(w_hi[:, j], raw[:, j], ACT.Copy).then_inc(hi_done, 1)

        @block.scalar
        def _(act):
            with act.Fori(0, KC) as e:
                for j in range(4):
                    split_hi(act, e, j)
                act.wait_ge(product, e * 4 + 5)
                act.wait_ge(y_ready, e + 1)
                nc.scalar.activation(c_sb[:], ps[0][:], ACT.Copy).then_inc(c_ready, 1)
                act.wait_ge(product, e * 4 + 7)
                act.wait_ge(u_ready, e + 1)
                nc.scalar.activation(c_sb[:], ps[0][:], ACT.Silu).then_inc(g_ready, 1)

        @block.vector
        def _(dve):
            nc.vector.memset(u[:, 0:2], 0.0)
            dve.wait_ge(cw_in, 48)
            with dve.Fori(0, KC) as e:
                for j in range(4):
                    dve.wait_ge(hi_done, e * 4 + (j + 1))
                    nc.vector.tensor_tensor(w_lo[:, j], raw[:, j], w_hi[:, j].bitcast(F32), ALU.subtract).then_inc(lo_done, 1)
                dve.wait_ge(product, e * 4 + 6)
                dve.wait_ge(c_ready, e + 1)
                nc.vector.tensor_tensor(u[:, 2:], ps[1][:], c_sb[:], ALU.mult).then_inc(u_ready, 1)
                dve.wait_ge(u_ready, e + 1)
                dve.wait_ge(y_out, e * 16 + 16)
                taps = cw[:, bass.ds(e, 1), :].rearrange("p a n -> p (a n)")
                nc.vector.tensor_scalar(y[:], u[:, 0:SEQ], taps[:, 0:1], None, ALU.mult).then_inc(chain, 1)
                for tap in (1, 2):
                    dve.wait_ge(chain, e * 4 + tap)
                    nc.vector.scalar_tensor_tensor(y[:], u[:, tap:tap + SEQ], taps[:, tap:tap + 1], y[:],
                                                   ALU.mult, ALU.add).then_inc(chain, 1)
                dve.wait_ge(chain, e * 4 + 3)
                dve.wait_ge(g_ready, e + 2)
                nc.vector.tensor_tensor(y[:], y[:], c_sb[:], ALU.mult).then_inc(chain, 1)
                dve.wait_ge(chain, e * 4 + 4)
                dve.wait_ge(product, e * 4 + 8)
                nc.vector.tensor_tensor(y[:], y[:], ps[1][:], ALU.mult).then_inc(y_ready, 1)

        @block.tensor
        def _(pe):
            pe.sem_inc(product, 4)
            pe.sem_inc(y_out, 16)
            pe.sem_inc(y_ready, 1)
            pe.sem_inc(g_ready, 1)
            with pe.Fori(0, KC) as e:
                for j in range(4):
                    pe.wait_ge(lo_done, e * 4 + (j + 1))
                    left, before = ((g_ready, 1), (y_ready, 1), (c_ready, 1), (u_ready, 1))[j]
                    pe.wait_ge(left, e + before)
                    for k in range(KC):
                        for n, (w, a) in enumerate(split_pass_list(w_hi, w_lo, xt_hi, xt_lo)):
                            for t in range(NT):
                                ins = nc.tensor.matmul(ps[j % 2][:, t * 512:(t + 1) * 512], w[:, j, k, :], a[:, k, t * 512:(t + 1) * 512],
                                                       start=(k == 0 and n == 0), stop=(k == KC - 1 and n == 2))
                    ins.then_inc(product, 1)
def phase_out_a(nc, sem, x, w_out_a, y_t, ident, x1, xn_t):
    with ExitStack() as ctx:
        al = Alloc(nc, ctx)
        w_raw = al.sb("oa_w_raw", [P, 2, DM])
        w_hi = al.sb("oa_w_hi", [P, KC, DM], F32R)
        w_lo = al.sb("oa_w_lo", [P, KC, DM], F32R)
        y_raw = al.sb("oa_y_raw", [P, 2, KC, P])
        y_hi = al.sb("oa_y_hi", [P, 2, KC, P], F32R)
        y_lo = al.sb("oa_y_lo", [P, 2, KC, P], F32R)
        xin = al.sb("oa_x", [P, 2, DM])
        xo = al.sb("oa_x1", [P, 2, DM])
        xn = al.sb("oa_xn", [P, 2, DM])
        junk = al.sb("oa_junk", [P, 2, DM])
        stage = al.sb("oa_stage", [P, 2, KC, P])
        eps = al.sb("oa_eps", [P, 1])
        ss = al.sb("oa_ss", [P, 8])
        root = al.sb("oa_root", [P, 8])
        rinv = al.sb("oa_rinv", [P, 8])
        acc = [al.ps(f"oa_acc{j}", [P, DM]) for j in range(2)]
        pt = [al.ps(f"oa_pt{j}", [P, KC, P]) for j in range(2)]
        w_in = [sem(f"oa_w_in{j}") for j in range(2)]
        y_in = [sem(f"oa_y_in{j}") for j in range(2)]
        x_in = [sem(f"oa_x_in{j}") for j in range(2)]
        x1_out = [sem(f"oa_x1_out{j}") for j in range(2)]
        t_out = [sem(f"oa_t_out{j}") for j in range(2)]
        w_hi_done, w_lo_done, y_hi_done, y_lo_done = sem("oa_w_hi"), sem("oa_w_lo"), sem("oa_y_hi"), sem("oa_y_lo")
        product, added, squared, rooted = sem("oa_product"), sem("oa_added"), sem("oa_squared"), sem("oa_rooted")
        inverted, normed, transposed, staged, ready = (sem("oa_inverted"), sem("oa_normed"), sem("oa_transposed"),
                                                       sem("oa_staged"), sem("oa_ready"))
        w_v = w_out_a.rearrange("(k p) n -> k p n", p=P)
        y_v = y_t.rearrange("(k p) (t n) -> t p k n", p=P, n=P)
        x_v = x.rearrange("(t p) d -> t p d", p=P)
        x1_v = x1.rearrange("(t p) d -> t p d", p=P)
        xn_v = xn_t.rearrange("(k p) (t n) -> t p k n", p=P, n=P)
        PAIRS = TILES // 2
        block = ctx.enter_context(nc.Block())

        @block.sync
        def _(sp):
            def load(tile_y, tile_x, j):
                sp.dma_start(y_raw[:, j], tile_y).then_inc(y_in[j], 16)
                sp.dma_start(xin[:, j], tile_x).then_inc(x_in[j], 16)

            for j in range(2):
                load(y_v[j], x_v[j], j)
            for k in range(KC):
                if k >= 2:
                    sp.wait_ge(w_lo_done, k - 1)
                sp.dma_start(w_raw[:, k % 2], w_v[k]).then_inc(w_in[k % 2], 16)
            with sp.Fori(0, PAIRS - 1) as i:
                for j in range(2):
                    sp.wait_ge(added, i * 2 + (j + 3))
                    sp.dma_start(x1_v[bass.ds(i * 2 + j, 1)].rearrange("a p d -> (a p) d"), xo[:, j]).then_inc(x1_out[j], 16)
                    sp.wait_ge(y_lo_done, i * 2 + (j + 1))
                    load(y_v[bass.ds(i * 2 + (j + 2), 1)].rearrange("a p k n -> (a p) k n"),
                         x_v[bass.ds(i * 2 + (j + 2), 1)].rearrange("a p d -> (a p) d"), j)
            for j in range(2):
                sp.wait_ge(added, TILES + j + 1)
                sp.dma_start(x1_v[TILES - 2 + j], xo[:, j]).then_inc(x1_out[j], 16)
            for j in range(2):
                sp.wait_ge(x1_out[j], 16 * PAIRS + 16)
                sp.wait_ge(t_out[j], 16 * PAIRS + 16)

        @block.gpsimd
        def _(pool):
            nc.gpsimd.memset(eps[:], EPS).then_inc(ready, 1)

        @block.scalar
        def _(act):
            nc.scalar.preload_act_table(ACT.Sqrt)
            act.wait_ge(ready, 1)

            def hi(t, j):
                act.wait_ge(y_in[j], (t - j) * 8 + 16)
                act.wait_ge(product, t + 1)
                nc.scalar.activation(y_hi[:, j], y_raw[:, j], ACT.Copy).then_inc(y_hi_done, 1)

            def stats(t, j):
                act.wait_ge(added, t + 3)
                nc.scalar.activation(junk[:, j], xo[:, j], ACT.Square, accum_out=ss[:, 4 * j:4 * j + 1]).then_inc(squared, 1)
                act.wait_ge(squared, t + 1)
                nc.scalar.activation(root[:, 4 * j:4 * j + 1], ss[:, 4 * j:4 * j + 1], ACT.Sqrt, bias=eps[:], scale=1.0 / DM).then_inc(rooted, 1)

            def leave(t, j):
                act.wait_ge(transposed, t + 3)
                act.wait_ge(t_out[j], (t - j) * 8 + 16)
                nc.scalar.activation(stage[:, j], pt[j][:], ACT.Copy).then_inc(staged, 1)
                act.wait_ge(staged, t + 1)
                act.dma_start(xn_v[bass.ds(t, 1)].rearrange("a p k n -> (a p) k n"), stage[:, j]).then_inc(t_out[j], 16)

            for k in range(KC):
                act.wait_ge(w_in[k % 2], 16 * (k // 2 + 1))
                nc.scalar.activation(w_hi[:, k], w_raw[:, k % 2], ACT.Copy).then_inc(w_hi_done, 1)
            for j in range(2):
                hi(j, j)
            with act.Fori(0, PAIRS - 1) as i:
                for j in range(2):
                    stats(i * 2 + j, j)
                    hi(i * 2 + (j + 2), j)
                    leave(i * 2 + j, j)
            for j in range(2):
                stats(TILES - 2 + j, j)
                leave(TILES - 2 + j, j)

        @block.vector
        def _(dve):
            for k in range(KC):
                dve.wait_ge(w_hi_done, k + 1)
                nc.vector.tensor_tensor(w_lo[:, k], w_raw[:, k % 2], w_hi[:, k].bitcast(F32), ALU.subtract).then_inc(w_lo_done, 1)

            def lo(t, j):
                dve.wait_ge(y_hi_done, t + 1)
                nc.vector.tensor_tensor(y_lo[:, j], y_raw[:, j], y_hi[:, j].bitcast(F32), ALU.subtract).then_inc(y_lo_done, 1)

            def add(t, j):
                dve.wait_ge(product, t + 3)
                dve.wait_ge(x_in[j], (t - j) * 8 + 16)
                dve.wait_ge(x1_out[j], (t - j) * 8 + 16)
                nc.vector.tensor_tensor(xo[:, j], acc[j][:], xin[:, j], ALU.add).then_inc(added, 1)

            def norm(t, j):
                dve.wait_ge(rooted, t + 1)
                nc.vector.reciprocal(rinv[:, 4 * j:4 * j + 1], root[:, 4 * j:4 * j + 1]).then_inc(inverted, 1)
                dve.wait_ge(inverted, t + 1)
                dve.wait_ge(transposed, t + 1)
                nc.vector.tensor_scalar(xn[:, j], xo[:, j], rinv[:, 4 * j:4 * j + 1], None, ALU.mult).then_inc(normed, 1)

            for j in range(2):
                lo(j, j)
            with dve.Fori(0, PAIRS - 1) as i:
                for j in range(2):
                    add(i * 2 + j, j)
                    lo(i * 2 + (j + 2), j)
                    norm(i * 2 + j, j)
            for j in range(2):
                add(TILES - 2 + j, j)
                norm(TILES - 2 + j, j)

        @block.tensor
        def _(pe):
            pe.sem_inc(product, 2)
            pe.sem_inc(added, 2)
            pe.sem_inc(transposed, 2)
            for j in range(2):
                pe.sem_inc(x1_out[j], 16)
                pe.sem_inc(t_out[j], 16)

            def multiply(t, j):
                pe.wait_ge(y_lo_done, t + 1)
                pe.wait_ge(added, t + 1)
                for half in range(2):
                    cols = slice(half * 512, half * 512 + 512)
                    for k in range(KC):
                        for n, (w, a) in enumerate(split_pass_list(w_hi, w_lo, y_hi, y_lo)):
                            ins = nc.tensor.matmul(acc[j][:, cols], a[:, j, k, :], w[:, k, cols],
                                                   start=(k == 0 and n == 0), stop=(k == KC - 1 and n == 2))
                ins.then_inc(product, 1)

            def transpose(t, j):
                pe.wait_ge(normed, t + 1)
                pe.wait_ge(t_out[j], (t - j) * 8 + 16)
                for k in range(KC):
                    ins = nc.tensor.transpose(pt[j][:, k, :], xn[:, j, k * P:(k + 1) * P], ident[:])
                ins.then_inc(transposed, 1)

            pe.wait_ge(w_lo_done, KC)
            multiply(0, 0)
            with pe.Fori(0, PAIRS - 1) as i:
                multiply(i * 2 + 1, 1)
                transpose(i * 2, 0)
                multiply(i * 2 + 2, 0)
                transpose(i * 2 + 1, 1)
            multiply(TILES - 1, 1)
            transpose(TILES - 2, 0)
            transpose(TILES - 1, 1)


def phase_project(nc, sem, pre, weights, norms, xt_hi, xt_lo, out_t, xt_src=None):
    with ExitStack() as ctx:
        al = Alloc(nc, ctx)
        raw = al.sb(pre + "_raw", [P, 2, KC, P])
        w_hi = al.sb(pre + "_w_hi", [P, 2, KC, P], F32R)
        w_lo = al.sb(pre + "_w_lo", [P, 2, KC, P], F32R)
        stage = al.sb(pre + "_stage", [P, 2, SEQ])
        x_raw = al.sb(pre + "_x_raw", [P, 2, SEQ]) if xt_src is not None else None
        scale = al.sb(pre + "_scale", [P, len(weights), KC])
        ps = [al.ps(f"{pre}_ps{j}", [P, SEQ]) for j in range(2)]
        w_in = [sem(f"{pre}_w_in{j}") for j in range(2)]
        x_in = [sem(f"{pre}_x_in{j}") for j in range(2)]
        out_done = [sem(f"{pre}_out{j}") for j in range(2)]
        n_in, scaled, hi_done, lo_done = sem(pre + "_n_in"), sem(pre + "_scaled"), sem(pre + "_hi"), sem(pre + "_lo")
        x_hi, x_lo, product, staged = sem(pre + "_x_hi"), sem(pre + "_x_lo"), sem(pre + "_product"), sem(pre + "_staged")
        w_v, base, blocks, tails = [], [], [], []
        at = 0
        for w in weights:
            full = w.shape[1] // P // 2 * 2
            w_v.append(w[:, :full * P].rearrange("(k p) (b n) -> b p k n", p=P, n=P))
            base.append(at)
            blocks.append(full)
            at += full
        tail = weights[-1].shape[1] - blocks[-1] * P
        assert tail < P
        tail_v = weights[-1][:, blocks[-1] * P:].rearrange("(k p) n -> p k n", p=P)
        total = at
        out_v = out_t[0:total * P, :].rearrange("(b p) t -> b p t", p=P)
        block = ctx.enter_context(nc.Block())

        @block.sync
        def _(sp):
            with nc.allow_non_contiguous_dma(reason="a norm's weight, once"):
                for n, norm in enumerate(norms):
                    if norm is not None:
                        sp.dma_start(scale[:, n], norm.rearrange("(k p) -> p k", p=P)).then_inc(n_in, 16)
            for j in range(2):
                sp.dma_start(raw[:, j], w_v[0][j]).then_inc(w_in[j], 16)
            if xt_src is not None:
                x_v = xt_src.rearrange("(k p) t -> k p t", p=P)
                for k in range(KC):
                    if k >= 2:
                        sp.wait_ge(x_lo, k - 1)
                    sp.dma_start(x_raw[:, k % 2], x_v[k]).then_inc(x_in[k % 2], 16)

            def store(b, j):
                sp.wait_ge(staged, b + 3)
                sp.dma_start(out_v[bass.ds(b, 1)].rearrange("a p t -> (a p) t"), stage[:, j]).then_inc(out_done[j], 16)

            for n in range(len(weights)):
                with sp.Fori(0, blocks[n] // 2 - 1) as i:
                    for j in range(2):
                        sp.wait_ge(lo_done, i * 2 + (base[n] + j + 1))
                        sp.dma_start(raw[:, j], w_v[n][bass.ds(i * 2 + (j + 2), 1)].rearrange("a p k n -> (a p) k n")).then_inc(w_in[j], 16)
                        store(i * 2 + (base[n] + j), j)
                for j in range(2):
                    sp.wait_ge(lo_done, base[n] + blocks[n] - 1 + j)
                    if n + 1 < len(weights):
                        sp.dma_start(raw[:, j], w_v[n + 1][j]).then_inc(w_in[j], 16)
                    elif tail and j == 0:
                        sp.dma_start(raw[:, j, :, 0:tail], tail_v).then_inc(w_in[j], 16)
                    store(base[n] + blocks[n] - 2 + j, j)
            if tail:
                sp.wait_ge(staged, total + 3)
                sp.dma_start(out_t[total * P:total * P + tail, :], stage[0:tail, 0]).then_inc(out_done[0], 16)
            for j in range(2):
                sp.wait_ge(out_done[j], 8 * total + 16 + (16 if tail and j == 0 else 0))

        def each_block(eng, body):
            for n in range(len(weights)):
                with eng.Fori(0, blocks[n] // 2) as i:
                    for j in range(2):
                        body(i * 2 + (base[n] + j), j, n, P)
            if tail:
                body(total, 0, len(weights) - 1, tail)

        @block.scalar
        def _(act):
            if xt_src is not None:
                for k in range(KC):
                    act.wait_ge(x_in[k % 2], 16 * (k // 2 + 1))
                    nc.scalar.activation(xt_hi[:, k], x_raw[:, k % 2], ACT.Copy).then_inc(x_hi, 1)

            def body(b, j, n, cols):
                if norms[n] is not None:
                    act.wait_ge(scaled, b + 1)
                else:
                    act.wait_ge(w_in[j], (b - j) * 8 + 16)
                act.wait_ge(product, b + 1)
                nc.scalar.activation(w_hi[:, j, :, 0:cols], raw[:, j, :, 0:cols], ACT.Copy).then_inc(hi_done, 1)

            each_block(act, body)

        @block.vector
        def _(dve):
            for n, norm in enumerate(norms):
                if norm is not None:
                    dve.wait_ge(n_in, 16 * sum(x is not None for x in norms))
            if xt_src is not None:
                for k in range(KC):
                    dve.wait_ge(x_hi, k + 1)
                    nc.vector.tensor_tensor(xt_lo[:, k], x_raw[:, k % 2], xt_hi[:, k].bitcast(F32), ALU.subtract).then_inc(x_lo, 1)

            def split(b, j, n, cols):
                if norms[n] is not None:
                    dve.wait_ge(w_in[j], (b - j) * 8 + 16)
                    nc.vector.tensor_tensor(raw[:, j], raw[:, j], scale[:, n].unsqueeze(2).to_broadcast([P, KC, P]), ALU.mult).then_inc(scaled, 1)
                    dve.wait_ge(scaled, b + 1)
                dve.wait_ge(hi_done, b + 1)
                nc.vector.tensor_tensor(w_lo[:, j, :, 0:cols], raw[:, j, :, 0:cols], w_hi[:, j, :, 0:cols].bitcast(F32), ALU.subtract).then_inc(lo_done, 1)

            def leave(b, j, cols):
                dve.wait_ge(product, b + 3)
                dve.wait_ge(out_done[j], (b - j) * 8 + 16)
                nc.vector.tensor_copy(stage[0:cols, j], ps[j][0:cols, :]).then_inc(staged, 1)

            split(0, 0, 0, P)
            for n in range(len(weights)):
                with dve.Fori(0, blocks[n] // 2 - 1) as i:
                    split(i * 2 + (base[n] + 1), 1, n, P)
                    leave(i * 2 + base[n], 0, P)
                    split(i * 2 + (base[n] + 2), 0, n, P)
                    leave(i * 2 + (base[n] + 1), 1, P)
                last = base[n] + blocks[n] - 2
                split(last + 1, 1, n, P)
                leave(last, 0, P)
                if n + 1 < len(weights):
                    split(last + 2, 0, n + 1, P)
                elif tail:
                    split(last + 2, 0, n, tail)
                leave(last + 1, 1, P)
            if tail:
                leave(total, 0, tail)

        @block.tensor
        def _(pe):
            pe.sem_inc(product, 2)
            pe.sem_inc(staged, 2)
            for j in range(2):
                pe.sem_inc(out_done[j], 16)

            def body(b, j, n, cols):
                pe.wait_ge(lo_done, b + 1)
                pe.wait_ge(staged, b + 1)
                for k in range(KC):
                    if xt_src is not None:
                        pe.wait_ge(x_lo, k + 1)
                    for m, (w, a) in enumerate(split_pass_list(w_hi, w_lo, xt_hi, xt_lo)):
                        for t in range(NT):
                            ins = nc.tensor.matmul(ps[j][0:cols, t * 512:(t + 1) * 512], w[:, j, k, 0:cols], a[:, k, t * 512:(t + 1) * 512],
                                                   start=(k == 0 and m == 0), stop=(k == KC - 1 and m == 2))
                ins.then_inc(product, 1)

            each_block(pe, body)
HD = 64
HEADS = 8
CHUNK = 1024


def chunks_of(qb):
    n = P * (qb + 1)
    return [(at, min(CHUNK, n - at)) for at in range(0, n, CHUNK)][::-1]


def phase_stick(nc, sem, kvqg_t, o_t, ident):
    ATT = HEADS * HD
    SCALE = HD ** -0.5
    CAP = 20.0
    FAR = -float(2 ** 100)
    units = [(qb, s, at, n) for qb in range(TILES) for s in range(2) for at, n in chunks_of(qb)]
    U = len(units)
    groups = [[(g, min(512, n - g)) for g in range(0, n, 512)] for _, _, _, n in units]
    G = sum(map(len, groups))
    g_base = [sum(map(len, groups[:u])) for u in range(U)]
    O = TILES * 2
    last_of = [u for u in range(U) if u + 1 == U or units[u][:2] != units[u + 1][:2]]
    with ExitStack() as ctx:
        al = Alloc(nc, ctx)
        k_raw = al.sb("st_k_raw", [P, 2, SEQ])
        q_raw = al.sb("st_q_raw", [P, 2, SEQ])
        v_raw = al.sb("st_v_raw", [P, SEQ])
        k_hi = al.sb("st_k_hi", [P, 2, SEQ], F32R)
        k_lo = al.sb("st_k_lo", [P, 2, SEQ], F32R)
        q_two = al.sb("st_q_two", [P, 2, SEQ], F32R)
        v_nat = al.sb("st_v_nat", [P, TILES, P])
        soft = al.sb("st_soft", [P, 2, CHUNK])
        csum = al.sb("st_csum", [P, 2, CHUNK])
        arg = al.sb("st_arg", [P, 2, CHUNK])
        prob = al.sb("st_prob", [P, 2, 512])
        o_sb = al.sb("st_o", [HD, 2, SEQ])
        ident_r = al.sb("st_ident_r", [P, P], F32R)
        far = al.sb("st_far", [P, P])
        far_r = al.sb("st_far_r", [P, P], F32R)
        z = [al.ps(f"st_z{j}", [P, CHUNK]) for j in range(2)]
        turn = [al.ps(f"st_turn{j}", [P, 512]) for j in range(2)]
        o_ps = [al.ps(f"st_o{j}", [HD, P]) for j in range(2)]
        k_in, q_in, v_in = sem("st_k_in"), sem("st_q_in"), sem("st_v_in")
        far_ready, const_ready = sem("st_far_ready"), sem("st_const_ready")
        kh_done, kl_done, qh_done, ql_done = sem("st_kh"), sem("st_kl"), sem("st_qh"), sem("st_ql")
        v_turned, v_ready = sem("st_v_turned"), sem("st_v_ready")
        z_ready, capped, exped, logged = sem("st_z_ready"), sem("st_capped"), sem("st_exped"), sem("st_logged")
        softened, summed, arg_ready = sem("st_softened"), sem("st_summed"), sem("st_arg_ready")
        turned, p_ready, weighed = sem("st_turned"), sem("st_p_ready"), sem("st_weighed")
        o_left, o_out = sem("st_o_left"), sem("st_o_out")
        rows = kvqg_t.rearrange("(w b p) t -> w b p t", w=4, p=P)
        o_v = o_t.rearrange("(b s p) t -> b s p t", s=2, p=HD)
        PAIRS = HEADS // 2
        block = ctx.enter_context(nc.Block())

        @block.sync
        def _(sp):
            def load(pair, row):
                sp.wait_ge(kl_done, pair * 2 + 2)
                sp.wait_ge(ql_done, pair * 2 + 2)
                for s in range(2):
                    for half in range(2):
                        for buf, w, done in ((k_raw, 0, k_in), (q_raw, 2, q_in)):
                            sp.dma_start(buf[half * HD:half * HD + HD, s], row(w)[s * HD:s * HD + HD, :]).then_inc(done, 16)
                sp.wait_ge(v_turned, pair * 2 + 2)
                sp.dma_start(v_raw[:], row(1)).then_inc(v_in, 16)

            def store(pair, out):
                sp.wait_ge(o_left, pair * O + (O + 2))
                for s in range(2):
                    sp.dma_start(out(s), o_sb[:, s]).then_inc(o_out, 16)

            load(0, lambda w: rows[w][0])
            with sp.Fori(0, PAIRS - 1) as i:
                load(i + 1, lambda w: rows[w][bass.ds(i + 1, 1)].rearrange("a p t -> (a p) t"))
                store(i, lambda s: o_v[bass.ds(i, 1), s].rearrange("a p t -> (a p) t"))
            store(PAIRS - 1, lambda s: o_v[PAIRS - 1, s])
            sp.wait_ge(o_out, 32 * PAIRS + 32)

        @block.gpsimd
        def _(pool):
            nc.gpsimd.memset(far[:], 0.0).then_inc(far_ready, 1)
            pool.wait_ge(far_ready, 1)
            nc.gpsimd.affine_select(out=far[:], in_=far[:], compare_op=ALU.is_gt, fill=FAR, base=0,
                                    pattern=[[-1, P]], channel_multiplier=1).then_inc(far_ready, 1)

        @block.scalar
        def _(act):
            nc.scalar.preload_act_table_set("natural_log_exp_and_others")
            nc.scalar.activation(ident_r[:], ident[:], ACT.Copy).then_inc(const_ready, 1)
            act.wait_ge(far_ready, 2)
            nc.scalar.activation(far_r[:], far[:], ACT.Copy).then_inc(const_ready, 1)
            with act.Fori(0, PAIRS) as i:
                act.wait_ge(z_ready, i * U + 2)
                act.wait_ge(k_in, i * 64 + 64)
                act.wait_ge(q_in, i * 64 + 64)
                for s in range(2):
                    nc.scalar.activation(k_hi[:, s], k_raw[:, s], ACT.Copy).then_inc(kh_done, 1)
                    nc.scalar.activation(q_two[:, s], q_raw[:, s], ACT.Copy, scale=SCALE).then_inc(qh_done, 1)
                act.wait_ge(weighed, i * G + 2)
                for j in range(2):
                    act.wait_ge(v_turned, i * 2 + (j + 3))
                    nc.scalar.activation(v_nat[:, j * 8:j * 8 + 8].rearrange("p a b -> p (a b)"), z[j][:], ACT.Copy).then_inc(v_ready, 1)

                def softplus(u):
                    n = units[u][3]
                    act.wait_ge(capped, i * U + (u + 1))
                    nc.scalar.activation(soft[:, u % 2, 0:n], soft[:, u % 2, 0:n], ACT.Exp).then_inc(exped, 1)
                    act.wait_ge(exped, i * U + (u + 1))
                    nc.scalar.activation(soft[:, u % 2, 0:n], soft[:, u % 2, 0:n], ACT.Ln, bias=1.0).then_inc(logged, 1)

                softplus(0)
                for u in range(U):
                    if u + 1 < U:
                        softplus(u + 1)
                    for m, (_, w) in enumerate(groups[u]):
                        g = g_base[u] + m
                        act.wait_ge(turned, i * G + (g + 1))
                        act.wait_ge(weighed, i * G + (g + 1))
                        nc.scalar.activation(prob[:, g % 2, 0:w], turn[g % 2][:, 0:w], ACT.Exp).then_inc(p_ready, 1)

        @block.vector
        def _(dve):
            with dve.Fori(0, PAIRS) as i:
                for s in range(2):
                    dve.wait_ge(kh_done, i * 2 + (s + 1))
                    nc.vector.tensor_tensor(k_lo[:, s], k_raw[:, s], k_hi[:, s].bitcast(F32), ALU.subtract).then_inc(kl_done, 1)
                    dve.wait_ge(qh_done, i * 2 + (s + 1))
                    nc.vector.scalar_tensor_tensor(q_two[HD:P, s], q_raw[HD:P, s], SCALE, q_two[HD:P, s].bitcast(F32),
                                                   ALU.mult, ALU.subtract).then_inc(ql_done, 1)

                def cap(u):
                    n = units[u][3]
                    dve.wait_ge(z_ready, i * U + (u + 3))
                    dve.wait_ge(summed, i * U + (u + 1))
                    nc.vector.tensor_scalar(soft[:, u % 2, 0:n], z[u % 2][:, 0:n], CAP, None, ALU.min).then_inc(capped, 1)

                def leave(u):
                    qb, s = units[u][:2]
                    done = last_of.index(u)
                    dve.wait_ge(weighed, i * G + (g_base[u] + len(groups[u]) + 2))
                    nc.vector.tensor_copy(o_sb[:, s, qb * P:qb * P + P], o_ps[done % 2][:]).then_inc(o_left, 1)

                cap(0)
                for u, (qb, s, at, n) in enumerate(units):
                    b = u % 2
                    dve.wait_ge(logged, i * U + (u + 1))
                    nc.vector.tensor_tensor(soft[:, b, 0:n], soft[:, b, 0:n], z[b][:, 0:n], ALU.max).then_inc(softened, 1)
                    if u + 1 < U:
                        cap(u + 1)
                    dve.wait_ge(softened, i * U + (u + 1))
                    dve.wait_ge(arg_ready, i * U + (u + 1))
                    if at + n == P * (qb + 1):
                        carry = 0.0
                    else:
                        dve.wait_ge(summed, i * U + (u + 2))
                        carry = csum[:, 1 - b, 0:1]
                    back = soft[:, b, 0:n][:, ::-1]
                    nc.vector.tensor_tensor_scan(csum[:, b, 0:n][:, ::-1], back, back, carry, ALU.add, ALU.bypass).then_inc(summed, 1)
                    dve.wait_ge(summed, i * U + (u + 3))
                    if u >= 2:
                        dve.wait_ge(turned, i * G + g_base[u - 1])
                    nc.vector.tensor_tensor(arg[:, b, 0:n], z[b][:, 0:n], csum[:, b, 0:n], ALU.subtract).then_inc(arg_ready, 1)
                    if u == 1:
                        dve.wait_ge(o_out, i * 32 + 32)
                    if u >= 1 and u - 1 in last_of:
                        leave(u - 1)
                leave(U - 1)

        @block.tensor
        def _(pe):
            for s, n in ((kl_done, 2), (ql_done, 2), (v_turned, 2), (z_ready, 2), (summed, 2), (arg_ready, 2),
                         (weighed, 2), (p_ready, 2), (o_left, 2), (o_out, 32)):
                pe.sem_inc(s, n)
            pe.wait_ge(const_ready, 2)
            with pe.Fori(0, PAIRS) as i:
                pe.wait_ge(v_in, i * 16 + 16)
                pe.wait_ge(arg_ready, i * U + 2)
                for j in range(2):
                    for t in range(8):
                        ins = nc.tensor.transpose(z[j][:, t * P:t * P + P], v_raw[:, (j * 8 + t) * P:(j * 8 + t + 1) * P], ident[:])
                    ins.then_inc(v_turned, 1)
                pe.wait_ge(kl_done, i * 2 + 4)
                pe.wait_ge(ql_done, i * 2 + 4)

                def scores(u):
                    qb, s, at, n = units[u]
                    if u < 2:
                        pe.wait_ge(v_ready, i * 2 + (u + 1))
                    pe.wait_ge(arg_ready, i * U + (u + 1))
                    for g, w in groups[u]:
                        q = q_two[:, s, qb * P:qb * P + P]
                        diagonal = at + g + w == P * (qb + 1)
                        nc.tensor.matmul(z[u % 2][:, g:g + w], q, k_hi[:, s, at + g:at + g + w], start=True, stop=False)
                        ins = nc.tensor.matmul(z[u % 2][:, g:g + w], q, k_lo[:, s, at + g:at + g + w], start=False, stop=not diagonal)
                        if diagonal:
                            ins = nc.tensor.matmul(z[u % 2][:, g + w - P:g + w], ident_r[:], far_r[:], start=False, stop=True)
                    ins.then_inc(z_ready, 1)

                scores(0)
                scores(1)
                for u, (qb, s, at, n) in enumerate(units):
                    pe.wait_ge(arg_ready, i * U + (u + 3))
                    for m, (g0, w) in enumerate(groups[u]):
                        g = g_base[u] + m
                        pe.wait_ge(p_ready, i * G + (g + 1))
                        for c in range(0, w, P):
                            ins = nc.tensor.transpose(turn[g % 2][:, c:c + P], arg[:, u % 2, g0 + c:g0 + c + P], ident[:])
                        ins.then_inc(turned, 1)
                    if u + 2 < U:
                        scores(u + 2)
                    done = sum(x < u for x in last_of)
                    first = u == 0 or u - 1 in last_of
                    if first:
                        pe.wait_ge(o_left, i * O + (done + 1))
                    for m, (g0, w) in enumerate(groups[u]):
                        g = g_base[u] + m
                        pe.wait_ge(p_ready, i * G + (g + 3))
                        for c in range(0, w, P):
                            ins = nc.tensor.matmul(o_ps[done % 2][:], v_nat[:, (at + g0 + c) // P, s * HD:s * HD + HD], prob[:, g % 2, c:c + P],
                                                   start=first and m == 0 and c == 0,
                                                   stop=u in last_of and m == len(groups[u]) - 1 and c + P == w)
                        ins.then_inc(weighed, 1)
def phase_modulation(nc, sem, c_in, w_ada, b_ada, norm_w, shift, scale_w, gate_row):
    PARTS = 2
    W = 3 * DM // PARTS
    with ExitStack() as ctx:
        al = Alloc(nc, ctx)
        c_col = al.sb("mo_c", [P, KC])
        c_silu = al.sb("mo_silu", [P, KC])
        c_wide = al.sb("mo_c_wide", [P, KC, P])
        w = al.sb("mo_w", [P, 4, W])
        bias = al.sb("mo_bias", [P, 3 * DM])
        norm_b = al.sb("mo_norm", [P, DM])
        mod = al.sb("mo_mod", [P, 3 * DM])
        ps = [al.ps(f"mo_ps{j}", [P, W]) for j in range(PARTS)]
        w_in = [sem(f"mo_w_in{j}") for j in range(4)]
        c_ready, wide, rows_in, used, added, done = (sem("mo_c_ready"), sem("mo_wide"), sem("mo_rows_in"), sem("mo_used"),
                                                      sem("mo_added"), sem("mo_done"))
        gate_out = sem("mo_gate_out")
        w_v = w_ada.rearrange("(k p) (h n) -> h k p n", p=P, h=PARTS)
        STEPS = PARTS * KC
        block = ctx.enter_context(nc.Block())

        @block.sync
        def _(sp):
            with nc.allow_non_contiguous_dma(reason="one vector, once"):
                sp.dma_start(c_col[:], c_in.rearrange("(k p) -> p k", p=P)).then_inc(rows_in, 16)
            for n in range(STEPS):
                if n >= 4:
                    sp.wait_ge(used, n - 3)
                sp.dma_start(w[:, n % 4], w_v[n // KC, n % KC]).then_inc(w_in[n % 4], 16)
                if n == 3:
                    sp.dma_start(bias[:], b_ada.partition_broadcast(P)).then_inc(rows_in, 16)
                    sp.dma_start(norm_b[:], norm_w.partition_broadcast(P)).then_inc(rows_in, 16)
            sp.wait_ge(added, PARTS)
            sp.dma_start(gate_row.rearrange("(a n) -> a n", a=1), mod[0:1, 2 * DM:]).then_inc(gate_out, 16)
            sp.wait_ge(gate_out, 16)

        @block.scalar
        def _(act):
            act.wait_ge(rows_in, 48)
            nc.scalar.activation(c_silu[:], c_col[:], ACT.Silu).then_inc(c_ready, 1)

        @block.vector
        def _(dve):
            dve.wait_ge(c_ready, 1)
            nc.vector.tensor_copy(c_wide[:], c_silu[:].unsqueeze(2).to_broadcast([P, KC, P])).then_inc(wide, 1)
            for h in range(PARTS):
                dve.wait_ge(used, (h + 1) * KC)
                nc.vector.tensor_tensor(mod[:, h * W:h * W + W], ps[h][:], bias[:, h * W:h * W + W], ALU.add).then_inc(added, 1)
            dve.wait_ge(added, PARTS)
            nc.vector.tensor_copy(shift[:], mod[:, 0:DM]).then_inc(done, 1)
            nc.vector.scalar_tensor_tensor(scale_w[:], mod[:, DM:2 * DM], 1.0, norm_b[:], ALU.add, ALU.mult).then_inc(done, 1)
            dve.wait_ge(done, 2)

        @block.tensor
        def _(pe):
            pe.wait_ge(wide, 1)
            for n in range(STEPS):
                pe.wait_ge(w_in[n % 4], 16 * (n // 4 + 1))
                for g in range(0, W, 512):
                    ins = nc.tensor.matmul(ps[n // KC][:, g:g + 512], c_wide[:, n % KC, :], w[:, n % 4, g:g + 512],
                                           start=n % KC == 0, stop=n % KC == KC - 1)
                ins.then_inc(used, 1)


def phase_out_b(nc, sem, x1, o_t, kvqg_t, w_out_b, norm_f, shift, scale_w, ident, xf, xt_hi, xt_lo):
    AC = HEADS * HD // P
    with ExitStack() as ctx:
        al = Alloc(nc, ctx)
        w_hi = al.sb("ob_w_hi", [P, AC, DM], F32R)
        w_lo = al.sb("ob_w_lo", [P, AC, DM], F32R)
        o_raw = al.sb("ob_o_raw", [P, 2, AC, P])
        g_raw = al.sb("ob_g_raw", [P, 2, AC, P])
        o_hi = al.sb("ob_o_hi", [P, 2, AC, P], F32R)
        o_lo = al.sb("ob_o_lo", [P, 2, AC, P], F32R)
        xin = al.sb("ob_x", [P, 2, DM])
        hn = al.sb("ob_hn", [P, 2, DM])
        norm_b = al.sb("ob_norm", [P, DM])
        w_raw = hn[:, 0]
        eps = al.sb("ob_eps", [P, 1])
        ss = al.sb("ob_ss", [P, 8])
        root = al.sb("ob_root", [P, 8])
        rinv = al.sb("ob_rinv", [P, 8])
        acc = [al.ps(f"ob_acc{j}", [P, DM]) for j in range(2)]
        pt = [al.ps(f"ob_pt{j}", [P, KC, P]) for j in range(2)]
        w_in, norm_in, ready = sem("ob_w_in"), sem("ob_norm_in"), sem("ob_ready")
        o_in = [sem(f"ob_o_in{j}") for j in range(2)]
        g_in = [sem(f"ob_g_in{j}") for j in range(2)]
        x_in = [sem(f"ob_x_in{j}") for j in range(2)]
        xf_out = [sem(f"ob_xf_out{j}") for j in range(2)]
        w_hi_done, w_lo_done, silued, gated, o_hi_done, o_lo_done = (sem("ob_w_hi"), sem("ob_w_lo"), sem("ob_silued"), sem("ob_gated"),
                                                                     sem("ob_o_hi"), sem("ob_o_lo"))
        product, added, squared, rooted, inverted = sem("ob_product"), sem("ob_added"), sem("ob_squared"), sem("ob_rooted"), sem("ob_inverted")
        normed, scaled, shifted, transposed, hi_done, lo_done = (sem("ob_normed"), sem("ob_scaled"), sem("ob_shifted"), sem("ob_transposed"),
                                                                 sem("ob_hi"), sem("ob_lo"))
        w_v = w_out_b.rearrange("(k p) n -> k p n", p=P)
        o_v = o_t.rearrange("(k p) (t n) -> t p k n", p=P, n=P)
        g_v = kvqg_t[3 * AC * P:, :].rearrange("(k p) (t n) -> t p k n", p=P, n=P)
        x_v = x1.rearrange("(t p) d -> t p d", p=P)
        xf_v = xf.rearrange("(t p) d -> t p d", p=P)
        PAIRS = TILES // 2
        block = ctx.enter_context(nc.Block())

        @block.sync
        def _(sp):
            def load(tile, j):
                sp.dma_start(o_raw[:, j], tile(o_v, "a p k n -> (a p) k n")).then_inc(o_in[j], 16)
                sp.dma_start(g_raw[:, j], tile(g_v, "a p k n -> (a p) k n")).then_inc(g_in[j], 16)

            sp.dma_start(norm_b[:], norm_f.partition_broadcast(P)).then_inc(norm_in, 16)
            for j in range(2):
                load(lambda v, _: v[j], j)
                sp.dma_start(xin[:, j], x_v[j]).then_inc(x_in[j], 16)
            for k in range(AC):
                if k:
                    sp.wait_ge(w_lo_done, k)
                sp.dma_start(w_raw, w_v[k]).then_inc(w_in, 16)
            with sp.Fori(0, PAIRS - 1) as i:
                for j in range(2):
                    sp.wait_ge(o_lo_done, i * 2 + (j + 1))
                    load(lambda v, r: v[bass.ds(i * 2 + (j + 2), 1)].rearrange(r), j)
                    sp.wait_ge(normed, i * 2 + (j + 1))
                    sp.dma_start(xf_v[bass.ds(i * 2 + j, 1)].rearrange("a p d -> (a p) d"), xin[:, j]).then_inc(xf_out[j], 16)
                    sp.wait_ge(scaled, i * 2 + (j + 1))
                    sp.wait_ge(xf_out[j], i * 16 + 16)
                    sp.dma_start(xin[:, j], x_v[bass.ds(i * 2 + (j + 2), 1)].rearrange("a p d -> (a p) d")).then_inc(x_in[j], 16)
            for j in range(2):
                sp.wait_ge(normed, TILES - 1 + j)
                sp.dma_start(xf_v[TILES - 2 + j], xin[:, j]).then_inc(xf_out[j], 16)
            for j in range(2):
                sp.wait_ge(xf_out[j], 16 * PAIRS)

        @block.gpsimd
        def _(pool):
            nc.gpsimd.memset(eps[:], EPS).then_inc(ready, 1)

        @block.scalar
        def _(act):
            act.wait_ge(ready, 1)
            for k in range(AC):
                act.wait_ge(w_in, 16 * (k + 1))
                nc.scalar.activation(w_hi[:, k], w_raw, ACT.Copy).then_inc(w_hi_done, 1)

            def silu(t, j):
                act.wait_ge(g_in[j], (t - j) * 8 + 16)
                nc.scalar.activation(g_raw[:, j], g_raw[:, j], ACT.Silu).then_inc(silued, 1)

            def hi(t, j):
                act.wait_ge(gated, t + 1)
                act.wait_ge(product, t + 1)
                nc.scalar.activation(o_hi[:, j], o_raw[:, j], ACT.Copy).then_inc(o_hi_done, 1)

            def root_of(n, j):
                act.wait_ge(squared, n + 1)
                nc.scalar.activation(root[:, 4 * j:4 * j + 1], ss[:, 4 * j:4 * j + 1], ACT.Sqrt, bias=eps[:], scale=1.0 / DM).then_inc(rooted, 1)

            def stats(t, j):
                act.wait_ge(added, t + 3)
                act.wait_ge(transposed, t + 1)
                nc.scalar.activation(hn[:, j], xin[:, j], ACT.Square, accum_out=ss[:, 4 * j:4 * j + 1]).then_inc(squared, 1)
                root_of(t * 2, j)
                act.wait_ge(normed, t + 1)
                nc.scalar.activation(hn[:, j], xin[:, j], ACT.Square, accum_out=ss[:, 4 * j:4 * j + 1]).then_inc(squared, 1)
                root_of(t * 2 + 1, j)

            def leave(t, j):
                act.wait_ge(transposed, t + 3)
                nc.scalar.activation(xt_hi[:, :, bass.ds(t * P, P)], pt[j][:], ACT.Copy).then_inc(hi_done, 1)

            act.wait_ge(w_lo_done, AC)
            for j in range(2):
                silu(j, j)
                hi(j, j)
            with act.Fori(0, PAIRS - 1) as i:
                for j in range(2):
                    silu(i * 2 + (j + 2), j)
                    stats(i * 2 + j, j)
                    hi(i * 2 + (j + 2), j)
                    leave(i * 2 + j, j)
            for j in range(2):
                stats(TILES - 2 + j, j)
                leave(TILES - 2 + j, j)

        @block.vector
        def _(dve):
            for k in range(AC):
                dve.wait_ge(w_hi_done, k + 1)
                nc.vector.tensor_tensor(w_lo[:, k], w_raw, w_hi[:, k].bitcast(F32), ALU.subtract).then_inc(w_lo_done, 1)
            dve.wait_ge(norm_in, 16)

            def gates(t, j):
                dve.wait_ge(o_in[j], (t - j) * 8 + 16)
                dve.wait_ge(silued, t + 1)
                nc.vector.tensor_tensor(o_raw[:, j], o_raw[:, j], g_raw[:, j], ALU.mult).then_inc(gated, 1)
                dve.wait_ge(gated, t + 1)
                dve.wait_ge(o_hi_done, t + 1)
                nc.vector.tensor_tensor(o_lo[:, j], o_raw[:, j], o_hi[:, j].bitcast(F32), ALU.subtract).then_inc(o_lo_done, 1)

            def invert(n, j):
                dve.wait_ge(rooted, n + 1)
                nc.vector.reciprocal(rinv[:, 4 * j:4 * j + 1], root[:, 4 * j:4 * j + 1]).then_inc(inverted, 1)
                dve.wait_ge(inverted, n + 1)

            def add(t, j):
                dve.wait_ge(product, t + 3)
                dve.wait_ge(x_in[j], (t - j) * 8 + 16)
                nc.vector.tensor_tensor(xin[:, j], acc[j][:], xin[:, j], ALU.add).then_inc(added, 1)

            def norm(t, j):
                invert(t * 2, j)
                nc.vector.scalar_tensor_tensor(xin[:, j], xin[:, j], rinv[:, 4 * j:4 * j + 1], norm_b[:], ALU.mult, ALU.mult).then_inc(normed, 1)

            def modulate(t, j):
                invert(t * 2 + 1, j)
                dve.wait_ge(transposed, t + 1)
                nc.vector.scalar_tensor_tensor(hn[:, j], xin[:, j], rinv[:, 4 * j:4 * j + 1], scale_w[:], ALU.mult, ALU.mult).then_inc(scaled, 1)
                dve.wait_ge(scaled, t + 1)
                nc.vector.tensor_tensor(hn[:, j], hn[:, j], shift[:], ALU.add).then_inc(shifted, 1)

            def lo(t, j):
                dve.wait_ge(hi_done, t + 1)
                nc.vector.tensor_tensor(xt_lo[:, :, bass.ds(t * P, P)], pt[j][:],
                                        xt_hi[:, :, bass.ds(t * P, P)].bitcast(F32), ALU.subtract).then_inc(lo_done, 1)

            for j in range(2):
                gates(j, j)
            with dve.Fori(0, PAIRS - 1) as i:
                for j in range(2):
                    add(i * 2 + j, j)
                    norm(i * 2 + j, j)
                    gates(i * 2 + (j + 2), j)
                    modulate(i * 2 + j, j)
                    lo(i * 2 + j, j)
            for j in range(2):
                add(TILES - 2 + j, j)
                norm(TILES - 2 + j, j)
                modulate(TILES - 2 + j, j)
                lo(TILES - 2 + j, j)

        @block.tensor
        def _(pe):
            pe.sem_inc(product, 2)
            pe.sem_inc(added, 2)
            pe.sem_inc(transposed, 2)
            pe.sem_inc(lo_done, 2)

            def multiply(t, j):
                pe.wait_ge(o_lo_done, t + 1)
                pe.wait_ge(added, t + 1)
                for half in range(2):
                    cols = slice(half * 512, half * 512 + 512)
                    for k in range(AC):
                        for n, (w, a) in enumerate(split_pass_list(w_hi, w_lo, o_hi, o_lo)):
                            ins = nc.tensor.matmul(acc[j][:, cols], a[:, j, k, :], w[:, k, cols],
                                                   start=(k == 0 and n == 0), stop=(k == AC - 1 and n == 2))
                ins.then_inc(product, 1)

            def transpose(t, j):
                pe.wait_ge(shifted, t + 1)
                pe.wait_ge(lo_done, t + 1)
                for k in range(KC):
                    ins = nc.tensor.transpose(pt[j][:, k, :], hn[:, j, k * P:(k + 1) * P], ident[:])
                ins.then_inc(transposed, 1)

            pe.wait_ge(w_lo_done, AC)
            multiply(0, 0)
            with pe.Fori(0, PAIRS - 1) as i:
                multiply(i * 2 + 1, 1)
                transpose(i * 2, 0)
                multiply(i * 2 + 2, 0)
                transpose(i * 2 + 1, 1)
            multiply(TILES - 1, 1)
            transpose(TILES - 2, 0)
            transpose(TILES - 1, 1)
POOL = 512
WINDOWS = (2, 4, 8, 16)
HALO = max(WINDOWS)
IDX_HEADS = 8
TOP = 256
KV_HEADS = 2
ROW_U, ROW_GP, ROW_Q, ROW_K, ROW_V, ROW_GA, ROW_QI, ROW_KI, ROW_WI = (int(r) for r in np.cumsum([0, 512, 512, 512, 128, 128, 512, 512, 64]))
D_PROJ = ROW_WI + IDX_HEADS
ROT_Q, ROT_K, ROT_QI, ROT_KI, ROT_ROWS = 0, 512, 640, 1152, 1216


def phase_pool_rope(nc, sem, p_t, w_pool, pool_scale, q_norm, k_norm, cos_t, sin_t, inv_count, mix_t, rot_t):
    WIDTHS = len(WINDOWS)
    rotated = [(ROW_Q + P * n, P, n, ROT_Q + P * n) for n in range(4)] + [(ROW_K, P, 4, ROT_K)]
    rotated += [(ROW_QI + P * n, P, None, ROT_QI + P * n) for n in range(4)] + [(ROW_KI, HD, None, ROT_KI)]
    NORMED = 5
    with ExitStack() as ctx:
        al = Alloc(nc, ctx)
        cos = al.sb("pr_cos", [P, SEQ])
        sin = al.sb("pr_sin", [P, SEQ])
        w_sb = al.sb("pr_w", [P, WIDTHS, P])
        scale = al.sb("pr_scale", [P, WIDTHS])
        inv = al.sb("pr_inv", [P, WIDTHS, HALO])
        norms = al.sb("pr_norms", [P, NORMED])
        norms_s = al.sb("pr_norms_s", [P, NORMED])
        eps = al.sb("pr_eps", [P, 1])
        ones = al.sb("pr_ones", [P, P])
        x = al.sb("pr_x", [P, 2, SEQ])
        xs = al.sb("pr_xs", [P, 2, SEQ])
        sq = al.sb("pr_sq", [P, 2, SEQ])
        u = al.sb("pr_u", [P, SEQ])
        sums = [al.sb(f"pr_sum{j}", [P, HALO + SEQ]) for j in range(2)]
        ps = [al.ps(f"pr_ps{j}", [P, SEQ]) for j in range(2)]
        const_in, ones_ready, done = sem("pr_const_in"), sem("pr_ones_ready"), sem("pr_chain")
        x_in = [sem(f"pr_x_in{j}") for j in range(2)]
        xs_in = [sem(f"pr_xs_in{j}") for j in range(2)]
        x_out = [sem(f"pr_x_out{j}") for j in range(2)]
        squared, summed, rooted, turned = sem("pr_squared"), sem("pr_summed"), sem("pr_rooted"), sem("pr_turned")
        u_in, gp_in, gp_ready, pooled, mixed, u_ready, mix_out = (sem("pr_u_in"), sem("pr_gp_in"), sem("pr_gp_ready"), sem("pr_pooled"),
                                                                  sem("pr_mixed"), sem("pr_u_ready"), sem("pr_mix_out"))
        block = ctx.enter_context(nc.Block())
        CONSTS = 0

        @block.sync
        def _(sp):
            def load(n):
                row, rows, _, _ = rotated[n]
                if n >= 2:
                    sp.wait_ge(x_out[n % 2], 16 * (n // 2))
                sp.dma_start(x[0:rows, n % 2], p_t[row:row + rows, :]).then_inc(x_in[n % 2], 16)
                for at in range(0, rows, 32):
                    other = row + (at ^ 32)
                    sp.dma_start(xs[at:at + 32, n % 2], p_t[other:other + 32, :]).then_inc(xs_in[n % 2], 16)

            sp.dma_start(u[:], p_t[ROW_U:ROW_U + P, :]).then_inc(u_in, 16)
            load(0)
            sp.dma_start(cos[:], cos_t).then_inc(const_in, 16)
            sp.dma_start(sin[:], sin_t).then_inc(const_in, 16)
            sp.dma_start(inv[:], inv_count.partition_broadcast(P)).then_inc(const_in, 16)
            sp.dma_start(w_sb[:], w_pool.rearrange("g c d -> c g d")).then_inc(const_in, 16)
            with nc.allow_non_contiguous_dma(reason="a few vectors, once"):
                sp.dma_start(scale[:], pool_scale.rearrange("(g p) -> p g", p=P)).then_inc(const_in, 16)
                for n in range(NORMED):
                    w = (q_norm if n < 4 else k_norm).rearrange("(p a) -> p a", a=1)
                    for at in range(0, P, 32):
                        half = at % HD
                        sp.dma_start(norms[at:at + 32, n:n + 1], w[half:half + 32]).then_inc(const_in, 16)
                        sp.dma_start(norms_s[at:at + 32, n:n + 1], w[half ^ 32:(half ^ 32) + 32]).then_inc(const_in, 16)
            load(1)
            for n, (_, rows, _, out) in enumerate(rotated):
                sp.wait_ge(turned, n + 1)
                sp.dma_start(rot_t[out:out + rows, :], x[0:rows, n % 2]).then_inc(x_out[n % 2], 16)
                if n + 2 < len(rotated):
                    load(n + 2)
                if n < 2 * WIDTHS:
                    g = n // 2
                    if n % 2:
                        sp.wait_ge(u_ready, g + 1)
                        sp.dma_start(mix_t[g * P:g * P + P, :], u[:]).then_inc(mix_out, 16)
                        if g + 1 < WIDTHS:
                            sp.wait_ge(mix_out, 16 * (g + 1))
                            sp.dma_start(u[:], p_t[ROW_U + (g + 1) * P:ROW_U + (g + 2) * P, :]).then_inc(u_in, 16)
            for j in range(2):
                sp.wait_ge(x_out[j], 16 * (len(rotated) // 2))
            sp.wait_ge(mix_out, 16 * WIDTHS)

        N_CONST = 16 * (5 + 2 * 4 * NORMED)

        @block.gpsimd
        def _(pool):
            nc.gpsimd.memset(eps[:], EPS).then_inc(ones_ready, 1)
            nc.gpsimd.memset(ones[:], 0.0).then_inc(ones_ready, 1)
            for s in sums:
                nc.gpsimd.memset(s[:, 0:HALO], 0.0).then_inc(ones_ready, 1)
            pool.wait_ge(ones_ready, 4)
            for h in range(2):
                nc.gpsimd.memset(ones[h * HD:h * HD + HD, h * HD:h * HD + HD], 1.0).then_inc(ones_ready, 1)

        @block.scalar
        def _(act):
            act.wait_ge(ones_ready, 6)
            act.wait_ge(const_in, N_CONST)
            for n in range(NORMED):
                act.wait_ge(x_in[n % 2], 16 * (n // 2 + 1))
                if n >= 2:
                    act.wait_ge(turned, n - 1)
                nc.scalar.activation(sq[:, n % 2], x[:, n % 2], ACT.Square).then_inc(squared, 1)
                act.wait_ge(summed, n + 1)
                nc.scalar.activation(sq[:, n % 2], ps[0][:], ACT.Sqrt, bias=eps[:], scale=1.0 / HD).then_inc(rooted, 1)

        @block.vector
        def _(dve):
            count = [0]

            def then(ins):
                count[0] += 1
                ins.then_inc(done, 1)
                dve.wait_ge(done, count[0])

            def rotate(n):
                _, rows, norm, _ = rotated[n]
                b = n % 2
                a, s, r = x[0:rows, b], xs[0:rows, b], sq[0:rows, b]
                dve.wait_ge(x_in[b], 16 * (n // 2 + 1))
                dve.wait_ge(xs_in[b], 64 * (n // 2 + 1) - (32 if rows < P else 0))
                if norm is None:
                    nc.vector.tensor_tensor(s, s, sin[0:rows], ALU.mult).then_inc(done, 1)
                    nc.vector.tensor_tensor(a, a, cos[0:rows], ALU.mult).then_inc(done, 1)
                    count[0] += 2
                    dve.wait_ge(done, count[0])
                    nc.vector.tensor_tensor(a, a, s, ALU.add).then_inc(turned, 1)
                    return
                dve.wait_ge(squared, n + 1)
                nc.vector.scalar_tensor_tensor(s, s, norms_s[:, norm:norm + 1], sin[:], ALU.mult, ALU.mult).then_inc(done, 1)
                nc.vector.scalar_tensor_tensor(a, a, norms[:, norm:norm + 1], cos[:], ALU.mult, ALU.mult).then_inc(done, 1)
                dve.wait_ge(rooted, n + 1)
                nc.vector.reciprocal(r, r).then_inc(done, 1)
                count[0] += 3
                dve.wait_ge(done, count[0])
                then(nc.vector.tensor_tensor(a, a, s, ALU.add))
                nc.vector.tensor_tensor(a, a, r, ALU.mult).then_inc(turned, 1)

            def window(g):
                w = WINDOWS[g]
                dve.wait_ge(u_in, 16 * (g + 1))
                if g:
                    dve.wait_ge(u_ready, g)
                now = u[:]
                size = 1
                while size < w:
                    s = sums[(size.bit_length() - 1) % 2]
                    if size == 1:
                        then(nc.vector.tensor_copy(s[:, HALO:HALO + 1], u[:, 0:1]))
                        then(nc.vector.tensor_tensor(s[:, HALO + 1:], u[:, 1:], u[:, 0:SEQ - 1], ALU.add))
                    else:
                        then(nc.vector.tensor_tensor(s[:, HALO:], now[:, HALO:], now[:, HALO - size:HALO + SEQ - size], ALU.add))
                    now = s
                    size *= 2
                other = sums[0] if now is sums[1] else sums[1]
                then(nc.vector.tensor_tensor(other[:, HALO:2 * HALO], now[:, HALO:2 * HALO], inv[:, g], ALU.mult))
                then(nc.vector.tensor_tensor(other[:, HALO:2 * HALO], other[:, HALO:2 * HALO], u[:, 0:HALO], ALU.subtract))
                nc.vector.scalar_tensor_tensor(other[:, 2 * HALO:], now[:, 2 * HALO:], 1.0 / w, u[:, HALO:],
                                               ALU.mult, ALU.subtract).then_inc(pooled, 1)

            def mix(g):
                dve.wait_ge(mixed, g + 1)
                nc.vector.tensor_scalar(u[:], ps[1][:], scale[:, g:g + 1], None, ALU.mult).then_inc(u_ready, 1)

            dve.wait_ge(ones_ready, 6)
            dve.wait_ge(const_in, N_CONST)
            for n in range(len(rotated)):
                if n < 2 * WIDTHS and n % 2 == 0:
                    window(n // 2)
                rotate(n)
                if n < 2 * WIDTHS and n % 2 == 1:
                    mix(n // 2)

        @block.tensor
        def _(pe):
            pe.wait_ge(ones_ready, 6)

            def sum_squares(n):
                pe.wait_ge(squared, n + 1)
                if n:
                    pe.wait_ge(rooted, n)
                for t in range(NT):
                    ins = nc.tensor.matmul(ps[0][:, t * 512:t * 512 + 512], ones[:], sq[:, n % 2, t * 512:t * 512 + 512], start=True, stop=True)
                ins.then_inc(summed, 1)

            def pool_mix(g):
                last = sums[1] if WINDOWS[g].bit_length() % 2 == 0 else sums[0]
                pe.wait_ge(pooled, g + 1)
                for t in range(NT):
                    ins = nc.tensor.matmul(ps[1][:, t * 512:t * 512 + 512], w_sb[:, g, :], last[:, HALO + t * 512:HALO + t * 512 + 512], start=True, stop=True)
                ins.then_inc(mixed, 1)

            pe.wait_ge(const_in, N_CONST)
            for n in range(len(rotated)):
                if n < 2 * WIDTHS and n % 2 == 0:
                    pool_mix(n // 2)
                if n < NORMED:
                    sum_squares(n)
def phase_select_attend(nc, sem, p_t, rot_t, bit_int, bit_val, half_powers, rank_row, mix_t, ident):
    CHUNK = 1024
    FAR = -1e30
    LOWEST = -3e38
    BITS = 31
    STEPS = 12
    EIGHT = 8
    BEST = 2 * EIGHT
    DEEP = 3
    SEARCH, TIES = 4 * BITS + 4, 7
    blocks = range(TILES)
    selecting = [qb for qb in blocks if P * (qb + 1) > TOP]
    first_selecting = selecting[0]

    def keys(qb):
        return P * (qb + 1)

    def parts(qb):
        return [(at, min(CHUNK, keys(qb) - at)) for at in range(0, keys(qb), CHUNK)]

    def quads(at, n):
        return [(g, min(512, at + n - g)) for g in range(at, at + n, 512)]

    def place_of(qb):
        return qb - first_selecting

    order = []
    for qb in blocks:
        order += ([("index", qb + 1)] if qb + 1 in selecting else []) + [("attend", qb)]
    number, products = {}, []
    for kind, qb in order:
        for h in range(HEADS):
            for m, (at, n) in enumerate(parts(qb)):
                number[kind, qb, h, m] = len(products)
                products.append((kind, qb, h, m, at, n))
    group_at, n_groups = {}, 0
    for qb in blocks:
        for h in range(HEADS):
            group_at[qb, h] = n_groups
            n_groups += len(quads(0, keys(qb)))
    relus, masks = {}, {}
    for kind, qb, h, m, _, _ in products:
        kept_in = relus if kind == "index" else masks
        kept_in[qb, h, m] = len(kept_in)
    with ExitStack() as ctx:
        al = Alloc(nc, ctx)
        ki_hi = al.sb("sa_ki_hi", [P, SEQ], F32R)
        ki_lo = al.sb("sa_ki_lo", [P, SEQ], F32R)
        k_hi = al.sb("sa_k_hi", [P, KV_HEADS, SEQ], F32R)
        k_lo = al.sb("sa_k_lo", [P, KV_HEADS, SEQ], F32R)
        v_one = al.sb("sa_v_one", [P, TILES, KV_HEADS, P])
        w_idx = al.sb("sa_w_idx", [P, TILES, IDX_HEADS])
        qi_raw = al.sb("sa_qi_raw", [P, 2, HEADS, P])
        qi_two = al.sb("sa_qi_two", [P, 2, HEADS, P], F32R)
        q_raw = al.sb("sa_q_raw", [P, 2, HEADS, P])
        q_two = al.sb("sa_q_two", [P, 2, HEADS, P], F32R)
        relu = al.sb("sa_relu", [P, 2, CHUNK])
        score = al.sb("sa_score", [P, 2, SEQ])
        tied = al.sb("sa_tied", [P, SEQ])
        place = al.sb("sa_place", [P, SEQ])
        raw, v_raw, wi_raw = score[:, 1], place, tied[0:IDX_HEADS]
        bias = al.sb("sa_bias", [P, 2, SEQ])
        arg = al.sb("sa_arg", [P, DEEP, SEQ])
        prob = al.sb("sa_prob", [P, 2, 512])
        top = al.sb("sa_top", [P, DEEP, 2])
        minus_top = al.sb("sa_minus_top", [P, DEEP])
        o_sb = al.sb("sa_o", [P, 2, HEADS, P])
        inv_sum = al.sb("sa_inv_sum", [HD, HEADS, P])
        bit_i = al.sb("sa_bit_i", [P, BITS], mybir.dt.int32)
        bit_f = al.sb("sa_bit_f", [P, BITS])
        pref = al.sb("sa_pref", [P, 1], mybir.dt.int32)
        flip = al.sb("sa_flip", [P, 1], mybir.dt.int32)
        cand = al.sb("sa_cand", [P, 1], mybir.dt.int32)
        kept = al.sb("sa_kept", [P, 1], mybir.dt.int32)
        thr = al.sb("sa_thr", [P, 1], mybir.dt.int32)
        count = al.sb("sa_count", [P, 8])
        edge = al.sb("sa_edge", [P, 3])
        halves = al.sb("sa_halves", [P, STEPS])
        width = al.sb("sa_width", [P, STEPS])
        guess = al.sb("sa_guess", [P, 1])
        go_up = al.sb("sa_go_up", [P, 1])
        ranks = al.sb("sa_ranks", [P, BEST + 1])
        short = al.sb("sa_short", [P, 1])
        is_rank = al.sb("sa_is_rank", [P, BEST + 1])
        best = al.sb("sa_best", [P, BEST + 1])
        cut = al.sb("sa_cut", [P, 1])
        lost = al.sb("sa_lost", [P, 1])
        report = al.sb("sa_report", [P, 2])
        reported = al.sb("sa_reported", [1, 2], mybir.dt.int32)
        pr = [al.ps(f"sa_pr{j}", [P, CHUNK]) for j in range(2)]
        turn = [al.ps(f"sa_turn{j}", [P, 512]) for j in range(2)]
        o_ps = [al.ps(f"sa_o{j}", [P, P]) for j in range(2)]
        report_ps = o_ps[0][0:1, 0:2]
        raw_in, vw_in, bits_in = sem("sa_raw_in"), sem("sa_vw_in"), sem("sa_bits_in")
        key_hi, key_lo, ones_set = sem("sa_key_hi"), sem("sa_key_lo"), sem("sa_ones_set")
        v_turned, v_left, wi_turned, wi_left = sem("sa_v_turned"), sem("sa_v_left"), sem("sa_wi_turned"), sem("sa_wi_left")
        qi_in = [sem(f"sa_qi_in{j}") for j in range(2)]
        q_in = [sem(f"sa_q_in{j}") for j in range(2)]
        qi_hi, qi_lo, q_hi, q_lo = sem("sa_qi_hi"), sem("sa_qi_lo"), sem("sa_q_hi"), sem("sa_q_lo")
        product, relu_done, scored, causal = sem("sa_product"), sem("sa_relu_done"), sem("sa_scored"), sem("sa_causal")
        ranged, step, selected, searched, repaired = sem("sa_ranged"), sem("sa_step"), sem("sa_selected"), sem("sa_searched"), sem("sa_repaired")
        report_summed, report_read, masked, negated, raised = sem("sa_report_summed"), sem("sa_report_read"), sem("sa_masked"), sem("sa_negated"), sem("sa_raised")
        turned, p_ready, weighed, o_ready, o_out = sem("sa_turned"), sem("sa_p_ready"), sem("sa_weighed"), sem("sa_o_ready"), [sem(f"sa_o_out{j}") for j in range(2)]
        logged, inverted, divided = sem("sa_logged"), sem("sa_inverted"), sem("sa_divided")
        qi_v = rot_t[ROT_QI:ROT_QI + 512, :].rearrange("(h d) (t n) -> t d h n", d=HD, n=P)
        q_v = rot_t[ROT_Q:ROT_Q + 512, :].rearrange("(h d) (t n) -> t d h n", d=HD, n=P)
        o_v = mix_t[POOL:, :].rearrange("(h d) (t n) -> t d h n", d=HD, n=P)
        key_rows = [(ROT_KI, ki_hi[:], ki_lo[:])] + [(ROT_K + HD * g, k_hi[:, g], k_lo[:, g]) for g in range(KV_HEADS)]
        block = ctx.enter_context(nc.Block())

        def left(eng, n):
            kind, qb, h, m, _, _ = products[n]
            if kind == "index":
                eng.wait_ge(relu_done, relus[qb, h, m] + 1)
            else:
                eng.wait_ge(masked, masks[qb, h, m] + 1)

        @block.sync
        def _(sp):
            def load_q(qb):
                if qb >= 2:
                    sp.wait_ge(q_lo, qb - 1)
                for half in range(2):
                    sp.dma_start(q_raw[half * HD:half * HD + HD, qb % 2], q_v[qb]).then_inc(q_in[qb % 2], 16)

            def load_qi(qb):
                if place_of(qb) >= 2:
                    sp.wait_ge(qi_lo, place_of(qb) - 1)
                for half in range(2):
                    sp.dma_start(qi_raw[half * HD:half * HD + HD, qb % 2], qi_v[qb]).then_inc(qi_in[qb % 2], 16)

            for n, (row, _, _) in enumerate(key_rows):
                if n:
                    sp.wait_ge(key_lo, n)
                for half in range(2):
                    sp.dma_start(raw[half * HD:half * HD + HD], rot_t[row:row + HD, :]).then_inc(raw_in, 16)
                if n == 0:
                    load_q(0)
                    load_qi(first_selecting)
                    sp.dma_start(wi_raw, p_t[ROW_WI:ROW_WI + IDX_HEADS, :]).then_inc(vw_in, 16)
                    sp.dma_start(v_raw[:], p_t[ROW_V:ROW_V + P, :]).then_inc(vw_in, 16)
                    for to, rows in ((bit_i, bit_int), (bit_f, bit_val), (halves, half_powers), (ranks, rank_row)):
                        sp.dma_start(to[:], rows.partition_broadcast(P)).then_inc(bits_in, 16)
            load_q(1)
            load_qi(first_selecting + 1)
            for qb in blocks:
                if qb + 2 < TILES:
                    load_q(qb + 2)
                if first_selecting + qb + 2 < TILES:
                    load_qi(first_selecting + qb + 2)
                sp.wait_ge(divided, qb + 1)
                sp.dma_start(o_v[qb], o_sb[0:HD, qb % 2]).then_inc(o_out[qb % 2], 16)
            for j in range(2):
                sp.wait_ge(o_out[j], 16 * (TILES // 2))

        @block.gpsimd
        def _(pool):
            nc.gpsimd.memset(v_one[:, :, :, HD:], 1.0).then_inc(ones_set, 1)

            def divide(qb):
                pool.wait_ge(inverted, qb + 1)
                o = o_sb[0:HD, qb % 2]
                nc.gpsimd.tensor_tensor(o, o, inv_sum[:], ALU.mult).then_inc(divided, 1)

            for qb in blocks:
                if qb in selecting:
                    pool.wait_ge(ranged, 2 * (place_of(qb) + 1))
                    own = score[:, qb % 2, qb * P:qb * P + P]
                    nc.gpsimd.affine_select(out=own, in_=own, compare_op=ALU.is_ge, fill=LOWEST, base=0,
                                            pattern=[[-1, P]], channel_multiplier=1).then_inc(causal, 1)
                else:
                    assert qb < 2
                    nc.gpsimd.memset(bias[:, qb, 0:keys(qb)], 0.0).then_inc(ones_set, 1)
                    pool.wait_ge(ones_set, qb + 2)
                    own = bias[:, qb, qb * P:qb * P + P]
                    nc.gpsimd.affine_select(out=own, in_=own, compare_op=ALU.is_ge, fill=FAR, base=0,
                                            pattern=[[-1, P]], channel_multiplier=1).then_inc(causal, 1)
                if qb:
                    divide(qb - 1)
            divide(TILES - 1)

        @block.scalar
        def _(act):
            nc.scalar.preload_act_table_set("natural_log_exp_and_others")

            def split_q(qb):
                j, i = qb % 2, place_of(qb)
                act.wait_ge(qi_in[j], 32 * (i // 2 + 1))
                if i >= 2:
                    act.wait_ge(product, number["index", qb - 2, HEADS - 1, len(parts(qb - 2)) - 1] + 1)
                nc.scalar.activation(qi_two[:, j], qi_raw[:, j], ACT.Copy).then_inc(qi_hi, 1)

            def split_q_attend(qb):
                j = qb % 2
                act.wait_ge(q_in[j], 32 * (qb // 2 + 1))
                if qb >= 2:
                    act.wait_ge(product, number["attend", qb - 2, HEADS - 1, len(parts(qb - 2)) - 1] + 1)
                nc.scalar.activation(q_two[:, j], q_raw[:, j], ACT.Copy, scale=HD ** -0.5).then_inc(q_hi, 1)

            for n, (_, hi, _) in enumerate(key_rows):
                act.wait_ge(raw_in, 32 * (n + 1))
                nc.scalar.activation(hi, raw[:], ACT.Copy).then_inc(key_hi, 1)
                if n == 0:
                    split_q(first_selecting)
                    split_q_attend(0)
            act.wait_ge(wi_turned, 1)
            nc.scalar.activation(w_idx[:], turn[0][:, 0:TILES * IDX_HEADS].rearrange("p (t h) -> p t h", h=IDX_HEADS), ACT.Copy,
                                 scale=HD ** -0.5 * IDX_HEADS ** -0.5).then_inc(wi_left, 1)
            for g in range(TILES // 4):
                act.wait_ge(v_turned, g + 1)
                for kv in range(KV_HEADS):
                    ins = nc.scalar.activation(v_one[:, g * 4:g * 4 + 4, kv, 0:HD],
                                               turn[(g + 1) % 2][:].rearrange("p (t k d) -> p t k d", k=KV_HEADS, d=HD)[:, :, kv], ACT.Copy)
                ins.then_inc(v_left, 1)

            def raise_e(qb, h):
                t = qb * HEADS + h
                act.wait_ge(negated, t + 1)
                row = arg[:, t % DEEP, 0:keys(qb)]
                nc.scalar.activation(row, row, ACT.Exp, bias=minus_top[:, t % DEEP:t % DEEP + 1]).then_inc(raised, 1)

            for kind, qb in order:
                if kind == "index":
                    if qb + 1 < TILES:
                        split_q(qb + 1)
                    for h in range(HEADS):
                        for m, (at, n) in enumerate(parts(qb)):
                            r = relus[qb, h, m]
                            act.wait_ge(product, number[kind, qb, h, m] + 1)
                            if r >= 2:
                                act.wait_ge(scored, r - 1)
                            nc.scalar.activation(relu[:, r % 2, 0:n], pr[number[kind, qb, h, m] % 2][:, 0:n], ACT.Relu).then_inc(relu_done, 1)
                    continue
                if qb + 1 < TILES:
                    split_q_attend(qb + 1)
                def leave(h):
                    act.wait_ge(weighed, group_at[qb, h] + len(quads(0, keys(qb))))
                    if h == 0 and qb >= 2:
                        act.wait_ge(o_out[qb % 2], 16 * (qb // 2))
                    nc.scalar.activation(o_sb[:, qb % 2, h, :], o_ps[h % 2][:], ACT.Copy).then_inc(o_ready, 1)

                for h in range(DEEP - 1):
                    raise_e(qb, h)
                for h in range(HEADS):
                    if h:
                        leave(h - 1)
                    for m, (_, w) in enumerate(quads(0, keys(qb))):
                        g = group_at[qb, h] + m
                        act.wait_ge(turned, g + 1)
                        if g >= 2:
                            act.wait_ge(weighed, g - 1)
                        nc.scalar.activation(prob[:, g % 2, 0:w], turn[g % 2][:, 0:w], ACT.Copy).then_inc(p_ready, 1)
                    if h + DEEP - 1 < HEADS:
                        raise_e(qb, h + DEEP - 1)
                leave(HEADS - 1)
                o_sum = o_sb[HD:P, qb % 2]
                act.wait_ge(o_ready, HEADS * (qb + 1))
                nc.scalar.activation(o_sum, o_sum, ACT.Ln).then_inc(logged, 1)
                act.wait_ge(logged, qb + 1)
                if qb:
                    act.wait_ge(divided, qb)
                nc.scalar.activation(inv_sum[:], o_sum, ACT.Exp, scale=-1.0).then_inc(inverted, 1)

        @block.vector
        def _(dve):
            steps = [0]

            def mark(ins):
                steps[0] += 1
                ins.then_inc(step, 1)

            def last_step():
                dve.wait_ge(step, steps[0])

            def split_q(qb):
                j = qb % 2
                dve.wait_ge(qi_hi, place_of(qb) + 1)
                nc.vector.tensor_tensor(qi_two[HD:P, j], qi_raw[HD:P, j], qi_two[HD:P, j].bitcast(F32), ALU.subtract).then_inc(qi_lo, 1)

            def split_q_attend(qb):
                j = qb % 2
                dve.wait_ge(q_hi, qb + 1)
                flat = lambda t: t[HD:P, j].rearrange("p h n -> p (h n)")
                nc.vector.scalar_tensor_tensor(flat(q_two), flat(q_raw), HD ** -0.5, flat(q_two).bitcast(F32),
                                               ALU.mult, ALU.subtract).then_inc(q_lo, 1)

            def add_scores(qb):
                for h in range(HEADS):
                    for m, (at, n) in enumerate(parts(qb)):
                        r = relus[qb, h, m]
                        dve.wait_ge(relu_done, r + 1)
                        w, s = w_idx[:, qb, h:h + 1], score[:, qb % 2, at:at + n]
                        if h == 0:
                            ins = nc.vector.tensor_scalar(s, relu[:, r % 2, 0:n], w, None, ALU.mult)
                        else:
                            dve.wait_ge(scored, r + 1 - len(parts(qb)))
                            ins = nc.vector.scalar_tensor_tensor(s, relu[:, r % 2, 0:n], w, s, ALU.mult, ALU.add)
                        ins.then_inc(scored, 1)

            def take_range(qb):
                s = score[:, qb % 2, 0:keys(qb)]
                dve.wait_ge(scored, relus[qb, HEADS - 1, len(parts(qb)) - 1] + 1)
                last_step()
                nc.vector.tensor_reduce(edge[:, 0:1], s, mybir.AxisListType.X, ALU.min).then_inc(ranged, 1)
                nc.vector.tensor_reduce(edge[:, 1:2], s, mybir.AxisListType.X, ALU.max).then_inc(ranged, 1)
                dve.wait_ge(ranged, 2 * (place_of(qb) + 1))
                mark(nc.vector.tensor_tensor(edge[:, 2:3], edge[:, 1:2], edge[:, 0:1], ALU.subtract))
                last_step()
                mark(nc.vector.tensor_scalar(width[:], halves[:], edge[:, 2:3], None, ALU.mult))
                mark(nc.vector.scalar_tensor_tensor(guess[:], edge[:, 2:3], 0.5, edge[:, 0:1], ALU.mult, ALU.add))

            def count_at_guess(qb):
                n = keys(qb)
                dve.wait_ge(causal, qb + 1)
                last_step()
                mark(nc.vector.tensor_scalar(tied[:, 0:n], score[:, qb % 2, 0:n], guess[:, 0:1], None, ALU.is_ge, ALU.add, accum_out=count[:, 0:1]))

            def decide(k):
                last_step()
                mark(nc.vector.tensor_scalar(go_up[:], count[:, 0:1], float(TOP), width[:, k:k + 1], ALU.is_ge, ALU.mult))

            def move(k):
                last_step()
                if k + 1 < STEPS:
                    mark(nc.vector.scalar_tensor_tensor(guess[:], go_up[:], width[:, k + 1:k + 2], guess[:], ALU.subtract, ALU.add))
                else:
                    mark(nc.vector.tensor_tensor(best[:, 0:1], go_up[:], guess[:], ALU.add))

            def count_above(qb):
                n = keys(qb)
                last_step()
                mark(nc.vector.tensor_scalar(tied[:, 0:n], score[:, qb % 2, 0:n], best[:, 0:1], None, ALU.is_ge, ALU.add, accum_out=count[:, 1:2]))

            def drop_above(qb):
                n = keys(qb)
                last_step()
                mark(nc.vector.scalar_tensor_tensor(place[:, 0:n], tied[:, 0:n], LOWEST, score[:, qb % 2, 0:n], ALU.mult, ALU.add))

            def find_short():
                mark(nc.vector.tensor_scalar(short[:], count[:, 1:2], -1.0, float(TOP), ALU.mult, ALU.add))

            def best_below(qb):
                last_step()
                below = place[:, 0:keys(qb)]
                mark(nc.vector.max(best[:, 1:1 + EIGHT], below))
                last_step()
                mark(nc.vector.match_replace(out=below, in_to_replace=best[:, 1:1 + EIGHT], in_values=below, imm_value=LOWEST))
                last_step()
                mark(nc.vector.max(best[:, 1 + EIGHT:], below))
                mark(nc.vector.tensor_scalar(is_rank[:], ranks[:], short[:, 0:1], None, ALU.is_equal))

            def pick():
                last_step()
                mark(nc.vector.tensor_tensor(is_rank[:], is_rank[:], best[:], ALU.mult))

            def find_cut():
                last_step()
                mark(nc.vector.tensor_reduce(cut[:], is_rank[:], mybir.AxisListType.X, ALU.add))

            def count_selected(qb):
                n = keys(qb)
                last_step()
                mark(nc.vector.tensor_scalar(tied[:, 0:n], score[:, qb % 2, 0:n], cut[:, 0:1], None, ALU.is_ge, ALU.add, accum_out=count[:, 2:3]))

            def set_bias(qb):
                n = keys(qb)
                if qb >= 2:
                    dve.wait_ge(masked, masks[qb - 2, HEADS - 1, len(parts(qb - 2)) - 1] + 1)
                mark(nc.vector.scalar_tensor_tensor(lost[:], short[:], float(BEST), short[:], ALU.subtract, ALU.mult))
                mark(nc.vector.tensor_scalar(bias[:, qb % 2, 0:n], score[:, qb % 2, 0:n], cut[:, 0:1], FAR, ALU.is_lt, ALU.mult))
                last_step()
                nc.vector.tensor_scalar(report[:, 0:1], count[:, 2:3], float(TOP), None, ALU.not_equal).then_inc(selected, 1)
                nc.vector.tensor_scalar(report[:, 1:2], lost[:], 0.0, None, ALU.is_gt).then_inc(selected, 1)

            def search(qb):
                n = keys(qb)
                s, ge = score[:, qb % 2, 0:n], tied[:, 0:n]
                done = [SEARCH * place_of(qb)]

                def then(ins):
                    done[0] += 1
                    ins.then_inc(searched, 1)
                    dve.wait_ge(searched, done[0])

                then(nc.vector.tensor_scalar(ge, s, 0.0, None, ALU.is_ge, ALU.add, accum_out=count[:, 3:4]))
                then(nc.vector.tensor_scalar(flip[:], count[:, 3:4], float(TOP), -1.0, ALU.is_ge, ALU.add))
                then(nc.vector.memset(pref[:], 0))
                before = done[0]
                with dve.Fori(0, BITS) as i:
                    nc.vector.tensor_scalar(cand[:], pref[:], bit_i[:, bass.ds(i, 1)], flip[:, 0:1], ALU.bitwise_or, ALU.bitwise_xor).then_inc(searched, 1)
                    dve.wait_ge(searched, i * 4 + (before + 1))
                    nc.vector.tensor_scalar(ge, s, cand[:].bitcast(F32), None, ALU.is_ge, ALU.add, accum_out=count[:, 3:4]).then_inc(searched, 1)
                    dve.wait_ge(searched, i * 4 + (before + 2))
                    nc.vector.tensor_scalar(kept[:], count[:, 3:4], float(TOP), bit_f[:, bass.ds(i, 1)], ALU.is_ge, ALU.mult).then_inc(searched, 1)
                    dve.wait_ge(searched, i * 4 + (before + 3))
                    nc.vector.tensor_tensor(pref[:], pref[:], kept[:], ALU.bitwise_or).then_inc(searched, 1)
                    dve.wait_ge(searched, i * 4 + (before + 4))
                done[0] = before + 4 * BITS
                then(nc.vector.tensor_tensor(thr[:], pref[:], flip[:], ALU.bitwise_xor))
                assert done[0] == SEARCH * (place_of(qb) + 1)

            def break_ties(qb):
                n = keys(qb)
                s, eq, pl, b, t = score[:, qb % 2, 0:n], tied[:, 0:n], place[:, 0:n], bias[:, qb % 2, 0:n], thr[:].bitcast(F32)
                done = [TIES * place_of(qb)]

                def then(ins):
                    done[0] += 1
                    ins.then_inc(repaired, 1)
                    dve.wait_ge(repaired, done[0])

                then(nc.vector.tensor_scalar(eq, s, t, None, ALU.is_gt, ALU.add, accum_out=count[:, 4:5]))
                then(nc.vector.tensor_scalar(count[:, 5:6], count[:, 4:5], -1.0, float(TOP), ALU.mult, ALU.add))
                then(nc.vector.tensor_scalar(eq, s, t, None, ALU.is_equal))
                then(nc.vector.tensor_tensor_scan(pl, eq, eq, 0.0, ALU.add, ALU.bypass))
                then(nc.vector.scalar_tensor_tensor(pl, pl, count[:, 5:6], eq, ALU.is_le, ALU.mult))
                then(nc.vector.scalar_tensor_tensor(pl, s, t, pl, ALU.is_gt, ALU.add))
                then(nc.vector.tensor_scalar(b, pl, -1.0, -FAR, ALU.add, ALU.mult))
                assert done[0] == TIES * (place_of(qb) + 1)

            def check_selection(qb):
                i = place_of(qb)
                dve.wait_ge(report_summed, i + 1)
                nc.vector.tensor_copy(reported[:], report_ps).then_inc(report_read, 1)
                dve.wait_ge(report_read, i + 1)
                unequal = dve.value_load(reported[0:1, 0:1], min_val=0, max_val=P)
                unfound = dve.value_load(reported[0:1, 1:2], min_val=0, max_val=P)
                with dve.If(unfound != 0):
                    search(qb)
                with dve.If(unfound == 0):
                    nc.vector.tensor_copy(thr[:].bitcast(F32), cut[:]).then_inc(searched, 1)
                    dve.sem_inc(searched, SEARCH - 1)
                dve.wait_ge(searched, SEARCH * (i + 1))
                with dve.If(unequal != 0):
                    break_ties(qb)
                with dve.If(unequal == 0):
                    dve.sem_inc(repaired, TIES)
                dve.wait_ge(repaired, TIES * (i + 1))

            def attend(qb, nxt):
                n, each = keys(qb), len(parts(qb))
                heads = qb * HEADS
                if qb not in selecting:
                    dve.wait_ge(causal, qb + 1)

                def mask(h, m):
                    j, (at, w) = (heads + h) % DEEP, parts(qb)[m]
                    if m == 0 and heads + h >= DEEP:
                        dve.wait_ge(turned, group_at[divmod(heads + h - DEEP + 1, HEADS)])
                    p = number["attend", qb, h, m]
                    dve.wait_ge(product, p + 1)
                    before = FAR
                    if m:
                        dve.wait_ge(masked, masks[qb, h, m - 1] + 1)
                        before = top[:, j, m - 1:m]
                    nc.vector.tensor_tensor_reduce(out=arg[:, j, at:at + w], in0=pr[p % 2][:, 0:w], in1=bias[:, qb % 2, at:at + w], scale=1.0,
                                                   scalar=before, op0=ALU.add, op1=ALU.max, accum_out=top[:, j, m:m + 1]).then_inc(masked, 1)

                def negate(h):
                    dve.wait_ge(masked, masks[qb, h, each - 1] + 1)
                    j = (heads + h) % DEEP
                    nc.vector.tensor_scalar(minus_top[:, j:j + 1], top[:, j, each - 1:each], -1.0, None, ALU.mult).then_inc(negated, 1)

                for h in range(DEEP - 1):
                    for m in range(each):
                        mask(h, m)
                    negate(h)
                for h in range(HEADS):
                    ahead = h + DEEP - 1
                    halvings = range(2 * h, 2 * h + 2) if nxt and 2 * h < STEPS else ()
                    last_two = HEADS - 2 if nxt else HEADS
                    if halvings:
                        count_at_guess(nxt)
                    if h == last_two:
                        count_above(nxt)
                    if h == last_two + 1:
                        best_below(nxt)
                    if ahead < HEADS:
                        mask(ahead, 0)
                    if halvings:
                        decide(halvings[0])
                    if h == last_two:
                        drop_above(nxt)
                        find_short()
                    if h == last_two + 1:
                        pick()
                        find_cut()
                    if ahead < HEADS:
                        for m in range(1, each):
                            mask(ahead, m)
                        negate(ahead)
                    if halvings:
                        move(halvings[0])
                    if h == last_two + 1:
                        count_selected(nxt)
                    if halvings:
                        count_at_guess(nxt)
                        decide(halvings[1])
                        move(halvings[1])
                if nxt:
                    set_bias(nxt)
            assert 2 * (HEADS - 2) == STEPS
            for n, (_, hi, lo) in enumerate(key_rows):
                dve.wait_ge(key_hi, n + 1)
                nc.vector.tensor_tensor(lo, raw[:], hi.bitcast(F32), ALU.subtract).then_inc(key_lo, 1)
                if n == 0:
                    split_q(first_selecting)
                    split_q_attend(0)
            dve.wait_ge(bits_in, 64)
            dve.wait_ge(wi_left, 1)
            dve.wait_ge(v_left, TILES // 4)
            for kind, qb in order:
                if kind == "index":
                    if qb + 1 < TILES:
                        split_q(qb + 1)
                    add_scores(qb)
                    take_range(qb)
                    continue
                if qb + 1 < TILES:
                    split_q_attend(qb + 1)
                if qb in selecting:
                    check_selection(qb)
                attend(qb, qb + 1 if qb + 1 in selecting else None)

        @block.tensor
        def _(pe):
            pe.wait_ge(vw_in, 32)
            for t in range(TILES):
                ins = nc.tensor.transpose(turn[0][:, t * IDX_HEADS:(t + 1) * IDX_HEADS], wi_raw[:, t * P:t * P + P], ident[0:IDX_HEADS, 0:IDX_HEADS])
            ins.then_inc(wi_turned, 1)
            for g in range(TILES // 4):
                if g == 1:
                    pe.wait_ge(wi_left, 1)
                if g >= 2:
                    pe.wait_ge(v_left, g - 1)
                for t in range(4):
                    ins = nc.tensor.transpose(turn[(g + 1) % 2][:, t * P:t * P + P], v_raw[:, (g * 4 + t) * P:(g * 4 + t + 1) * P], ident[:])
                ins.then_inc(v_turned, 1)
            pe.wait_ge(key_lo, len(key_rows))
            pe.wait_ge(v_left, TILES // 4)
            pe.wait_ge(ones_set, 1)

            def scores(n):
                kind, qb, h, m, at, width = products[n]
                if h == 0 and m == 0:
                    pe.wait_ge(*((qi_lo, place_of(qb) + 1) if kind == "index" else (q_lo, qb + 1)))
                if n >= 2:
                    left(pe, n - 2)
                q = (qi_two if kind == "index" else q_two)[:, qb % 2, h, :]
                kv = h // (HEADS // KV_HEADS)
                for g, w in quads(at, width):
                    hi, lo = (ki_hi[:, g:g + w], ki_lo[:, g:g + w]) if kind == "index" else (k_hi[:, kv, g:g + w], k_lo[:, kv, g:g + w])
                    nc.tensor.matmul(pr[n % 2][:, g - at:g - at + w], q, hi, start=True, stop=False)
                    ins = nc.tensor.matmul(pr[n % 2][:, g - at:g - at + w], q, lo, start=False, stop=True)
                ins.then_inc(product, 1)

            def weigh(qb, h, m):
                n = keys(qb)
                t = qb * HEADS + h
                at, w = quads(0, n)[m]
                g = group_at[qb, h] + m
                if m == 0 and t >= 2:
                    pe.wait_ge(o_ready, t - 1)
                if m == 0 and h == 0 and qb in selecting:
                    pe.wait_ge(report_read, place_of(qb) + 1)
                pe.wait_ge(p_ready, g + 1)
                for c in range(0, w, P):
                    ins = nc.tensor.matmul(o_ps[t % 2][:], v_one[:, (at + c) // P, h // (HEADS // KV_HEADS), :], prob[:, g % 2, c:c + P],
                                           start=at + c == 0, stop=at + c + P == n)
                ins.then_inc(weighed, 1)

            def turn_one(qb, h, m):
                at, w = quads(0, keys(qb))[m]
                g = group_at[qb, h] + m
                if m == 0:
                    pe.wait_ge(raised, qb * HEADS + h + 1)
                if g >= 2:
                    pe.wait_ge(p_ready, g - 1)
                for c in range(0, w, P):
                    ins = nc.tensor.transpose(turn[g % 2][:, c:c + P], arg[:, (qb * HEADS + h) % DEEP, at + c:at + c + P], ident[:])
                ins.then_inc(turned, 1)

            for kind, qb in order:
                first = number[kind, qb, 0, 0]
                each = len(parts(qb))
                if kind == "index":
                    for n in range(HEADS * each):
                        scores(first + n)
                    continue
                if qb in selecting:
                    pe.wait_ge(selected, 2 * (place_of(qb) + 1))
                    pe.wait_ge(o_ready, qb * HEADS - 1)
                    nc.tensor.matmul(report_ps, v_one[:, 0, 0, HD:HD + 1], report[:], start=True, stop=True).then_inc(report_summed, 1)
                for n in range((DEEP - 1) * each):
                    scores(first + n)
                for h in range(HEADS):
                    if h + DEEP - 1 < HEADS:
                        for m in range(each):
                            scores(first + (h + DEEP - 1) * each + m)
                    groups = quads(0, keys(qb))
                    for m in range(len(groups)):
                        turn_one(qb, h, m)
                        if m:
                            weigh(qb, h, m - 1)
                    weigh(qb, h, len(groups) - 1)
def phase_out_2(nc, sem, xf, mix_t, p_t, w_out, gate_row, out):
    with ExitStack() as ctx:
        al = Alloc(nc, ctx)
        w_raw = al.sb("oc_w_raw", [P, 2, DM])
        w_hi = al.sb("oc_w_hi", [P, KC, DM], F32R)
        w_lo = al.sb("oc_w_lo", [P, KC, DM], F32R)
        m_raw = al.sb("oc_m_raw", [P, 2, KC, P])
        g_raw = al.sb("oc_g_raw", [P, 2, KC, P])
        m_hi = al.sb("oc_m_hi", [P, 2, KC, P], F32R)
        m_lo = al.sb("oc_m_lo", [P, 2, KC, P], F32R)
        xin = al.sb("oc_x", [P, 2, DM])
        y = al.sb("oc_y", [P, 2, DM])
        gate = al.sb("oc_gate", [P, DM])
        acc = [al.ps(f"oc_acc{j}", [P, DM]) for j in range(2)]
        w_in = [sem(f"oc_w_in{j}") for j in range(2)]
        m_in = [sem(f"oc_m_in{j}") for j in range(2)]
        x_in = [sem(f"oc_x_in{j}") for j in range(2)]
        y_out = [sem(f"oc_y_out{j}") for j in range(2)]
        gate_in, w_hi_done, w_lo_done, silued, gated = sem("oc_gate_in"), sem("oc_w_hi"), sem("oc_w_lo"), sem("oc_silued"), sem("oc_gated")
        m_hi_done, m_lo_done, product, scaled, added = sem("oc_m_hi"), sem("oc_m_lo"), sem("oc_product"), sem("oc_scaled"), sem("oc_added")
        w_v = w_out.rearrange("(k p) n -> k p n", p=P)
        m_v = mix_t.rearrange("(k p) (t n) -> t p k n", p=P, n=P)
        gp_v = p_t[ROW_GP:ROW_GP + 512, :].rearrange("(k p) (t n) -> t p k n", p=P, n=P)
        ga_v = p_t[ROW_GA:ROW_GA + 512, :].rearrange("(k p) (t n) -> t p k n", p=P, n=P)
        x_v = xf.rearrange("(t p) d -> t p d", p=P)
        o_v = out.rearrange("(t p) d -> t p d", p=P)
        PAIRS = TILES // 2
        HALF = KC // 2
        block = ctx.enter_context(nc.Block())

        @block.sync
        def _(sp):
            def load(tile, j):
                sp.dma_start(m_raw[:, j], tile(m_v, "a p k n -> (a p) k n")).then_inc(m_in[j], 16)
                sp.dma_start(g_raw[:, j, 0:HALF], tile(gp_v, "a p k n -> (a p) k n")).then_inc(m_in[j], 16)
                sp.dma_start(g_raw[:, j, HALF:], tile(ga_v, "a p k n -> (a p) k n")).then_inc(m_in[j], 16)

            def load_x(tile, j):
                sp.dma_start(xin[:, j], tile(x_v, "a p d -> (a p) d")).then_inc(x_in[j], 16)

            for j in range(2):
                load(lambda v, _: v[j], j)
            for k in range(KC):
                if k >= 2:
                    sp.wait_ge(w_lo_done, k - 1)
                sp.dma_start(w_raw[:, k % 2], w_v[k]).then_inc(w_in[k % 2], 16)
            sp.dma_start(gate[:], gate_row.partition_broadcast(P)).then_inc(gate_in, 16)
            for j in range(2):
                load_x(lambda v, _: v[j], j)
            with sp.Fori(0, PAIRS - 1) as i:
                for j in range(2):
                    sp.wait_ge(m_lo_done, i * 2 + (j + 1))
                    load(lambda v, r: v[bass.ds(i * 2 + (j + 2), 1)].rearrange(r), j)
                    sp.wait_ge(added, i * 2 + (j + 1))
                    sp.dma_start(o_v[bass.ds(i * 2 + j, 1)].rearrange("a p d -> (a p) d"), y[:, j]).then_inc(y_out[j], 16)
                    load_x(lambda v, r: v[bass.ds(i * 2 + (j + 2), 1)].rearrange(r), j)
            for j in range(2):
                sp.wait_ge(added, TILES - 1 + j)
                sp.dma_start(o_v[TILES - 2 + j], y[:, j]).then_inc(y_out[j], 16)
            for j in range(2):
                sp.wait_ge(y_out[j], 16 * PAIRS + 16)

        @block.scalar
        def _(act):
            for k in range(KC):
                act.wait_ge(w_in[k % 2], 16 * (k // 2 + 1))
                nc.scalar.activation(w_hi[:, k], w_raw[:, k % 2], ACT.Copy).then_inc(w_hi_done, 1)

            with act.Fori(0, PAIRS) as i:
                for j in range(2):
                    act.wait_ge(m_in[j], i * 48 + 48)
                    nc.scalar.activation(g_raw[:, j], g_raw[:, j], ACT.Silu).then_inc(silued, 1)
                    act.wait_ge(gated, i * 2 + (j + 1))
                    act.wait_ge(product, i * 2 + (j + 1))
                    nc.scalar.activation(m_hi[:, j], m_raw[:, j], ACT.Copy).then_inc(m_hi_done, 1)

        @block.vector
        def _(dve):
            for k in range(KC):
                dve.wait_ge(w_hi_done, k + 1)
                nc.vector.tensor_tensor(w_lo[:, k], w_raw[:, k % 2], w_hi[:, k].bitcast(F32), ALU.subtract).then_inc(w_lo_done, 1)

            def gates(t, j):
                dve.wait_ge(m_in[j], (t - j) * 24 + 48)
                dve.wait_ge(silued, t + 1)
                nc.vector.tensor_tensor(m_raw[:, j], m_raw[:, j], g_raw[:, j], ALU.mult).then_inc(gated, 1)
                dve.wait_ge(gated, t + 1)
                dve.wait_ge(m_hi_done, t + 1)
                nc.vector.tensor_tensor(m_lo[:, j], m_raw[:, j], m_hi[:, j].bitcast(F32), ALU.subtract).then_inc(m_lo_done, 1)

            def finish(t, j):
                dve.wait_ge(product, t + 3)
                dve.wait_ge(y_out[j], (t - j) * 8 + 16)
                nc.vector.tensor_tensor(y[:, j], acc[j][:], gate[:], ALU.mult).then_inc(scaled, 1)
                dve.wait_ge(scaled, t + 3)
                dve.wait_ge(x_in[j], (t - j) * 8 + 16)
                nc.vector.tensor_tensor(y[:, j], y[:, j], xin[:, j], ALU.add).then_inc(added, 1)

            dve.wait_ge(gate_in, 16)
            for j in range(2):
                gates(j, j)
            with dve.Fori(0, PAIRS - 1) as i:
                for j in range(2):
                    finish(i * 2 + j, j)
                    gates(i * 2 + (j + 2), j)
            for j in range(2):
                finish(TILES - 2 + j, j)

        @block.tensor
        def _(pe):
            pe.sem_inc(product, 2)
            pe.sem_inc(scaled, 2)
            for j in range(2):
                pe.sem_inc(y_out[j], 16)
            pe.wait_ge(w_lo_done, KC)
            with pe.Fori(0, PAIRS) as i:
                for j in range(2):
                    pe.wait_ge(m_lo_done, i * 2 + (j + 1))
                    pe.wait_ge(scaled, i * 2 + (j + 1))
                    for half in range(2):
                        cols = slice(half * 512, half * 512 + 512)
                        for k in range(KC):
                            for n, (w, a) in enumerate(split_pass_list(w_hi, w_lo, m_hi, m_lo)):
                                ins = nc.tensor.matmul(acc[j][:, cols], a[:, j, k, :], w[:, k, cols],
                                                       start=(k == 0 and n == 0), stop=(k == KC - 1 and n == 2))
                    ins.then_inc(product, 1)


def program(nc, a):
    def dram(name, shape):
        return nc.dram_tensor(name, shape, F32, kind="Internal").ap()

    y_t, x1, xn_t, kvqg_t = dram("d_y_t", [DM, SEQ]), dram("d_x1", [SEQ, DM]), dram("d_xn_t", [DM, SEQ]), dram("d_kvqg_t", [4 * 512, SEQ])
    o_t, gate_row, xf = dram("d_o_t", [512, SEQ]), dram("d_gate_row", [DM]), dram("d_xf", [SEQ, DM])
    p_t, rot_t, mix_t = dram("d_p_t", [D_PROJ, SEQ]), dram("d_rot_t", [ROT_ROWS, SEQ]), dram("d_mix_t", [DM, SEQ])
    @contextmanager
    def semaphores():
        taken = []

        def sem(name):
            taken.append(nc.alloc_semaphore(name=name))
            return taken[-1]

        yield sem
        nc.clear_and_free_semaphores(taken)
        nc.all_engine_barrier()

    def halves(ctx, name):
        al = Alloc(nc, ctx)
        return al.sb(name + "_hi", [P, KC, SEQ], F32R), al.sb(name + "_lo", [P, KC, SEQ], F32R)

    with ExitStack() as ctx:
        ident = Alloc(nc, ctx).sb("ident", [P, P])
        with ExitStack() as inner:
            xt = halves(inner, "h_a")
            with semaphores() as sem:
                phase_norm_x(nc, sem, a["x"][0], a["norm_a"][0], ident, *xt)
            with semaphores() as sem:
                phase_mixer(nc, sem, a["w_in_a"][0], a["conv_a"][0], *xt, y_t)
        with semaphores() as sem:
            phase_out_a(nc, sem, a["x"][0], a["w_out_a"][0], y_t, ident, x1, xn_t)
        with ExitStack() as inner, semaphores() as sem:
            phase_project(nc, sem, "pb", [a["w_kv"], a["w_in_b"][0]], [a["norm_kv"], a["norm_b"][0]], *halves(inner, "h_b"), kvqg_t, xn_t)
        with semaphores() as sem:
            phase_stick(nc, sem, kvqg_t, o_t, ident)
        with ExitStack() as inner:
            xt = halves(inner, "h_2")
            with ExitStack() as rows:
                al = Alloc(nc, rows)
                shift, scale_w = al.sb("shift", [P, DM]), al.sb("scale_w", [P, DM])
                with semaphores() as sem:
                    phase_modulation(nc, sem, a["c_2"][0], a["w_ada_2"][0], a["b_ada_2"][0], a["norm_w_2"][0], shift, scale_w, gate_row)
                with semaphores() as sem:
                    phase_out_b(nc, sem, x1, o_t, kvqg_t, a["w_out_b"][0], a["norm_f"], shift, scale_w, ident, xf, *xt)
            with semaphores() as sem:
                phase_project(nc, sem, "p2", [a["w_in_2"][0]], [None], *xt, p_t)
        with semaphores() as sem:
            phase_pool_rope(nc, sem, p_t, a["w_pool_2"][0], a["pool_scale_2"][0], a["q_norm_w_2"][0], a["k_norm_w_2"][0],
                            a["cos_t"], a["sin_t"], a["inv_count"], mix_t, rot_t)
        with semaphores() as sem:
            phase_select_attend(nc, sem, p_t, rot_t, a["bit_int"], a["bit_val"], a["half_powers"], a["rank_row"], mix_t, ident)
        with semaphores() as sem:
            phase_out_2(nc, sem, xf, mix_t, p_t, a["w_out_2"][0], gate_row, a["out"][0])


INPUTS = ("x", "norm_a", "w_in_a", "conv_a", "w_out_a", "norm_kv", "w_kv", "norm_b", "w_in_b", "w_out_b", "norm_f", "c_2",
          "norm_w_2", "w_ada_2", "b_ada_2", "w_in_2", "q_norm_w_2", "k_norm_w_2", "w_pool_2", "pool_scale_2", "w_out_2")


def shape_constants():
    half = HD // 2
    freqs = np.float32(10000.0) ** (-np.arange(half, dtype=np.float32) / np.float32(half))
    angle = (np.arange(SEQ, dtype=np.float32)[:, None] * freqs[None, :]).astype(np.float32).T
    cos, sin = np.cos(angle), np.sin(angle)
    counts = np.minimum(np.arange(1, HALO + 1)[None, :], np.array(WINDOWS)[:, None]).astype(np.float32)
    bits = (1 << np.arange(30, -1, -1)).astype(np.int32)
    return {"cos_t": np.tile(cos, (4, 1)).astype(np.float32), "sin_t": np.concatenate([-sin, sin, -sin, sin]).astype(np.float32),
            "inv_count": (np.float32(1) / counts).astype(np.float32), "bit_int": bits, "bit_val": bits.astype(np.float32),
            "half_powers": (np.float32(0.5) ** np.arange(1, 13)).astype(np.float32), "rank_row": np.arange(17, dtype=np.float32)}


def kernel(**inputs):
    import concourse.bacc as bacc
    from concourse.bass_utils import run_bass_kernel_spmd

    nc = bacc.Bacc("TRN2", target_bir_lowering=False, num_devices=1)
    arrays = {name: np.ascontiguousarray(inputs[name]) for name in INPUTS}
    arrays.update(shape_constants())
    a = {name: nc.dram_tensor("in_" + name, v.shape, mybir.dt.from_np(v.dtype), kind="ExternalInput").ap() for name, v in arrays.items()}
    a["out"] = nc.dram_tensor("out", [1, SEQ, DM], F32, kind="ExternalOutput").ap()
    program(nc, a)
    r = run_bass_kernel_spmd(nc, [{"in_" + name: v for name, v in arrays.items()}], core_ids=[0])
    return r.results[0]["out"]
```

```python
import concourse.bass as bass
import numpy as np
from concourse import mybir
from contextlib import ExitStack, contextmanager

F32 = mybir.dt.float32
F32R = mybir.dt.float32r
ALU = mybir.AluOpType
ACT = mybir.ActivationFunctionType

P = 128
SEQ, DM = 2048, 1024
TILES = SEQ // P
KC = DM // P
NT = SEQ // 512
EPS = 1e-6


class Alloc:

    def __init__(self, nc, ctx):
        self.nc, self.ctx = nc, ctx

    def sb(self, name, shape, dt=F32):
        return self.ctx.enter_context(self.nc.sbuf_tensor("s_" + name, shape, dt))

    def ps(self, name, shape, dt=F32):
        return self.ctx.enter_context(self.nc.psum_tensor("p_" + name, shape, dt))


def split_pass_list(w_hi, w_lo, a_hi, a_lo):
    return ((w_hi, a_hi), (w_hi, a_lo), (w_lo, a_hi))


def phase_norm_x(nc, sem, x, norm_a, ident, xt_hi, xt_lo):
    with ExitStack() as ctx:
        al = Alloc(nc, ctx)
        xin = al.sb("nx_xin", [P, 2, DM])
        xn = al.sb("nx_xn", [P, 2, DM])
        junk = al.sb("nx_junk", [P, 2, DM])
        norm_b = al.sb("nx_norm", [P, DM])
        ss = al.sb("nx_ss", [P, 8])
        root = al.sb("nx_root", [P, 8])
        rinv = al.sb("nx_rinv", [P, 8])
        eps = al.sb("nx_eps", [P, 1])
        pt = [al.ps(f"nx_pt{j}", [P, KC, P]) for j in range(2)]
        x_in = [sem(f"nx_x_in{j}") for j in range(2)]
        norm_in, ready = sem("nx_norm_in"), sem("nx_ready")
        squared, rooted, inverted, normed = sem("nx_squared"), sem("nx_rooted"), sem("nx_inverted"), sem("nx_normed")
        transposed, hi_done, lo_done = sem("nx_transposed"), sem("nx_hi_done"), sem("nx_lo_done")
        x_v = x.rearrange("(t p) d -> t p d", p=P)
        block = ctx.enter_context(nc.Block())

        @block.sync
        def _(sp):
            sp.dma_start(norm_b[:], norm_a.partition_broadcast(P)).then_inc(norm_in, 16)
            for j in range(2):
                sp.dma_start(xin[:, j], x_v[j]).then_inc(x_in[j], 16)
            with sp.Fori(1, TILES // 2) as i:
                for j in range(2):
                    sp.wait_ge(normed, i * 2 + (j - 1))
                    sp.dma_start(xin[:, j], x_v[bass.ds(i * 2 + j, 1)].rearrange("a p d -> (a p) d")).then_inc(x_in[j], 16)

        @block.gpsimd
        def _(pool):
            nc.gpsimd.memset(eps[:], EPS).then_inc(ready, 1)
            nc.gpsimd.memset(ident[:], 0.0).then_inc(ready, 1)
            pool.wait_ge(ready, 2)
            nc.gpsimd.affine_select(out=ident[:], in_=ident[:], compare_op=ALU.not_equal, fill=1.0, base=0,
                                    pattern=[[-1, P]], channel_multiplier=1).then_inc(ready, 1)

        @block.scalar
        def _(act):
            nc.scalar.preload_act_table(ACT.Sqrt)
            act.wait_ge(ready, 3)
            with act.Fori(0, TILES // 2) as i:
                for j in range(2):
                    act.wait_ge(x_in[j], i * 16 + 16)
                    nc.scalar.activation(junk[:, j], xin[:, j], ACT.Square, accum_out=ss[:, 4 * j:4 * j + 1]).then_inc(squared, 1)
                    act.wait_ge(squared, i * 2 + (j + 1))
                    nc.scalar.activation(root[:, 4 * j:4 * j + 1], ss[:, 4 * j:4 * j + 1], ACT.Sqrt, bias=eps[:], scale=1.0 / DM).then_inc(rooted, 1)
                for j in range(2):
                    act.wait_ge(transposed, i * 2 + (j + 1))
                    nc.scalar.activation(xt_hi[:, :, bass.ds((i * 2 + j) * P, P)], pt[j][:], ACT.Copy).then_inc(hi_done, 1)

        @block.vector
        def _(dve):
            dve.wait_ge(norm_in, 16)
            with dve.Fori(0, TILES // 2) as i:
                for j in range(2):
                    dve.wait_ge(rooted, i * 2 + (j + 1))
                    nc.vector.reciprocal(rinv[:, 4 * j:4 * j + 1], root[:, 4 * j:4 * j + 1]).then_inc(inverted, 1)
                    dve.wait_ge(inverted, i * 2 + (j + 1))
                    nc.vector.scalar_tensor_tensor(xn[:, j], xin[:, j], rinv[:, 4 * j:4 * j + 1], norm_b[:],
                                                   ALU.mult, ALU.mult).then_inc(normed, 1)
                for j in range(2):
                    dve.wait_ge(hi_done, i * 2 + (j + 1))
                    nc.vector.tensor_tensor(xt_lo[:, :, bass.ds((i * 2 + j) * P, P)], pt[j][:],
                                            xt_hi[:, :, bass.ds((i * 2 + j) * P, P)].bitcast(F32), ALU.subtract).then_inc(lo_done, 1)

        @block.tensor
        def _(pe):
            pe.wait_ge(ready, 3)
            for j in range(2):
                pe.sem_inc(lo_done, 1)
            with pe.Fori(0, TILES // 2) as i:
                for j in range(2):
                    pe.wait_ge(normed, i * 2 + (j + 1))
                    pe.wait_ge(lo_done, i * 2 + (j + 1))
                    for k in range(KC):
                        ins = nc.tensor.transpose(pt[j][:, k, :], xn[:, j, k * P:(k + 1) * P], ident[:])
                    ins.then_inc(transposed, 1)


def phase_mixer(nc, sem, w_in_a, conv_a, xt_hi, xt_lo, y_t):
    with ExitStack() as ctx:
        al = Alloc(nc, ctx)
        raw = al.sb("mx_raw", [P, 4, KC, P])
        w_hi = al.sb("mx_w_hi", [P, 4, KC, P], F32R)
        w_lo = al.sb("mx_w_lo", [P, 4, KC, P], F32R)
        c_sb = al.sb("mx_c", [P, SEQ])
        u = al.sb("mx_u", [P, SEQ + 2])
        y = al.sb("mx_y", [P, SEQ])
        cw = al.sb("mx_cw", [P, KC, 3])
        ps = [al.ps(f"mx_ps{s}", [P, SEQ]) for s in range(2)]
        ORDER = (1, 2, 3, 0)
        w_in = [sem(f"mx_w_in{j}") for j in range(4)]
        cw_in, hi_done, lo_done, product = sem("mx_cw_in"), sem("mx_hi_done"), sem("mx_lo_done"), sem("mx_product")
        c_ready, g_ready, u_ready = sem("mx_c_ready"), sem("mx_g_ready"), sem("mx_u_ready")
        chain, y_ready, y_out = sem("mx_chain"), sem("mx_y_ready"), sem("mx_y_out")
        w_v = w_in_a.rearrange("(k p) (b e n) -> b e p k n", p=P, b=4, n=P)
        y_v = y_t.rearrange("(e p) t -> e p t", p=P)
        block = ctx.enter_context(nc.Block())

        @block.sync
        def _(sp):
            with nc.allow_non_contiguous_dma(reason="three taps of each channel, once"):
                for tap in range(3):
                    sp.dma_start(cw[:, :, tap], conv_a[tap].rearrange("(e p) -> p e", p=P)).then_inc(cw_in, 16)
            for j in range(4):
                sp.dma_start(raw[:, j], w_v[ORDER[j], 0]).then_inc(w_in[j], 16)
            with sp.Fori(1, KC) as e:
                sp.wait_ge(lo_done, e * 4)
                for j in range(4):
                    sp.dma_start(raw[:, j], w_v[ORDER[j]][bass.ds(e, 1)].rearrange("a p k n -> (a p) k n")).then_inc(w_in[j], 16)
                sp.wait_ge(y_ready, e + 1)
                sp.dma_start(y_v[bass.ds(e - 1, 1)].rearrange("a p t -> (a p) t"), y[:]).then_inc(y_out, 16)
            sp.wait_ge(y_ready, KC + 1)
            sp.dma_start(y_v[KC - 1], y[:]).then_inc(y_out, 16)
            sp.wait_ge(y_out, 16 * KC + 16)

        def split_hi(act, e, j):
            act.wait_ge(w_in[j], e * 16 + 16)
            act.wait_ge(product, e * 4 + (j + 1))
            nc.scalar.activation(w_hi[:, j], raw[:, j], ACT.Copy).then_inc(hi_done, 1)

        @block.scalar
        def _(act):
            with act.Fori(0, KC) as e:
                for j in range(4):
                    split_hi(act, e, j)
                act.wait_ge(product, e * 4 + 5)
                act.wait_ge(y_ready, e + 1)
                nc.scalar.activation(c_sb[:], ps[0][:], ACT.Copy).then_inc(c_ready, 1)
                act.wait_ge(product, e * 4 + 7)
                act.wait_ge(u_ready, e + 1)
                nc.scalar.activation(c_sb[:], ps[0][:], ACT.Silu).then_inc(g_ready, 1)

        @block.vector
        def _(dve):
            nc.vector.memset(u[:, 0:2], 0.0)
            dve.wait_ge(cw_in, 48)

            def lo(e, j):
                dve.wait_ge(hi_done, e * 4 + (j + 1))
                nc.vector.tensor_tensor(w_lo[:, j], raw[:, j], w_hi[:, j].bitcast(F32), ALU.subtract).then_inc(lo_done, 1)

            def convolve(e):
                dve.wait_ge(product, e * 4 + 6)
                dve.wait_ge(c_ready, e + 1)
                nc.vector.tensor_tensor(u[:, 2:], ps[1][:], c_sb[:], ALU.mult).then_inc(u_ready, 1)
                dve.wait_ge(u_ready, e + 1)
                dve.wait_ge(y_out, e * 16 + 16)
                taps = cw[:, e, :] if isinstance(e, int) else cw[:, bass.ds(e, 1), :].rearrange("p a n -> p (a n)")
                nc.vector.tensor_scalar(y[:], u[:, 0:SEQ], taps[:, 0:1], None, ALU.mult).then_inc(chain, 1)
                for tap in (1, 2):
                    dve.wait_ge(chain, e * 4 + tap)
                    nc.vector.scalar_tensor_tensor(y[:], u[:, tap:tap + SEQ], taps[:, tap:tap + 1], y[:],
                                                   ALU.mult, ALU.add).then_inc(chain, 1)
                dve.wait_ge(chain, e * 4 + 3)
                dve.wait_ge(g_ready, e + 2)
                nc.vector.tensor_tensor(y[:], y[:], c_sb[:], ALU.mult).then_inc(chain, 1)

            def gate(e):
                dve.wait_ge(chain, e * 4 + 4)
                dve.wait_ge(product, e * 4 + 8)
                nc.vector.tensor_tensor(y[:], y[:], ps[1][:], ALU.mult).then_inc(y_ready, 1)

            for j in range(4):
                lo(0, j)
            with dve.Fori(0, KC - 1) as e:
                convolve(e)
                for j in range(3):
                    lo(e + 1, j)
                gate(e)
                lo(e + 1, 3)
            convolve(KC - 1)
            gate(KC - 1)

        @block.tensor
        def _(pe):
            pe.sem_inc(product, 4)
            pe.sem_inc(y_out, 16)
            pe.sem_inc(y_ready, 1)
            pe.sem_inc(g_ready, 1)
            with pe.Fori(0, KC) as e:
                for j in range(4):
                    pe.wait_ge(lo_done, e * 4 + (j + 1))
                    left, before = ((g_ready, 1), (y_ready, 1), (c_ready, 1), (u_ready, 1))[j]
                    pe.wait_ge(left, e + before)
                    for k in range(KC):
                        for n, (w, a) in enumerate(split_pass_list(w_hi, w_lo, xt_hi, xt_lo)):
                            for t in range(NT):
                                ins = nc.tensor.matmul(ps[j % 2][:, t * 512:(t + 1) * 512], w[:, j, k, :], a[:, k, t * 512:(t + 1) * 512],
                                                       start=(k == 0 and n == 0), stop=(k == KC - 1 and n == 2))
                    ins.then_inc(product, 1)
def phase_out_a(nc, sem, x, w_out_a, y_t, ident, x1, xn_t):
    with ExitStack() as ctx:
        al = Alloc(nc, ctx)
        w_raw = al.sb("oa_w_raw", [P, 2, DM])
        w_hi = al.sb("oa_w_hi", [P, KC, DM], F32R)
        w_lo = al.sb("oa_w_lo", [P, KC, DM], F32R)
        y_raw = al.sb("oa_y_raw", [P, 2, KC, P])
        y_hi = al.sb("oa_y_hi", [P, 2, KC, P], F32R)
        y_lo = al.sb("oa_y_lo", [P, 2, KC, P], F32R)
        xin = al.sb("oa_x", [P, 2, DM])
        xo = al.sb("oa_x1", [P, 2, DM])
        xn = al.sb("oa_xn", [P, 2, DM])
        junk = al.sb("oa_junk", [P, 2, DM])
        stage = al.sb("oa_stage", [P, 2, KC, P])
        eps = al.sb("oa_eps", [P, 1])
        ss = al.sb("oa_ss", [P, 8])
        root = al.sb("oa_root", [P, 8])
        rinv = al.sb("oa_rinv", [P, 8])
        acc = [al.ps(f"oa_acc{j}", [P, DM]) for j in range(2)]
        pt = [al.ps(f"oa_pt{j}", [P, KC, P]) for j in range(2)]
        w_in = [sem(f"oa_w_in{j}") for j in range(2)]
        y_in = [sem(f"oa_y_in{j}") for j in range(2)]
        x_in = [sem(f"oa_x_in{j}") for j in range(2)]
        x1_out = [sem(f"oa_x1_out{j}") for j in range(2)]
        t_out = [sem(f"oa_t_out{j}") for j in range(2)]
        w_hi_done, w_lo_done, y_hi_done, y_lo_done = sem("oa_w_hi"), sem("oa_w_lo"), sem("oa_y_hi"), sem("oa_y_lo")
        product, added, squared, rooted = sem("oa_product"), sem("oa_added"), sem("oa_squared"), sem("oa_rooted")
        inverted, normed, transposed, staged, ready = (sem("oa_inverted"), sem("oa_normed"), sem("oa_transposed"),
                                                       sem("oa_staged"), sem("oa_ready"))
        w_v = w_out_a.rearrange("(k p) n -> k p n", p=P)
        y_v = y_t.rearrange("(k p) (t n) -> t p k n", p=P, n=P)
        x_v = x.rearrange("(t p) d -> t p d", p=P)
        x1_v = x1.rearrange("(t p) d -> t p d", p=P)
        xn_v = xn_t.rearrange("(k p) (t n) -> t p k n", p=P, n=P)
        PAIRS = TILES // 2
        block = ctx.enter_context(nc.Block())

        @block.sync
        def _(sp):
            def load(tile_y, tile_x, j):
                sp.dma_start(y_raw[:, j], tile_y).then_inc(y_in[j], 16)
                sp.dma_start(xin[:, j], tile_x).then_inc(x_in[j], 16)

            for j in range(2):
                load(y_v[j], x_v[j], j)
            for k in range(KC):
                if k >= 2:
                    sp.wait_ge(w_lo_done, k - 1)
                sp.dma_start(w_raw[:, k % 2], w_v[k]).then_inc(w_in[k % 2], 16)
            with sp.Fori(0, PAIRS - 1) as i:
                for j in range(2):
                    sp.wait_ge(added, i * 2 + (j + 3))
                    sp.dma_start(x1_v[bass.ds(i * 2 + j, 1)].rearrange("a p d -> (a p) d"), xo[:, j]).then_inc(x1_out[j], 16)
                    sp.wait_ge(y_lo_done, i * 2 + (j + 1))
                    load(y_v[bass.ds(i * 2 + (j + 2), 1)].rearrange("a p k n -> (a p) k n"),
                         x_v[bass.ds(i * 2 + (j + 2), 1)].rearrange("a p d -> (a p) d"), j)
            for j in range(2):
                sp.wait_ge(added, TILES + j + 1)
                sp.dma_start(x1_v[TILES - 2 + j], xo[:, j]).then_inc(x1_out[j], 16)
            for j in range(2):
                sp.wait_ge(x1_out[j], 16 * PAIRS + 16)
                sp.wait_ge(t_out[j], 16 * PAIRS + 16)

        @block.gpsimd
        def _(pool):
            nc.gpsimd.memset(eps[:], EPS).then_inc(ready, 1)

        @block.scalar
        def _(act):
            nc.scalar.preload_act_table(ACT.Sqrt)
            act.wait_ge(ready, 1)

            def hi(t, j):
                act.wait_ge(y_in[j], (t - j) * 8 + 16)
                act.wait_ge(product, t + 1)
                nc.scalar.activation(y_hi[:, j], y_raw[:, j], ACT.Copy).then_inc(y_hi_done, 1)

            def stats(t, j):
                act.wait_ge(added, t + 3)
                nc.scalar.activation(junk[:, j], xo[:, j], ACT.Square, accum_out=ss[:, 4 * j:4 * j + 1]).then_inc(squared, 1)
                act.wait_ge(squared, t + 1)
                nc.scalar.activation(root[:, 4 * j:4 * j + 1], ss[:, 4 * j:4 * j + 1], ACT.Sqrt, bias=eps[:], scale=1.0 / DM).then_inc(rooted, 1)

            def leave(t, j):
                act.wait_ge(transposed, t + 3)
                act.wait_ge(t_out[j], (t - j) * 8 + 16)
                nc.scalar.activation(stage[:, j], pt[j][:], ACT.Copy).then_inc(staged, 1)
                act.wait_ge(staged, t + 1)
                act.dma_start(xn_v[bass.ds(t, 1)].rearrange("a p k n -> (a p) k n"), stage[:, j]).then_inc(t_out[j], 16)

            for k in range(KC):
                act.wait_ge(w_in[k % 2], 16 * (k // 2 + 1))
                nc.scalar.activation(w_hi[:, k], w_raw[:, k % 2], ACT.Copy).then_inc(w_hi_done, 1)
            for j in range(2):
                hi(j, j)
            with act.Fori(0, PAIRS - 1) as i:
                for j in range(2):
                    stats(i * 2 + j, j)
                    hi(i * 2 + (j + 2), j)
                    leave(i * 2 + j, j)
            for j in range(2):
                stats(TILES - 2 + j, j)
                leave(TILES - 2 + j, j)

        @block.vector
        def _(dve):
            for k in range(KC):
                dve.wait_ge(w_hi_done, k + 1)
                nc.vector.tensor_tensor(w_lo[:, k], w_raw[:, k % 2], w_hi[:, k].bitcast(F32), ALU.subtract).then_inc(w_lo_done, 1)

            def lo(t, j):
                dve.wait_ge(y_hi_done, t + 1)
                nc.vector.tensor_tensor(y_lo[:, j], y_raw[:, j], y_hi[:, j].bitcast(F32), ALU.subtract).then_inc(y_lo_done, 1)

            def add(t, j):
                dve.wait_ge(product, t + 3)
                dve.wait_ge(x_in[j], (t - j) * 8 + 16)
                dve.wait_ge(x1_out[j], (t - j) * 8 + 16)
                nc.vector.tensor_tensor(xo[:, j], acc[j][:], xin[:, j], ALU.add).then_inc(added, 1)

            def norm(t, j):
                dve.wait_ge(rooted, t + 1)
                nc.vector.reciprocal(rinv[:, 4 * j:4 * j + 1], root[:, 4 * j:4 * j + 1]).then_inc(inverted, 1)
                dve.wait_ge(inverted, t + 1)
                dve.wait_ge(transposed, t + 1)
                nc.vector.tensor_scalar(xn[:, j], xo[:, j], rinv[:, 4 * j:4 * j + 1], None, ALU.mult).then_inc(normed, 1)

            for j in range(2):
                lo(j, j)
            with dve.Fori(0, PAIRS - 1) as i:
                for j in range(2):
                    add(i * 2 + j, j)
                    lo(i * 2 + (j + 2), j)
                    norm(i * 2 + j, j)
            for j in range(2):
                add(TILES - 2 + j, j)
                norm(TILES - 2 + j, j)

        @block.tensor
        def _(pe):
            pe.sem_inc(product, 2)
            pe.sem_inc(added, 2)
            pe.sem_inc(transposed, 2)
            for j in range(2):
                pe.sem_inc(x1_out[j], 16)
                pe.sem_inc(t_out[j], 16)

            def multiply(t, j):
                pe.wait_ge(y_lo_done, t + 1)
                pe.wait_ge(added, t + 1)
                for half in range(2):
                    cols = slice(half * 512, half * 512 + 512)
                    for k in range(KC):
                        for n, (w, a) in enumerate(split_pass_list(w_hi, w_lo, y_hi, y_lo)):
                            ins = nc.tensor.matmul(acc[j][:, cols], a[:, j, k, :], w[:, k, cols],
                                                   start=(k == 0 and n == 0), stop=(k == KC - 1 and n == 2))
                ins.then_inc(product, 1)

            def transpose(t, j):
                pe.wait_ge(normed, t + 1)
                pe.wait_ge(t_out[j], (t - j) * 8 + 16)
                for k in range(KC):
                    ins = nc.tensor.transpose(pt[j][:, k, :], xn[:, j, k * P:(k + 1) * P], ident[:])
                ins.then_inc(transposed, 1)

            pe.wait_ge(w_lo_done, KC)
            multiply(0, 0)
            with pe.Fori(0, PAIRS - 1) as i:
                multiply(i * 2 + 1, 1)
                transpose(i * 2, 0)
                multiply(i * 2 + 2, 0)
                transpose(i * 2 + 1, 1)
            multiply(TILES - 1, 1)
            transpose(TILES - 2, 0)
            transpose(TILES - 1, 1)


def phase_project(nc, sem, pre, weights, norms, xt_hi, xt_lo, out_t, xt_src, c_in, w_ada, b_ada, mod_row):
    MOD = 3 * DM // 2
    with ExitStack() as ctx:
        al = Alloc(nc, ctx)
        raw = al.sb(pre + "_raw", [P, 2, KC, P])
        w_hi = al.sb(pre + "_w_hi", [P, 2, KC, P], F32R)
        w_lo = al.sb(pre + "_w_lo", [P, 2, KC, P], F32R)
        stage = al.sb(pre + "_stage", [P, 2, SEQ])
        x_raw = al.sb(pre + "_x_raw", [P, 2, SEQ])
        ada = [x_raw[:, j, 0:MOD] for j in range(2)]
        mod = al.sb(pre + "_mod", [P, 2, MOD])
        c_col = al.sb(pre + "_c", [P, KC])
        ones = al.sb(pre + "_ones", [P, 1])
        scale = al.sb(pre + "_scale", [P, len(weights), KC])
        ps = [al.ps(f"{pre}_ps{j}", [P, SEQ]) for j in range(2)]
        w_in = [sem(f"{pre}_w_in{j}") for j in range(2)]
        x_in = [sem(f"{pre}_x_in{j}") for j in range(2)]
        out_done = [sem(f"{pre}_out{j}") for j in range(2)]
        ada_in = [sem(f"{pre}_ada_in{j}") for j in range(2)]
        c_ready, mod_ready, mod_in, mod_added, mod_summed, mod_staged, mod_out = (sem(pre + "_c_ready"), sem(pre + "_mod_ready"), sem(pre + "_mod_in"), sem(pre + "_mod_added"),
                                                                      sem(pre + "_mod_summed"), sem(pre + "_mod_staged"), sem(pre + "_mod_out"))
        ada_v = w_ada.rearrange("(k p) (h n) -> h k p n", p=P, h=2)
        n_in, scaled, hi_done, lo_done = sem(pre + "_n_in"), sem(pre + "_scaled"), sem(pre + "_hi"), sem(pre + "_lo")
        x_hi, x_lo, product, staged = sem(pre + "_x_hi"), sem(pre + "_x_lo"), sem(pre + "_product"), sem(pre + "_staged")
        w_v, base, blocks, tails = [], [], [], []
        at = 0
        for w in weights:
            full = w.shape[1] // P // 2 * 2
            w_v.append(w[:, :full * P].rearrange("(k p) (b n) -> b p k n", p=P, n=P))
            base.append(at)
            blocks.append(full)
            at += full
        total = at
        assert total == 2 * KC
        out_v = out_t[0:total * P, :].rearrange("(b p) t -> b p t", p=P)
        block = ctx.enter_context(nc.Block())

        @block.sync
        def _(sp):
            with nc.allow_non_contiguous_dma(reason="a norm's weight, once"):
                for n, norm in enumerate(norms):
                    if norm is not None:
                        sp.dma_start(scale[:, n], norm.rearrange("(k p) -> p k", p=P)).then_inc(n_in, 16)
            for j in range(2):
                sp.dma_start(raw[:, j], w_v[0][j]).then_inc(w_in[j], 16)
            x_v = xt_src.rearrange("(k p) t -> k p t", p=P)
            for k in range(KC):
                if k >= 2:
                    sp.wait_ge(x_lo, k - 1)
                sp.dma_start(x_raw[:, k % 2], x_v[k]).then_inc(x_in[k % 2], 16)
            with nc.allow_non_contiguous_dma(reason="one vector, once"):
                sp.dma_start(c_col[:], c_in.rearrange("(k p) -> p k", p=P)).then_inc(mod_in, 16)
            sp.wait_ge(mod_ready, 1)
            for h in range(2):
                sp.dma_start(mod[0:1, h], b_ada[h * MOD:h * MOD + MOD].rearrange("(a n) -> a n", a=1)).then_inc(mod_in, 16)
            sp.wait_ge(x_lo, KC)
            for j in range(2):
                sp.dma_start(ada[j], ada_v[j, 0]).then_inc(ada_in[j], 16)

            def load_ada(k, j):
                sp.wait_ge(mod_added, k * 2 + (j - 1))
                sp.dma_start(ada[j], ada_v[j, bass.ds(k, 1)].rearrange("a p n -> (a p) n")).then_inc(ada_in[j], 16)

            def store(b, j):
                sp.wait_ge(staged, b + 3)
                sp.dma_start(out_v[bass.ds(b, 1)].rearrange("a p t -> (a p) t"), stage[:, j]).then_inc(out_done[j], 16)

            for n in range(len(weights)):
                with sp.Fori(0, blocks[n] // 2 - 1) as i:
                    for j in range(2):
                        sp.wait_ge(lo_done, i * 2 + (base[n] + j + 1))
                        sp.dma_start(raw[:, j], w_v[n][bass.ds(i * 2 + (j + 2), 1)].rearrange("a p k n -> (a p) k n")).then_inc(w_in[j], 16)
                        store(i * 2 + (base[n] + j), j)
                        load_ada(i + (base[n] // 2 + 1), j)
                for j in range(2):
                    sp.wait_ge(lo_done, base[n] + blocks[n] - 1 + j)
                    if n + 1 < len(weights):
                        sp.dma_start(raw[:, j], w_v[n + 1][j]).then_inc(w_in[j], 16)
                    store(base[n] + blocks[n] - 2 + j, j)
                    if n + 1 < len(weights):
                        k = (base[n] + blocks[n]) // 2
                        sp.wait_ge(mod_added, k * 2 + (j - 1))
                        sp.dma_start(ada[j], ada_v[j, k]).then_inc(ada_in[j], 16)
            sp.wait_ge(mod_staged, 2)
            for h in range(2):
                sp.dma_start(mod_row[h * MOD:h * MOD + MOD].rearrange("(a n) -> a n", a=1), mod[0:1, h]).then_inc(mod_out, 16)
            for j in range(2):
                sp.wait_ge(out_done[j], 8 * total + 16)
            sp.wait_ge(mod_out, 32)

        @block.gpsimd
        def _(pool):
            nc.gpsimd.memset(mod[:], 0.0).then_inc(mod_ready, 1)
            nc.gpsimd.memset(ones[:], 1.0).then_inc(mod_ready, 1)

        @block.scalar
        def _(act):
            nc.scalar.preload_act_table(ACT.Silu)
            for k in range(KC):
                act.wait_ge(x_in[k % 2], 16 * (k // 2 + 1))
                nc.scalar.activation(xt_hi[:, k], x_raw[:, k % 2], ACT.Copy).then_inc(x_hi, 1)
            act.wait_ge(mod_in, 48)
            nc.scalar.activation(c_col[:], c_col[:], ACT.Silu).then_inc(c_ready, 1)

            def hi(b, j):
                act.wait_ge(scaled, b + 1)
                act.wait_ge(product, b + 1)
                nc.scalar.activation(w_hi[:, j], raw[:, j], ACT.Copy).then_inc(hi_done, 1)

            def leave(b, j, n):
                act.wait_ge(product, b + 3)
                act.wait_ge(out_done[j], (b - j) * 8 + 16)
                nc.scalar.activation(stage[:, j], ps[j][:], ACT.Silu if n == len(weights) - 1 else ACT.Copy).then_inc(staged, 1)

            hi(0, 0)
            for n in range(len(weights)):
                with act.Fori(0, blocks[n] // 2 - 1) as i:
                    for j in range(2):
                        hi(i * 2 + (base[n] + j + 1), 1 - j)
                        leave(i * 2 + (base[n] + j), j, n)
                last = base[n] + blocks[n] - 2
                hi(last + 1, 1)
                leave(last, 0, n)
                if n + 1 < len(weights):
                    hi(last + 2, 0)
                leave(last + 1, 1, n)

        @block.vector
        def _(dve):
            dve.wait_ge(n_in, 16 * len(norms))
            for k in range(KC):
                dve.wait_ge(x_hi, k + 1)
                nc.vector.tensor_tensor(xt_lo[:, k], x_raw[:, k % 2], xt_hi[:, k].bitcast(F32), ALU.subtract).then_inc(x_lo, 1)
            dve.wait_ge(mod_in, 48)
            dve.wait_ge(c_ready, 1)

            def split(b, j, n):
                dve.wait_ge(w_in[j], (b - j) * 8 + 16)
                nc.vector.tensor_tensor(raw[:, j], raw[:, j], scale[:, n].unsqueeze(2).to_broadcast([P, KC, P]), ALU.mult).then_inc(scaled, 1)
                dve.wait_ge(scaled, b + 1)
                dve.wait_ge(hi_done, b + 1)
                nc.vector.tensor_tensor(w_lo[:, j], raw[:, j], w_hi[:, j].bitcast(F32), ALU.subtract).then_inc(lo_done, 1)

            def modulate(b, k, j):
                dve.wait_ge(ada_in[j], (b - j) * 8 + 16)
                if not isinstance(k, int) or k:
                    dve.wait_ge(mod_added, b - 1)
                c = c_col[:, k:k + 1] if isinstance(k, int) else c_col[:, bass.ds(k, 1)]
                nc.vector.scalar_tensor_tensor(mod[:, j], ada[j], c, mod[:, j], ALU.mult, ALU.add).then_inc(mod_added, 1)

            split(0, 0, 0)
            for j in range(2):
                split(j + 1, 1 - j, 0)
                modulate(j, 0, j)
            for n in range(len(weights)):
                skipped = 1 if n == 0 else 0
                with dve.Fori(skipped, blocks[n] // 2 - 1) as i:
                    for j in range(2):
                        split(i * 2 + (base[n] + j + 1), 1 - j, n)
                        modulate(i * 2 + (base[n] + j), i + base[n] // 2, j)
                last = base[n] + blocks[n] - 2
                split(last + 1, 1, n)
                modulate(last, last // 2, 0)
                if n + 1 < len(weights):
                    split(last + 2, 0, n + 1)
                modulate(last + 1, last // 2, 1)
            for h in range(2):
                dve.wait_ge(mod_summed, h + 1)
                nc.vector.tensor_copy(mod[0:1, h], ps[h][0:1, 0:MOD]).then_inc(mod_staged, 1)

        @block.tensor
        def _(pe):
            pe.sem_inc(product, 2)
            pe.sem_inc(staged, 2)
            for j in range(2):
                pe.sem_inc(out_done[j], 16)

            def body(b, j, n):
                pe.wait_ge(lo_done, b + 1)
                pe.wait_ge(staged, b + 1)
                for k in range(KC):
                    pe.wait_ge(x_lo, k + 1)
                    for m, (w, a) in enumerate(split_pass_list(w_hi, w_lo, xt_hi, xt_lo)):
                        for t in range(NT):
                            ins = nc.tensor.matmul(ps[j][:, t * 512:(t + 1) * 512], w[:, j, k, :], a[:, k, t * 512:(t + 1) * 512],
                                                   start=(k == 0 and m == 0), stop=(k == KC - 1 and m == 2))
                ins.then_inc(product, 1)

            for n in range(len(weights)):
                with pe.Fori(0, blocks[n] // 2) as i:
                    for j in range(2):
                        body(i * 2 + (base[n] + j), j, n)
            pe.wait_ge(mod_ready, 2)
            pe.wait_ge(mod_added, total)
            for h in range(2):
                pe.wait_ge(staged, total + 1 + h)
                for g in range(0, MOD, 512):
                    ins = nc.tensor.matmul(ps[h][0:1, g:g + 512], ones[:], mod[:, h, g:g + 512], start=True, stop=True)
                ins.then_inc(mod_summed, 1)


HD = 64
HEADS = 8
CHUNK = 512


def chunks_of(qb):
    n = P * (qb + 1)
    return [(at, min(CHUNK, n - at)) for at in range(0, n, CHUNK)][::-1]


def phase_stick(nc, sem, kvqg_t, o_t, ident):
    ATT = HEADS * HD
    SCALE = HD ** -0.5
    FAR = -float(2 ** 100)
    units = [(qb, s, at, n) for qb in range(TILES) for s in range(2) for at, n in chunks_of(qb)]
    U = len(units)
    DEEP = 4
    assert U % DEEP == 0
    O = TILES * 2
    last_of = [u for u in range(U) if u + 1 == U or units[u][:2] != units[u + 1][:2]]
    with ExitStack() as ctx:
        al = Alloc(nc, ctx)
        k_raw = al.sb("st_k_raw", [P, 2, SEQ])
        q_raw = al.sb("st_q_raw", [P, 2, SEQ])
        v_raw = al.sb("st_v_raw", [P, SEQ])
        k_hi = al.sb("st_k_hi", [P, 2, SEQ], F32R)
        k_lo = al.sb("st_k_lo", [P, 2, SEQ], F32R)
        q_two = al.sb("st_q_two", [P, 2, SEQ], F32R)
        v_nat = al.sb("st_v_nat", [P, TILES, P])
        soft = al.sb("st_soft", [P, DEEP, CHUNK])
        csum = al.sb("st_csum", [P, DEEP, CHUNK])
        arg = al.sb("st_arg", [P, DEEP, CHUNK])
        prob = al.sb("st_prob", [P, DEEP, CHUNK])
        o_sb = al.sb("st_o", [HD, 2, SEQ])
        ident_r = al.sb("st_ident_r", [P, P], F32R)
        far = al.sb("st_far", [P, P])
        far_r = al.sb("st_far_r", [P, P], F32R)
        z = [al.ps(f"st_z{j}", [P, CHUNK]) for j in range(DEEP)]
        turn = [al.ps(f"st_turn{j}", [P, CHUNK]) for j in range(2)]
        o_ps = [al.ps(f"st_o{j}", [HD, P]) for j in range(2)]
        k_in, q_in, v_in = sem("st_k_in"), sem("st_q_in"), sem("st_v_in")
        far_ready, const_ready = sem("st_far_ready"), sem("st_const_ready")
        kh_done, kl_done, qh_done, ql_done = sem("st_kh"), sem("st_kl"), sem("st_qh"), sem("st_ql")
        v_turned, v_ready = sem("st_v_turned"), sem("st_v_ready")
        z_ready, sized, exped, logged = sem("st_z_ready"), sem("st_sized"), sem("st_exped"), sem("st_logged")
        softened, summed, arg_ready = sem("st_softened"), sem("st_summed"), sem("st_arg_ready")
        turned, p_ready, weighed = sem("st_turned"), sem("st_p_ready"), sem("st_weighed")
        o_left, o_out = sem("st_o_left"), sem("st_o_out")
        rows = kvqg_t.rearrange("(w b p) t -> w b p t", w=4, p=P)
        o_v = o_t.rearrange("(b s p) t -> b s p t", s=2, p=HD)
        PAIRS = HEADS // 2
        block = ctx.enter_context(nc.Block())

        @block.sync
        def _(sp):
            def load(pair, row):
                sp.wait_ge(kl_done, pair * 2 + 2)
                sp.wait_ge(ql_done, pair * 2 + 2)
                for s in range(2):
                    for half in range(2):
                        for buf, w, done in ((k_raw, 0, k_in), (q_raw, 2, q_in)):
                            sp.dma_start(buf[half * HD:half * HD + HD, s], row(w)[s * HD:s * HD + HD, :]).then_inc(done, 16)
                sp.wait_ge(v_turned, pair * DEEP + DEEP)
                sp.dma_start(v_raw[:], row(1)).then_inc(v_in, 16)

            def store(pair, out):
                sp.wait_ge(o_left, pair * O + (O + 2))
                for s in range(2):
                    sp.dma_start(out(s), o_sb[:, s]).then_inc(o_out, 16)

            load(0, lambda w: rows[w][0])
            with sp.Fori(0, PAIRS - 1) as i:
                load(i + 1, lambda w: rows[w][bass.ds(i + 1, 1)].rearrange("a p t -> (a p) t"))
                store(i, lambda s: o_v[bass.ds(i, 1), s].rearrange("a p t -> (a p) t"))
            store(PAIRS - 1, lambda s: o_v[PAIRS - 1, s])
            sp.wait_ge(o_out, 32 * PAIRS + 32)

        @block.gpsimd
        def _(pool):
            nc.gpsimd.memset(far[:], 0.0).then_inc(far_ready, 1)
            pool.wait_ge(far_ready, 1)
            nc.gpsimd.affine_select(out=far[:], in_=far[:], compare_op=ALU.is_gt, fill=FAR, base=0,
                                    pattern=[[-1, P]], channel_multiplier=1).then_inc(far_ready, 1)

        @block.scalar
        def _(act):
            nc.scalar.preload_act_table_set("natural_log_exp_and_others")
            nc.scalar.activation(ident_r[:], ident[:], ACT.Copy).then_inc(const_ready, 1)
            act.wait_ge(far_ready, 2)
            nc.scalar.activation(far_r[:], far[:], ACT.Copy).then_inc(const_ready, 1)
            with act.Fori(0, PAIRS) as i:
                act.wait_ge(z_ready, i * U + DEEP)
                act.wait_ge(k_in, i * 64 + 64)
                act.wait_ge(q_in, i * 64 + 64)
                for s in range(2):
                    nc.scalar.activation(k_hi[:, s], k_raw[:, s], ACT.Copy).then_inc(kh_done, 1)
                    nc.scalar.activation(q_two[:, s], q_raw[:, s], ACT.Copy, scale=SCALE).then_inc(qh_done, 1)
                act.wait_ge(weighed, i * U + DEEP)
                for j in range(DEEP):
                    act.wait_ge(v_turned, i * DEEP + (j + DEEP + 1))
                    nc.scalar.activation(v_nat[:, j * 4:j * 4 + 4].rearrange("p a b -> p (a b)"), z[j][:], ACT.Copy).then_inc(v_ready, 1)

                def size(u):
                    n = units[u][3]
                    act.wait_ge(z_ready, i * U + (u + DEEP + 1))
                    act.wait_ge(summed, i * U + (u + 1))
                    nc.scalar.activation(soft[:, u % DEEP, 0:n], z[u % DEEP][:, 0:n], ACT.Abs).then_inc(sized, 1)

                def exponential(u):
                    n = units[u][3]
                    act.wait_ge(sized, i * U + (u + 1))
                    nc.scalar.activation(soft[:, u % DEEP, 0:n], soft[:, u % DEEP, 0:n], ACT.Exp, scale=-1.0).then_inc(exped, 1)

                def logarithm(u):
                    n = units[u][3]
                    act.wait_ge(exped, i * U + (u + 1))
                    nc.scalar.activation(soft[:, u % DEEP, 0:n], soft[:, u % DEEP, 0:n], ACT.Ln, bias=1.0).then_inc(logged, 1)

                def weights(u):
                    n = units[u][3]
                    act.wait_ge(turned, i * U + (u + DEEP + 1))
                    act.wait_ge(weighed, i * U + (u + 1))
                    nc.scalar.activation(prob[:, u % DEEP, 0:n], turn[u % 2][:, 0:n], ACT.Exp).then_inc(p_ready, 1)

                for t in range(-2, U + 2):
                    if t + 2 < U:
                        size(t + 2)
                    if 0 <= t + 1 < U:
                        logarithm(t + 1)
                    if t >= 2:
                        weights(t - 2)
                    if t + 2 < U:
                        exponential(t + 2)

        @block.vector
        def _(dve):
            with dve.Fori(0, PAIRS) as i:
                for s in range(2):
                    dve.wait_ge(kh_done, i * 2 + (s + 1))
                    nc.vector.tensor_tensor(k_lo[:, s], k_raw[:, s], k_hi[:, s].bitcast(F32), ALU.subtract).then_inc(kl_done, 1)
                    dve.wait_ge(qh_done, i * 2 + (s + 1))
                    nc.vector.scalar_tensor_tensor(q_two[HD:P, s], q_raw[HD:P, s], SCALE, q_two[HD:P, s].bitcast(F32),
                                                   ALU.mult, ALU.subtract).then_inc(ql_done, 1)

                def soften(u):
                    b, n = u % DEEP, units[u][3]
                    dve.wait_ge(logged, i * U + (u + 1))
                    nc.vector.scalar_tensor_tensor(soft[:, b, 0:n], z[b][:, 0:n], 0.0, soft[:, b, 0:n], ALU.max, ALU.add).then_inc(softened, 1)

                def add_up(u):
                    qb, _, at, n = units[u]
                    b = u % DEEP
                    dve.wait_ge(softened, i * U + (u + 1))
                    dve.wait_ge(arg_ready, i * U + (u + 1))
                    if at + n == P * (qb + 1):
                        carry = 0.0
                    else:
                        dve.wait_ge(summed, i * U + (u + DEEP))
                        carry = csum[:, (u - 1) % DEEP, 0:1]
                    back = soft[:, b, 0:n][:, ::-1]
                    nc.vector.tensor_tensor_scan(csum[:, b, 0:n][:, ::-1], back, back, carry, ALU.add, ALU.bypass).then_inc(summed, 1)

                def exponents(u):
                    b, n = u % DEEP, units[u][3]
                    dve.wait_ge(summed, i * U + (u + DEEP + 1))
                    dve.wait_ge(turned, i * U + (u + 1))
                    nc.vector.tensor_tensor(arg[:, b, 0:n], z[b][:, 0:n], csum[:, b, 0:n], ALU.subtract).then_inc(arg_ready, 1)

                def leave(u):
                    qb, s = units[u][:2]
                    done = last_of.index(u)
                    dve.wait_ge(weighed, i * U + (u + DEEP + 1))
                    nc.vector.tensor_copy(o_sb[:, s, qb * P:qb * P + P], o_ps[done % 2][:]).then_inc(o_left, 1)

                for t in range(U + 4):
                    if t < U:
                        soften(t)
                    if 0 <= t - 1 < U:
                        exponents(t - 1)
                    if t < U:
                        add_up(t)
                    if t == 3:
                        dve.wait_ge(o_out, i * 32 + 32)
                    if t - 4 in last_of:
                        leave(t - 4)

        @block.tensor
        def _(pe):
            for s, n in ((kl_done, 2), (ql_done, 2), (v_turned, DEEP), (z_ready, DEEP), (summed, DEEP), (arg_ready, DEEP), (turned, DEEP),
                         (weighed, DEEP), (p_ready, 2), (o_left, 2), (o_out, 32)):
                pe.sem_inc(s, n)
            pe.wait_ge(const_ready, 2)
            with pe.Fori(0, PAIRS) as i:
                pe.wait_ge(v_in, i * 16 + 16)
                pe.wait_ge(arg_ready, i * U + DEEP)
                for j in range(DEEP):
                    for t in range(4):
                        ins = nc.tensor.transpose(z[j][:, t * P:t * P + P], v_raw[:, (j * 4 + t) * P:(j * 4 + t + 1) * P], ident[:])
                    ins.then_inc(v_turned, 1)
                pe.wait_ge(kl_done, i * 2 + 4)
                pe.wait_ge(ql_done, i * 2 + 4)

                def scores(u):
                    qb, s, at, n = units[u]
                    if u < DEEP:
                        pe.wait_ge(v_ready, i * DEEP + (u + 1))
                    pe.wait_ge(arg_ready, i * U + (u + 1))
                    q = q_two[:, s, qb * P:qb * P + P]
                    nc.tensor.matmul(z[u % DEEP][:, 0:n], q, k_hi[:, s, at:at + n], start=True, stop=False)
                    diagonal = at + n == P * (qb + 1)
                    ins = nc.tensor.matmul(z[u % DEEP][:, 0:n], q, k_lo[:, s, at:at + n], start=False, stop=not diagonal)
                    if diagonal:
                        ins = nc.tensor.matmul(z[u % DEEP][:, n - P:n], ident_r[:], far_r[:], start=False, stop=True)
                    ins.then_inc(z_ready, 1)

                def transpose(u):
                    n = units[u][3]
                    pe.wait_ge(arg_ready, i * U + (u + DEEP + 1))
                    pe.wait_ge(p_ready, i * U + (u + 1))
                    for c in range(0, n, P):
                        ins = nc.tensor.transpose(turn[u % 2][:, c:c + P], arg[:, u % DEEP, c:c + P], ident[:])
                    ins.then_inc(turned, 1)

                def weigh(u):
                    _, s, at, n = units[u]
                    done = sum(x < u for x in last_of)
                    first = u == 0 or u - 1 in last_of
                    pe.wait_ge(p_ready, i * U + (u + 3))
                    if first:
                        pe.wait_ge(o_left, i * O + (done + 1))
                    for c in range(0, n, P):
                        ins = nc.tensor.matmul(o_ps[done % 2][:], v_nat[:, (at + c) // P, s * HD:s * HD + HD], prob[:, u % DEEP, c:c + P],
                                               start=first and c == 0, stop=u in last_of and c + P == n)
                    ins.then_inc(weighed, 1)

                for t in range(-3, U + 3):
                    if 0 <= t - 1 < U:
                        transpose(t - 1)
                    if t + 3 < U:
                        scores(t + 3)
                    if t >= 3:
                        weigh(t - 3)


def phase_out_b(nc, sem, x1, o_t, kvqg_t, w_out_b, norm_f, mod_row, norm_w, ident, xf, xt_hi, xt_lo):
    AC = HEADS * HD // P
    O_DEEP = 4
    with ExitStack() as ctx:
        al = Alloc(nc, ctx)
        w = al.sb("ob_w", [P, AC, DM])
        o_raw = al.sb("ob_o_raw", [P, O_DEEP, AC, P])
        g_raw = al.sb("ob_g_raw", [P, 2, AC, P])
        xin = al.sb("ob_x", [P, 2, DM])
        y = al.sb("ob_y", [P, 2, DM])
        xo = al.sb("ob_xf", [P, 2, DM])
        hn = al.sb("ob_hn", [P, 2, DM])
        norm_b = al.sb("ob_norm", [P, DM])
        shift = al.sb("ob_shift", [P, DM])
        scale_w = al.sb("ob_scale_w", [P, DM])
        norm_w_b = y[:, 0]
        eps = al.sb("ob_eps", [P, 1])
        ss = al.sb("ob_ss", [P, 2, 2])
        root = al.sb("ob_root", [P, 2, 2])
        r1 = al.sb("ob_r1", [P, 2])
        mean = al.sb("ob_mean", [P, 2])
        r2 = al.sb("ob_r2", [P, 2])
        r12 = al.sb("ob_r12", [P, 2])
        acc = [al.ps(f"ob_acc{j}", [P, DM]) for j in range(2)]
        pt = [al.ps(f"ob_pt{j}", [P, KC, P]) for j in range(2)]
        w_in, rows_in, ready, scale_ready = sem("ob_w_in"), sem("ob_rows_in"), sem("ob_ready"), sem("ob_scale_ready")
        o_in = [sem(f"ob_o_in{j}") for j in range(O_DEEP)]
        g_in = [sem(f"ob_g_in{j}") for j in range(2)]
        x_in = [sem(f"ob_x_in{j}") for j in range(2)]
        xf_out = [sem(f"ob_xf_out{j}") for j in range(2)]
        gated, product, added, weighted, squared = sem("ob_gated"), sem("ob_product"), sem("ob_added"), sem("ob_weighted"), sem("ob_squared")
        rooted1, inverted1, averaged, rooted2, inverted2, joined = (sem("ob_rooted1"), sem("ob_inverted1"), sem("ob_averaged"),
                                                                    sem("ob_rooted2"), sem("ob_inverted2"), sem("ob_joined"))
        normed, scaled, shifted, transposed, hi_done, lo_done = (sem("ob_normed"), sem("ob_scaled"), sem("ob_shifted"), sem("ob_transposed"),
                                                                 sem("ob_hi"), sem("ob_lo"))
        o_v = o_t.rearrange("(k p) (t n) -> t p k n", p=P, n=P)
        g_v = kvqg_t[3 * AC * P:, :].rearrange("(k p) (t n) -> t p k n", p=P, n=P)
        x_v = x1.rearrange("(t p) d -> t p d", p=P)
        xf_v = xf.rearrange("(t p) d -> t p d", p=P)
        SLOTS = TILES + 4
        block = ctx.enter_context(nc.Block())

        @block.sync
        def _(sp):
            def load_o(t):
                if t >= O_DEEP:
                    sp.wait_ge(product, t - O_DEEP + 1)
                if t >= 2:
                    sp.wait_ge(gated, t - 1)
                sp.dma_start(o_raw[:, t % O_DEEP], o_v[t]).then_inc(o_in[t % O_DEEP], 16)
                sp.dma_start(g_raw[:, t % 2], g_v[t]).then_inc(g_in[t % 2], 16)

            def load_x(t):
                if t >= 2:
                    sp.wait_ge(squared, 2 * (t - 2) + 1)
                    sp.wait_ge(weighted, t - 1)
                sp.dma_start(xin[:, t % 2], x_v[t]).then_inc(x_in[t % 2], 16)

            load_o(0)
            sp.dma_start(w[:], w_out_b.rearrange("(k p) n -> p k n", p=P)).then_inc(w_in, 16)
            load_x(0)
            sp.dma_start(norm_b[:], norm_f.partition_broadcast(P)).then_inc(rows_in, 16)
            load_o(1)
            load_x(1)
            sp.dma_start(shift[:], mod_row[0:DM].partition_broadcast(P)).then_inc(rows_in, 16)
            sp.dma_start(scale_w[:], mod_row[DM:2 * DM].partition_broadcast(P)).then_inc(rows_in, 16)
            sp.dma_start(norm_w_b, norm_w.partition_broadcast(P)).then_inc(rows_in, 16)
            for t in range(2, SLOTS):
                if t < TILES:
                    load_o(t)
                    load_x(t)
                if 3 <= t < TILES + 3:
                    sp.wait_ge(normed, t - 2)
                    sp.dma_start(xf_v[t - 3], xo[:, (t - 3) % 2]).then_inc(xf_out[(t - 3) % 2], 16)
            for j in range(2):
                sp.wait_ge(xf_out[j], 16 * (TILES // 2))

        @block.gpsimd
        def _(pool):
            nc.gpsimd.memset(eps[:], EPS).then_inc(ready, 1)

        @block.scalar
        def _(act):
            nc.scalar.preload_act_table(ACT.Sqrt)
            act.wait_ge(ready, 1)

            def squares(t):
                j = t % 2
                act.wait_ge(added, t + 1)
                if t >= 2:
                    act.wait_ge(xf_out[j], 16 * (t // 2))
                    act.wait_ge(averaged, t - 1)
                nc.scalar.activation(xo[:, j], xin[:, j], ACT.Square, accum_out=ss[:, j, 0:1]).then_inc(squared, 1)
                act.wait_ge(squared, 2 * t + 1)
                nc.scalar.activation(root[:, j, 0:1], ss[:, j, 0:1], ACT.Sqrt, bias=eps[:], scale=1.0 / DM).then_inc(rooted1, 1)
                act.wait_ge(weighted, t + 1)
                nc.scalar.activation(xo[:, j], y[:, j], ACT.Square, accum_out=ss[:, j, 1:2]).then_inc(squared, 1)

            def second_root(t):
                j = t % 2
                act.wait_ge(averaged, t + 1)
                nc.scalar.activation(root[:, j, 1:2], mean[:, j:j + 1], ACT.Sqrt, bias=eps[:], scale=r1[:, j:j + 1]).then_inc(rooted2, 1)

            def norm(t):
                j = t % 2
                act.wait_ge(inverted1, t + 1)
                act.wait_ge(squared, 2 * t + 2)
                nc.scalar.activation(xo[:, j], y[:, j], ACT.Copy, scale=r1[:, j:j + 1]).then_inc(normed, 1)

            def hi(t):
                act.wait_ge(transposed, t + 1)
                nc.scalar.activation(xt_hi[:, :, t * P:t * P + P], pt[t % 2][:], ACT.Copy).then_inc(hi_done, 1)

            for t in range(SLOTS):
                if 0 <= t - 1 < TILES:
                    squares(t - 1)
                if 0 <= t - 3 < TILES:
                    hi(t - 3)
                if 0 <= t - 1 < TILES:
                    second_root(t - 1)
                if 0 <= t - 2 < TILES:
                    norm(t - 2)

        @block.vector
        def _(dve):
            def gate(t):
                o = o_raw[:, t % O_DEEP]
                dve.wait_ge(o_in[t % O_DEEP], 16 * (t // O_DEEP + 1))
                dve.wait_ge(g_in[t % 2], 16 * (t // 2 + 1))
                nc.vector.tensor_tensor(o, o, g_raw[:, t % 2], ALU.mult).then_inc(gated, 1)

            def add(t):
                j = t % 2
                dve.wait_ge(product, t + 1)
                dve.wait_ge(x_in[j], 16 * (t // 2 + 1))
                nc.vector.tensor_tensor(xin[:, j], acc[j][:], xin[:, j], ALU.add).then_inc(added, 1)

            def weight(t):
                j = t % 2
                dve.wait_ge(added, t + 1)
                if t >= 2:
                    dve.wait_ge(normed, t - 1)
                    dve.wait_ge(scaled, t - 1)
                nc.vector.tensor_tensor(y[:, j], xin[:, j], norm_b[:], ALU.mult).then_inc(weighted, 1)

            def first_inverse(t):
                j = t % 2
                dve.wait_ge(rooted1, t + 1)
                if t >= 2:
                    dve.wait_ge(normed, t - 1)
                    dve.wait_ge(rooted2, t - 1)
                nc.vector.reciprocal(r1[:, j:j + 1], root[:, j, 0:1]).then_inc(inverted1, 1)
                dve.wait_ge(inverted1, t + 1)
                dve.wait_ge(squared, 2 * t + 2)
                nc.vector.tensor_scalar(mean[:, j:j + 1], ss[:, j, 1:2], r1[:, j:j + 1], 1.0 / DM, ALU.mult, ALU.mult).then_inc(averaged, 1)

            def second_inverse(t):
                j = t % 2
                dve.wait_ge(rooted2, t + 1)
                nc.vector.reciprocal(r2[:, j:j + 1], root[:, j, 1:2]).then_inc(inverted2, 1)
                dve.wait_ge(inverted2, t + 1)
                nc.vector.tensor_tensor(r12[:, j:j + 1], r1[:, j:j + 1], r2[:, j:j + 1], ALU.mult).then_inc(joined, 1)

            def modulate(t):
                j = t % 2
                dve.wait_ge(joined, t + 1)
                if t >= 2:
                    dve.wait_ge(transposed, t - 1)
                nc.vector.scalar_tensor_tensor(hn[:, j], y[:, j], r12[:, j:j + 1], scale_w[:], ALU.mult, ALU.mult).then_inc(scaled, 1)
                dve.wait_ge(scaled, t + 1)
                nc.vector.tensor_tensor(hn[:, j], hn[:, j], shift[:], ALU.add).then_inc(shifted, 1)

            def lo(t):
                dve.wait_ge(hi_done, t + 1)
                cols = slice(t * P, t * P + P)
                nc.vector.tensor_tensor(xt_lo[:, :, cols], pt[t % 2][:], xt_hi[:, :, cols].bitcast(F32), ALU.subtract).then_inc(lo_done, 1)

            gate(0)
            gate(1)
            dve.wait_ge(rows_in, 64)
            nc.vector.scalar_tensor_tensor(scale_w[:], scale_w[:], 1.0, norm_w_b, ALU.add, ALU.mult).then_inc(scale_ready, 1)
            dve.wait_ge(scale_ready, 1)
            for t in range(1, SLOTS):
                if t - 1 < TILES:
                    add(t - 1)
                    weight(t - 1)
                if t + 1 < TILES:
                    gate(t + 1)
                if 0 <= t - 2 < TILES:
                    modulate(t - 2)
                if t - 1 < TILES:
                    first_inverse(t - 1)
                if 0 <= t - 3 < TILES:
                    lo(t - 3)
                if t - 1 < TILES:
                    second_inverse(t - 1)

        @block.tensor
        def _(pe):
            def multiply(t):
                pe.wait_ge(gated, t + 1)
                if t >= 2:
                    pe.wait_ge(added, t - 1)
                for half in range(2):
                    cols = slice(half * 512, half * 512 + 512)
                    for k in range(AC):
                        ins = nc.tensor.matmul(acc[t % 2][:, cols], o_raw[:, t % O_DEEP, k, :], w[:, k, cols], start=k == 0, stop=k == AC - 1)
                ins.then_inc(product, 1)

            def transpose(t):
                pe.wait_ge(shifted, t + 1)
                if t >= 2:
                    pe.wait_ge(lo_done, t - 1)
                for k in range(KC):
                    ins = nc.tensor.transpose(pt[t % 2][:, k, :], hn[:, t % 2, k * P:(k + 1) * P], ident[:])
                ins.then_inc(transposed, 1)

            pe.wait_ge(w_in, 16)
            for t in range(SLOTS):
                if t < TILES:
                    multiply(t)
                if 0 <= t - 3 < TILES:
                    transpose(t - 3)


POOL = 512
WINDOWS = (2, 4, 8, 16)
HALO = max(WINDOWS)
IDX_HEADS = 8
TOP = 256
KV_HEADS = 2
ROW_U, ROW_GP, ROW_Q, ROW_K, ROW_V, ROW_GA, ROW_QI, ROW_KI, ROW_WI = (int(r) for r in np.cumsum([0, 512, 512, 512, 128, 128, 512, 512, 64]))
D_PROJ = ROW_WI + IDX_HEADS
ROT_Q, ROT_K, ROT_QI, ROT_KI, ROT_ROWS = 0, 512, 640, 1152, 1216


def phase_project_rotate(nc, sem, w_in, xt_hi, xt_lo, w_pool, pool_scale, q_norm, k_norm, cos_t, sin_t, inv_count, p_t, mix_t, rot_t):
    HALF = SEQ // 2
    WIDTHS = len(WINDOWS)
    TAIL = D_PROJ - ROW_KI
    order = []
    for n in range(4):
        order += [("norm", ROW_Q + P * n, P, n), ("plain", ROW_GP + P * n, P, None)]
    order += [("norm", ROW_K, P, 4), ("plain", ROW_V, P, None)]
    for n in range(4):
        order += [("pool", ROW_U + P * n, P, n), ("turn", ROW_QI + P * n, P, None)]
        order += [("plain", ROW_GA + P * n, P, None)] if n < 3 else []
    order += [("turn", ROW_KI, TAIL, None), ("plain", ROW_GA + 3 * P, P, None)]
    gates = [first + P * n for first in (ROW_GP, ROW_GA) for n in range(4)]
    assert sum(c for _, _, c, _ in order) == D_PROJ
    B = len(order)
    NORMED = 5
    posts = {b: n for n, b in enumerate(b for b in range(B) if order[b][0] != "plain")}
    norms_of = {b: n for n, b in enumerate(b for b in range(B) if order[b][0] == "norm")}
    pools_of = {b: n for n, b in enumerate(b for b in range(B) if order[b][0] == "pool")}
    turned_rows = {b: (HD if order[b][1] == ROW_KI else P) for b in posts if b not in pools_of}
    loads_of, at = {}, 0
    for b in turned_rows:
        at += turned_rows[b] // 32
        loads_of[b] = at

    def outputs(b):
        kind, first, cols, g = order[b]
        if kind == "pool":
            return [(0, P, mix_t[g * P:g * P + P, :])]
        if kind == "plain":
            return [(0, P, p_t[first:first + P, :])]
        to = {True: ROT_Q + first - ROW_Q, first >= ROW_K: ROT_K + first - ROW_K, first >= ROW_QI: ROT_QI + first - ROW_QI}[True]
        rows = turned_rows[b]
        rest = [(rows, cols, p_t[first + rows:first + cols, :])] if rows < cols else []
        return [(0, rows, rot_t[to:to + rows, :])] + rest

    outs_of, stored = {}, [0, 0]
    for b in range(B):
        stored[b % 2] += len(outputs(b))
        outs_of[b] = stored[b % 2]

    with ExitStack() as ctx:
        al = Alloc(nc, ctx)
        raw = al.sb("pr_raw", [P, KC, P])
        w_hi = al.sb("pr_w_hi", [P, 2, KC, P], F32R)
        w_lo = al.sb("pr_w_lo", [P, 2, KC, P], F32R)
        stage = al.sb("pr_stage", [P, 2, SEQ])
        cos = al.sb("pr_cos", [P, SEQ])
        sin = al.sb("pr_sin", [P, SEQ])
        work = al.sb("pr_work", [P, 2, HALO + HALF])
        wide = al.sb("pr_wide", [P, SEQ])
        w_mix = al.sb("pr_w_mix", [P, WIDTHS, P])
        scale = al.sb("pr_scale", [P, WIDTHS])
        inv = al.sb("pr_inv", [P, WIDTHS, HALO])
        norms = al.sb("pr_norms", [P, NORMED])
        norms_s = al.sb("pr_norms_s", [P, NORMED])
        eps = al.sb("pr_eps", [P, 1])
        ones = al.sb("pr_ones", [P, P])
        ps = [al.ps(f"pr_ps{j}", [P, SEQ]) for j in range(2)]
        w_loaded, hi_done, lo_done, product, left = sem("pr_w_loaded"), sem("pr_hi"), sem("pr_lo"), sem("pr_product"), sem("pr_left")
        const_in, ones_ready, done, xs_in = sem("pr_const_in"), sem("pr_ones_ready"), sem("pr_chain"), sem("pr_xs_in")
        squared, summed, rooted = sem("pr_squared"), sem("pr_summed"), sem("pr_rooted")
        posted, mixed, blended = sem("pr_posted"), sem("pr_mixed"), sem("pr_blended")
        out_done = [sem(f"pr_out{j}") for j in range(2)]
        N_CONST = 16 * (5 + 2 * 4 * NORMED)
        block = ctx.enter_context(nc.Block())

        def wide_free(eng, b):
            before = [c for c in range(b) if c in norms_of or c in pools_of]
            if before and before[-1] in norms_of:
                eng.wait_ge(posted, posts[before[-1]] + 1)
            elif before:
                eng.wait_ge(mixed, pools_of[before[-1]] + 1)

        @block.sync
        def _(sp):
            def load(b):
                _, first, cols, _ = order[b]
                if b:
                    sp.wait_ge(lo_done, b)
                sp.dma_start(raw[:, :, 0:cols], w_in[:, first:first + cols].rearrange("(k p) n -> p k n", p=P)).then_inc(w_loaded, 16)

            def load_swapped(b):
                sp.wait_ge(left, b + 1)
                if posts[b]:
                    sp.wait_ge(posted, posts[b])
                for to in range(0, turned_rows[b], 32):
                    sp.dma_start(work[to:to + 32, :, 0:HALF],
                                 stage[to ^ 32:(to ^ 32) + 32, b % 2].rearrange("p (c n) -> p c n", c=2)).then_inc(xs_in, 16)

            load(0)
            load(1)
            sp.dma_start(cos[:], cos_t).then_inc(const_in, 16)
            sp.dma_start(sin[:], sin_t).then_inc(const_in, 16)
            sp.dma_start(inv[:], inv_count.partition_broadcast(P)).then_inc(const_in, 16)
            sp.dma_start(w_mix[:], w_pool.rearrange("g c d -> c g d")).then_inc(const_in, 16)
            with nc.allow_non_contiguous_dma(reason="a few vectors, once"):
                sp.dma_start(scale[:], pool_scale.rearrange("(g p) -> p g", p=P)).then_inc(const_in, 16)
                for n in range(NORMED):
                    w = (q_norm if n < 4 else k_norm).rearrange("(p a) -> p a", a=1)
                    for at in range(0, P, 32):
                        half = at % HD
                        sp.dma_start(norms[at:at + 32, n:n + 1], w[half:half + 32]).then_inc(const_in, 16)
                        sp.dma_start(norms_s[at:at + 32, n:n + 1], w[half ^ 32:(half ^ 32) + 32]).then_inc(const_in, 16)
            for b in range(B):
                if b + 2 < B:
                    load(b + 2)
                if b in turned_rows:
                    load_swapped(b)

        @block.gpsimd
        def _(pool):
            nc.gpsimd.memset(eps[:], EPS).then_inc(ones_ready, 1)
            nc.gpsimd.memset(ones[:], 0.0).then_inc(ones_ready, 1)
            pool.wait_ge(ones_ready, 2)
            for h in range(2):
                nc.gpsimd.memset(ones[h * HD:h * HD + HD, h * HD:h * HD + HD], 1.0).then_inc(ones_ready, 1)
            for b in range(B):
                if b in pools_of:
                    pool.wait_ge(blended, pools_of[b] + 1)
                elif b in posts:
                    pool.wait_ge(posted, posts[b] + 1)
                pool.wait_ge(left, b + 1)
                for at, to, dst in outputs(b):
                    nc.gpsimd.dma_start(dst, stage[at:to, b % 2]).then_inc(out_done[b % 2], 16)
            for j in range(2):
                pool.wait_ge(out_done[j], 16 * stored[j])

        @block.scalar
        def _(act):
            nc.scalar.preload_act_table(ACT.Sqrt)

            def split(b):
                cols = order[b][2]
                act.wait_ge(w_loaded, 16 * (b + 1))
                if b >= 2:
                    act.wait_ge(product, b - 1)
                nc.scalar.activation(w_hi[:, b % 2, :, 0:cols], raw[:, :, 0:cols], ACT.Copy).then_inc(hi_done, 1)

            def leave(b):
                cols = order[b][2]
                act.wait_ge(product, b + 1)
                if b >= 2:
                    act.wait_ge(out_done[b % 2], 16 * outs_of[b - 2])
                gate = order[b][1] in gates
                nc.scalar.activation(stage[0:cols, b % 2], ps[b % 2][0:cols], ACT.Silu if gate else ACT.Copy).then_inc(left, 1)
                if b in norms_of:
                    wide_free(act, b)
                    act.wait_ge(left, b + 1)
                    nc.scalar.activation(wide[:], stage[:, b % 2], ACT.Square).then_inc(squared, 1)

            def behind(b):
                if b in norms_of:
                    act.wait_ge(summed, norms_of[b] + 1)
                    nc.scalar.activation(wide[:], ps[b % 2][:], ACT.Sqrt, bias=eps[:], scale=1.0 / HD).then_inc(rooted, 1)
                if b in pools_of:
                    g = order[b][3]
                    act.wait_ge(mixed, pools_of[b] + 1)
                    nc.scalar.activation(stage[:, b % 2], ps[b % 2][:], ACT.Copy, scale=scale[:, g:g + 1]).then_inc(blended, 1)

            split(0)
            act.wait_ge(ones_ready, 4)
            act.wait_ge(const_in, N_CONST)
            for b in range(B):
                if b:
                    leave(b - 1)
                if b + 1 < B:
                    split(b + 1)
                if b:
                    behind(b - 1)
            leave(B - 1)

        @block.vector
        def _(dve):
            count = [0]

            def then(ins):
                count[0] += 1
                ins.then_inc(done, 1)
                dve.wait_ge(done, count[0])

            def split(b):
                cols = order[b][2]
                dve.wait_ge(hi_done, b + 1)
                nc.vector.tensor_tensor(w_lo[:, b % 2, :, 0:cols], raw[:, :, 0:cols], w_hi[:, b % 2, :, 0:cols].bitcast(F32), ALU.subtract).then_inc(lo_done, 1)

            def rotate(b):
                kind, _, _, norm = order[b]
                rows = turned_rows[b]

                def halves(t):
                    return t.rearrange("p (c n) -> p c n", c=2)

                a, s, r = halves(stage[0:rows, b % 2]), work[0:rows, :, 0:HALF], halves(wide[0:rows])
                c_v, s_v = halves(cos[0:rows]), halves(sin[0:rows])
                dve.wait_ge(left, b + 1)
                dve.wait_ge(xs_in, 16 * loads_of[b])
                if kind == "turn":
                    nc.vector.tensor_tensor(s, s, s_v, ALU.mult).then_inc(done, 1)
                    nc.vector.tensor_tensor(a, a, c_v, ALU.mult).then_inc(done, 1)
                    count[0] += 2
                    dve.wait_ge(done, count[0])
                    nc.vector.tensor_tensor(a, a, s, ALU.add).then_inc(posted, 1)
                    return
                dve.wait_ge(squared, norms_of[b] + 1)
                for c in range(2):
                    nc.vector.scalar_tensor_tensor(s[:, c], s[:, c], norms_s[:, norm:norm + 1], s_v[:, c], ALU.mult, ALU.mult).then_inc(done, 1)
                    nc.vector.scalar_tensor_tensor(a[:, c], a[:, c], norms[:, norm:norm + 1], c_v[:, c], ALU.mult, ALU.mult).then_inc(done, 1)
                dve.wait_ge(rooted, norms_of[b] + 1)
                nc.vector.reciprocal(wide[:], wide[:]).then_inc(done, 1)
                count[0] += 5
                dve.wait_ge(done, count[0])
                then(nc.vector.tensor_tensor(a, a, s, ALU.add))
                nc.vector.tensor_tensor(a, a, r, ALU.mult).then_inc(posted, 1)

            def pool(b):
                g = order[b][3]
                w = WINDOWS[g]
                u = stage[:, b % 2]
                dve.wait_ge(left, b + 1)
                dve.wait_ge(posted, posts[b])
                wide_free(dve, b)
                for c in range(2):
                    at = c * HALF
                    if c == 0:
                        for s in range(2):
                            then(nc.vector.memset(work[:, s, 0:HALO], 0.0))
                        then(nc.vector.tensor_copy(work[:, 0, HALO:HALO + 1], u[:, 0:1]))
                        then(nc.vector.tensor_tensor(work[:, 0, HALO + 1:], u[:, 1:HALF], u[:, 0:HALF - 1], ALU.add))
                    else:
                        then(nc.vector.tensor_tensor(work[:, 0, 1:], u[:, at - HALO + 1:], u[:, at - HALO:-1], ALU.add))
                    now, size = 0, 2
                    while size < w:
                        low = HALO if c == 0 else 2 * size - 1
                        then(nc.vector.tensor_tensor(work[:, 1 - now, low:], work[:, now, low:], work[:, now, low - size:-size], ALU.add))
                        now, size = 1 - now, 2 * size
                    first = 0
                    if c == 0:
                        first = HALO
                        then(nc.vector.tensor_tensor(wide[:, 0:HALO], work[:, now, HALO:2 * HALO], inv[:, g], ALU.mult))
                        then(nc.vector.tensor_tensor(wide[:, 0:HALO], wide[:, 0:HALO], u[:, 0:HALO], ALU.subtract))
                    ins = nc.vector.scalar_tensor_tensor(wide[:, at + first:at + HALF], work[:, now, HALO + first:], 1.0 / w, u[:, at + first:at + HALF],
                                                         ALU.mult, ALU.subtract)
                    if c == 0:
                        then(ins)
                    else:
                        ins.then_inc(posted, 1)

            split(0)
            dve.wait_ge(const_in, N_CONST)
            for b in range(B + 1):
                if b + 1 < B:
                    split(b + 1)
                if b - 1 in pools_of:
                    pool(b - 1)
                elif b - 1 in posts:
                    rotate(b - 1)

        @block.tensor
        def _(pe):
            def sum_squares(b):
                pe.wait_ge(squared, norms_of[b] + 1)
                for t in range(NT):
                    ins = nc.tensor.matmul(ps[b % 2][:, t * 512:t * 512 + 512], ones[:], wide[:, t * 512:t * 512 + 512], start=True, stop=True)
                ins.then_inc(summed, 1)

            def pool_mix(b):
                pe.wait_ge(posted, posts[b] + 1)
                for t in range(NT):
                    ins = nc.tensor.matmul(ps[b % 2][:, t * 512:t * 512 + 512], w_mix[:, order[b][3], :], wide[:, t * 512:t * 512 + 512], start=True, stop=True)
                ins.then_inc(mixed, 1)

            for b in range(B):
                cols = order[b][2]
                pe.wait_ge(lo_done, b + 1)
                if b >= 2:
                    pe.wait_ge(left, b - 1)
                if b - 2 in norms_of:
                    pe.wait_ge(rooted, norms_of[b - 2] + 1)
                if b - 2 in pools_of:
                    pe.wait_ge(blended, pools_of[b - 2] + 1)
                for k in range(KC):
                    if k == 3 and b - 1 in norms_of:
                        if b == 1:
                            pe.wait_ge(ones_ready, 4)
                        sum_squares(b - 1)
                    for m, (w, a) in enumerate(split_pass_list(w_hi, w_lo, xt_hi, xt_lo)):
                        for t in range(NT):
                            ins = nc.tensor.matmul(ps[b % 2][0:cols, t * 512:(t + 1) * 512], w[:, b % 2, k, 0:cols], a[:, k, t * 512:(t + 1) * 512],
                                                   start=(k == 0 and m == 0), stop=(k == KC - 1 and m == 2))
                ins.then_inc(product, 1)
                if b - 1 in pools_of:
                    pool_mix(b - 1)


def phase_select_attend(nc, sem, p_t, rot_t, bit_int, bit_val, half_powers, rank_row, mix_t, ident):
    CHUNK = 1024
    FAR = -1e30
    LOWEST = -3e38
    BITS = 31
    STEPS = 10
    EIGHT = 8
    BEST = 2 * EIGHT
    DEEP = 3
    SEARCH, TIES = 4 * BITS + 4, 8
    blocks = range(TILES)
    selecting = [qb for qb in blocks if P * (qb + 1) > TOP]
    first_selecting = selecting[0]

    def keys(qb):
        return P * (qb + 1)

    def parts(qb):
        return [(at, min(CHUNK, keys(qb) - at)) for at in range(0, keys(qb), CHUNK)]

    def quads(at, n):
        return [(g, min(512, at + n - g)) for g in range(at, at + n, 512)]

    def place_of(qb):
        return qb - first_selecting

    number, products = {}, []

    def multiplied(kind, qb, h):
        for m, (at, n) in enumerate(parts(qb)):
            number[kind, qb, h, m] = len(products)
            products.append((kind, qb, h, m, at, n))

    for qb in blocks:
        for h in range(DEEP - 1):
            multiplied("attend", qb, h)
        for h in range(HEADS):
            if qb + 2 in selecting:
                multiplied("index", qb + 2, h)
            if h + DEEP - 1 < HEADS:
                multiplied("attend", qb, h + DEEP - 1)
    group_at, n_groups = {}, 0
    for qb in blocks:
        for h in range(HEADS):
            group_at[qb, h] = n_groups
            n_groups += len(quads(0, keys(qb)))
    relus, masks = {}, {}
    for kind, qb, h, m, _, _ in products:
        kept_in = relus if kind == "index" else masks
        kept_in[qb, h, m] = len(kept_in)
    with ExitStack() as ctx:
        al = Alloc(nc, ctx)
        ki_hi = al.sb("sa_ki_hi", [P, SEQ], F32R)
        ki_lo = al.sb("sa_ki_lo", [P, SEQ], F32R)
        k_hi = al.sb("sa_k_hi", [P, KV_HEADS, SEQ], F32R)
        k_lo = al.sb("sa_k_lo", [P, KV_HEADS, SEQ], F32R)
        v_one = al.sb("sa_v_one", [P, TILES, KV_HEADS, P])
        w_idx = al.sb("sa_w_idx", [P, TILES, IDX_HEADS])
        qi_raw = al.sb("sa_qi_raw", [P, 2, HEADS, P])
        qi_two = al.sb("sa_qi_two", [P, 2, HEADS, P], F32R)
        q_raw = al.sb("sa_q_raw", [P, 2, HEADS, P])
        q_two = al.sb("sa_q_two", [P, 2, HEADS, P], F32R)
        relu = al.sb("sa_relu", [P, 2, CHUNK])
        score = al.sb("sa_score", [P, 2, SEQ])
        tied = al.sb("sa_tied", [P, SEQ])
        place = al.sb("sa_place", [P, SEQ])
        bias = al.sb("sa_bias", [P, 2, SEQ])
        arg = al.sb("sa_arg", [P, DEEP, SEQ])
        raw, v_raw, wi_raw = arg, place, tied[0:IDX_HEADS]
        prob = al.sb("sa_prob", [P, 2, 512])
        top = al.sb("sa_top", [P, DEEP, 2])
        minus_top = al.sb("sa_minus_top", [P, DEEP])
        o_sb = al.sb("sa_o", [P, 2, HEADS, P])
        inv_sum = al.sb("sa_inv_sum", [HD, HEADS, P])
        bit_i = al.sb("sa_bit_i", [P, BITS], mybir.dt.int32)
        bit_f = al.sb("sa_bit_f", [P, BITS])
        pref = al.sb("sa_pref", [P, 1], mybir.dt.int32)
        flip = al.sb("sa_flip", [P, 1], mybir.dt.int32)
        cand = al.sb("sa_cand", [P, 1], mybir.dt.int32)
        kept = al.sb("sa_kept", [P, 1], mybir.dt.int32)
        thr = al.sb("sa_thr", [P, 1], mybir.dt.int32)
        count = al.sb("sa_count", [P, 8])
        sign_sum = al.sb("sa_sign_sum", [P, 1])
        edge = al.sb("sa_edge", [P, 3])
        halves = al.sb("sa_halves", [P, STEPS])
        width = al.sb("sa_width", [P, STEPS])
        guess = al.sb("sa_guess", [P, 1])
        go_up = al.sb("sa_go_up", [P, 1])
        ranks = al.sb("sa_ranks", [P, BEST + 1])
        short = al.sb("sa_short", [P, 1])
        signs = al.sb("sa_signs", [P, SEQ], mybir.dt.bfloat16)
        is_rank = al.sb("sa_is_rank", [P, BEST + 1])
        best = al.sb("sa_best", [P, BEST + 1])
        cut = al.sb("sa_cut", [P, 1])
        lost = al.sb("sa_lost", [P, 1])
        report = al.sb("sa_report", [P, 2])
        reported = al.sb("sa_reported", [1, 2], mybir.dt.int32)
        pr = [al.ps(f"sa_pr{j}", [P, CHUNK]) for j in range(2)]
        turn = [al.ps(f"sa_turn{j}", [P, 512]) for j in range(2)]
        o_ps = [al.ps(f"sa_o{j}", [P, P]) for j in range(2)]
        report_ps = o_ps[0][0:1, 0:2]
        key_rows = [(ROT_KI, ki_hi[:], ki_lo[:])] + [(ROT_K + HD * g, k_hi[:, g], k_lo[:, g]) for g in range(KV_HEADS)]
        raw_in, vw_in, bits_in = [sem(f"sa_raw_in{n}") for n in range(len(key_rows))], sem("sa_vw_in"), sem("sa_bits_in")
        key_hi, key_lo, ones_set = sem("sa_key_hi"), sem("sa_key_lo"), sem("sa_ones_set")
        v_turned, v_left, wi_turned, wi_left = sem("sa_v_turned"), sem("sa_v_left"), sem("sa_wi_turned"), sem("sa_wi_left")
        qi_in = [sem(f"sa_qi_in{j}") for j in range(2)]
        q_in = [sem(f"sa_q_in{j}") for j in range(2)]
        qi_hi, qi_lo, q_hi, q_lo = sem("sa_qi_hi"), sem("sa_qi_lo"), sem("sa_q_hi"), sem("sa_q_lo")
        product, relu_done, scored, causal = sem("sa_product"), sem("sa_relu_done"), sem("sa_scored"), sem("sa_causal")
        guessed, signed = sem("sa_guessed"), sem("sa_signed")
        ranged, step, selected, searched, repaired = sem("sa_ranged"), sem("sa_step"), sem("sa_selected"), sem("sa_searched"), sem("sa_repaired")
        report_summed, report_read, masked, negated, raised = sem("sa_report_summed"), sem("sa_report_read"), sem("sa_masked"), sem("sa_negated"), sem("sa_raised")
        turned, p_ready, weighed, o_ready, o_out = sem("sa_turned"), sem("sa_p_ready"), sem("sa_weighed"), sem("sa_o_ready"), [sem(f"sa_o_out{j}") for j in range(2)]
        logged, inverted, divided = sem("sa_logged"), sem("sa_inverted"), sem("sa_divided")
        qi_v = rot_t[ROT_QI:ROT_QI + 512, :].rearrange("(h d) (t n) -> t d h n", d=HD, n=P)
        q_v = rot_t[ROT_Q:ROT_Q + 512, :].rearrange("(h d) (t n) -> t d h n", d=HD, n=P)
        o_v = mix_t[POOL:, :].rearrange("(h d) (t n) -> t d h n", d=HD, n=P)
        block = ctx.enter_context(nc.Block())

        def left(eng, n):
            kind, qb, h, m, _, _ = products[n]
            if kind == "index":
                eng.wait_ge(relu_done, relus[qb, h, m] + 1)
            else:
                eng.wait_ge(masked, masks[qb, h, m] + 1)

        @block.sync
        def _(sp):
            def load_q(qb):
                if qb >= 2:
                    sp.wait_ge(q_lo, qb - 1)
                for half in range(2):
                    sp.dma_start(q_raw[half * HD:half * HD + HD, qb % 2], q_v[qb]).then_inc(q_in[qb % 2], 16)

            def load_qi(qb):
                if place_of(qb) >= 2:
                    sp.wait_ge(qi_lo, place_of(qb) - 1)
                for half in range(2):
                    sp.dma_start(qi_raw[half * HD:half * HD + HD, qb % 2], qi_v[qb]).then_inc(qi_in[qb % 2], 16)

            load_q(0)
            for n in (1, 0, 2):
                row = key_rows[n][0]
                for half in range(2):
                    sp.dma_start(raw[half * HD:half * HD + HD, n], rot_t[row:row + HD, :]).then_inc(raw_in[n], 16)
                if n == 1:
                    sp.dma_start(wi_raw, p_t[ROW_WI:ROW_WI + IDX_HEADS, :]).then_inc(vw_in, 16)
                    sp.dma_start(v_raw[:], p_t[ROW_V:ROW_V + P, :]).then_inc(vw_in, 16)
                    load_qi(first_selecting)
            for to, rows in ((bit_i, bit_int), (bit_f, bit_val), (halves, half_powers), (ranks, rank_row)):
                sp.dma_start(to[:], rows.partition_broadcast(P)).then_inc(bits_in, 16)
            load_q(1)
            load_qi(first_selecting + 1)
            for qb in blocks:
                if qb + 2 < TILES:
                    load_q(qb + 2)
                if first_selecting + qb + 2 < TILES:
                    load_qi(first_selecting + qb + 2)
                sp.wait_ge(divided, qb + 1)
                sp.dma_start(o_v[qb], o_sb[0:HD, qb % 2]).then_inc(o_out[qb % 2], 16)
            for j in range(2):
                sp.wait_ge(o_out[j], 16 * (TILES // 2))

        @block.gpsimd
        def _(pool):
            nc.gpsimd.memset(v_one[:, :, :, HD:], 1.0).then_inc(ones_set, 1)

            def divide(qb):
                pool.wait_ge(inverted, qb + 1)
                o = o_sb[0:HD, qb % 2]
                nc.gpsimd.tensor_tensor(o, o, inv_sum[:], ALU.mult).then_inc(divided, 1)

            for qb in blocks:
                if qb in selecting:
                    pool.wait_ge(ranged, 2 * (place_of(qb) + 1))
                    own = score[:, qb % 2, qb * P:qb * P + P]
                    nc.gpsimd.affine_select(out=own, in_=own, compare_op=ALU.is_ge, fill=LOWEST, base=0,
                                            pattern=[[-1, P]], channel_multiplier=1).then_inc(causal, 1)
                else:
                    assert qb < 2
                    nc.gpsimd.memset(bias[:, qb, 0:keys(qb)], 0.0).then_inc(ones_set, 1)
                    pool.wait_ge(ones_set, qb + 2)
                    own = bias[:, qb, qb * P:qb * P + P]
                    nc.gpsimd.affine_select(out=own, in_=own, compare_op=ALU.is_ge, fill=FAR, base=0,
                                            pattern=[[-1, P]], channel_multiplier=1).then_inc(causal, 1)
                if qb:
                    divide(qb - 1)
            divide(TILES - 1)

        @block.scalar
        def _(act):
            nc.scalar.preload_act_table_set("natural_log_exp_and_others")

            def split_q(qb):
                j, i = qb % 2, place_of(qb)
                act.wait_ge(qi_in[j], 32 * (i // 2 + 1))
                if i >= 2:
                    act.wait_ge(product, number["index", qb - 2, HEADS - 1, len(parts(qb - 2)) - 1] + 1)
                nc.scalar.activation(qi_two[:, j], qi_raw[:, j], ACT.Copy).then_inc(qi_hi, 1)

            def split_q_attend(qb):
                j = qb % 2
                act.wait_ge(q_in[j], 32 * (qb // 2 + 1))
                if qb >= 2:
                    act.wait_ge(product, number["attend", qb - 2, HEADS - 1, len(parts(qb - 2)) - 1] + 1)
                nc.scalar.activation(q_two[:, j], q_raw[:, j], ACT.Copy, scale=HD ** -0.5).then_inc(q_hi, 1)

            split_q_attend(0)
            for n in (1, 0, 2):
                act.wait_ge(raw_in[n], 32)
                nc.scalar.activation(key_rows[n][1], raw[:, n], ACT.Copy).then_inc(key_hi, 1)
            split_q(first_selecting)
            act.wait_ge(wi_turned, 1)
            nc.scalar.activation(w_idx[:], turn[0][:, 0:TILES * IDX_HEADS].rearrange("p (t h) -> p t h", h=IDX_HEADS), ACT.Copy,
                                 scale=HD ** -0.5 * IDX_HEADS ** -0.5).then_inc(wi_left, 1)
            for g in range(TILES // 4):
                act.wait_ge(v_turned, g + 1)
                for kv in range(KV_HEADS):
                    ins = nc.scalar.activation(v_one[:, g * 4:g * 4 + 4, kv, 0:HD],
                                               turn[(g + 1) % 2][:].rearrange("p (t k d) -> p t k d", k=KV_HEADS, d=HD)[:, :, kv], ACT.Copy)
                ins.then_inc(v_left, 1)

            def raise_e(qb, h):
                t = qb * HEADS + h
                act.wait_ge(negated, t + 1)
                row = arg[:, t % DEEP, 0:keys(qb)]
                nc.scalar.activation(row, row, ACT.Exp, bias=minus_top[:, t % DEEP:t % DEEP + 1]).then_inc(raised, 1)

            def count_signs(qb, i):
                done = STEPS // 2 * place_of(qb) + i + 1
                act.wait_ge(guessed, done)
                n = keys(qb)
                nc.scalar.activation(signs[:, 0:n], score[:, qb % 2, 0:n], ACT.Sign, scale=-1.0, bias=guess[:], accum_out=sign_sum[:]).then_inc(signed, 1)

            def relu_part(qb, h, m):
                n = parts(qb)[m][1]
                p, r = number["index", qb, h, m], relus[qb, h, m]
                act.wait_ge(product, p + 1)
                if r >= 2:
                    act.wait_ge(scored, r - 1)
                nc.scalar.activation(relu[:, r % 2, 0:n], pr[p % 2][:, 0:n], ACT.Relu).then_inc(relu_done, 1)

            for qb in blocks:
                if qb + 1 < TILES:
                    split_q_attend(qb + 1)
                if qb + 3 in selecting:
                    split_q(qb + 3)

                def leave(h):
                    act.wait_ge(weighed, group_at[qb, h] + len(quads(0, keys(qb))))
                    if h == 0 and qb >= 2:
                        act.wait_ge(o_out[qb % 2], 16 * (qb // 2))
                    nc.scalar.activation(o_sb[:, qb % 2, h, :], o_ps[h % 2][:], ACT.Copy).then_inc(o_ready, 1)

                raise_e(qb, 0)
                for h in range(HEADS):
                    if qb + 1 in selecting and 1 <= h <= STEPS // 2:
                        count_signs(qb + 1, h - 1)
                    groups = quads(0, keys(qb))
                    index = len(parts(qb + 2)) if qb + 2 in selecting else 0
                    for m in range(max(len(groups), index)):
                        if m < len(groups):
                            g, w = group_at[qb, h] + m, groups[m][1]
                            act.wait_ge(turned, g + 1)
                            if g >= 2:
                                act.wait_ge(weighed, g - 1)
                            nc.scalar.activation(prob[:, g % 2, 0:w], turn[g % 2][:, 0:w], ACT.Copy).then_inc(p_ready, 1)
                        if m < index:
                            relu_part(qb + 2, h, m)
                        if m == 0 and h:
                            leave(h - 1)
                    if h + 1 < HEADS:
                        raise_e(qb, h + 1)
                leave(HEADS - 1)
                o_sum = o_sb[HD:P, qb % 2]
                act.wait_ge(o_ready, HEADS * (qb + 1))
                nc.scalar.activation(o_sum, o_sum, ACT.Ln).then_inc(logged, 1)
                act.wait_ge(logged, qb + 1)
                if qb:
                    act.wait_ge(divided, qb)
                nc.scalar.activation(inv_sum[:], o_sum, ACT.Exp, scale=-1.0).then_inc(inverted, 1)

        @block.vector
        def _(dve):
            steps = [0]

            def mark(ins):
                steps[0] += 1
                ins.then_inc(step, 1)

            def last_step():
                dve.wait_ge(step, steps[0])

            def split_q(qb):
                j = qb % 2
                dve.wait_ge(qi_hi, place_of(qb) + 1)
                nc.vector.tensor_tensor(qi_two[HD:P, j], qi_raw[HD:P, j], qi_two[HD:P, j].bitcast(F32), ALU.subtract).then_inc(qi_lo, 1)

            def split_q_attend(qb):
                j = qb % 2
                dve.wait_ge(q_hi, qb + 1)
                flat = lambda t: t[HD:P, j].rearrange("p h n -> p (h n)")
                nc.vector.scalar_tensor_tensor(flat(q_two), flat(q_raw), HD ** -0.5, flat(q_two).bitcast(F32),
                                               ALU.mult, ALU.subtract).then_inc(q_lo, 1)

            def add_scores(qb, h):
                for m, (at, n) in enumerate(parts(qb)):
                    r = relus[qb, h, m]
                    dve.wait_ge(relu_done, r + 1)
                    w, s = w_idx[:, qb, h:h + 1], score[:, qb % 2, at:at + n]
                    if h == 0:
                        ins = nc.vector.tensor_scalar(s, relu[:, r % 2, 0:n], w, None, ALU.mult)
                    else:
                        dve.wait_ge(scored, r + 1 - len(parts(qb)))
                        ins = nc.vector.scalar_tensor_tensor(s, relu[:, r % 2, 0:n], w, s, ALU.mult, ALU.add)
                    ins.then_inc(scored, 1)

            def take_range(qb):
                s = score[:, qb % 2, 0:keys(qb)]
                dve.wait_ge(scored, relus[qb, HEADS - 1, len(parts(qb)) - 1] + 1)
                last_step()
                nc.vector.tensor_reduce(edge[:, 0:1], s, mybir.AxisListType.X, ALU.min).then_inc(ranged, 1)
                nc.vector.tensor_reduce(edge[:, 1:2], s, mybir.AxisListType.X, ALU.max).then_inc(ranged, 1)
                dve.wait_ge(ranged, 2 * (place_of(qb) + 1))
                mark(nc.vector.tensor_tensor(edge[:, 2:3], edge[:, 1:2], edge[:, 0:1], ALU.subtract))
                last_step()
                mark(nc.vector.tensor_scalar(width[:], halves[:], edge[:, 2:3], None, ALU.mult))
                mark(nc.vector.scalar_tensor_tensor(guess[:], edge[:, 2:3], 0.5, edge[:, 0:1], ALU.mult, ALU.add))

            def count_at_guess(qb):
                n = keys(qb)
                dve.wait_ge(causal, qb + 1)
                last_step()
                mark(nc.vector.tensor_scalar(tied[:, 0:n], score[:, qb % 2, 0:n], guess[:, 0:1], None, ALU.is_ge, ALU.add, accum_out=count[:, 0:1]))

            def decide(qb, k):
                if k % 2:
                    dve.wait_ge(signed, STEPS // 2 * place_of(qb) + k // 2 + 1)
                    mark(nc.vector.tensor_scalar(go_up[:], sign_sum[:], float(keys(qb) - 2 * TOP), width[:, k:k + 1], ALU.is_le, ALU.mult))
                else:
                    last_step()
                    mark(nc.vector.tensor_scalar(go_up[:], count[:, 0:1], float(TOP), width[:, k:k + 1], ALU.is_ge, ALU.mult))

            def move(k):
                last_step()
                if k + 1 < STEPS:
                    ins = nc.vector.scalar_tensor_tensor(guess[:], go_up[:], width[:, k + 1:k + 2], guess[:], ALU.subtract, ALU.add)
                    if k % 2:
                        mark(ins)
                    else:
                        ins.then_inc(guessed, 1)
                else:
                    mark(nc.vector.tensor_tensor(best[:, 0:1], go_up[:], guess[:], ALU.add))

            def count_above(qb):
                n = keys(qb)
                last_step()
                mark(nc.vector.tensor_scalar(tied[:, 0:n], score[:, qb % 2, 0:n], best[:, 0:1], None, ALU.is_ge, ALU.add, accum_out=count[:, 1:2]))

            def drop_above(qb):
                n = keys(qb)
                last_step()
                mark(nc.vector.scalar_tensor_tensor(place[:, 0:n], tied[:, 0:n], LOWEST, score[:, qb % 2, 0:n], ALU.mult, ALU.add))

            def find_short():
                mark(nc.vector.tensor_scalar(short[:], count[:, 1:2], -1.0, float(TOP), ALU.mult, ALU.add))

            def best_below(qb):
                last_step()
                below = place[:, 0:keys(qb)]
                mark(nc.vector.max(best[:, 1:1 + EIGHT], below))
                last_step()
                mark(nc.vector.match_replace(out=below, in_to_replace=best[:, 1:1 + EIGHT], in_values=below, imm_value=LOWEST))
                last_step()
                mark(nc.vector.max(best[:, 1 + EIGHT:], below))
                mark(nc.vector.tensor_scalar(is_rank[:], ranks[:], short[:, 0:1], None, ALU.is_equal))

            def pick():
                last_step()
                mark(nc.vector.tensor_tensor(is_rank[:], is_rank[:], best[:], ALU.mult))

            def find_cut():
                last_step()
                mark(nc.vector.tensor_reduce(cut[:], is_rank[:], mybir.AxisListType.X, ALU.add))

            def count_selected(qb):
                n = keys(qb)
                last_step()
                mark(nc.vector.tensor_scalar(tied[:, 0:n], score[:, qb % 2, 0:n], cut[:, 0:1], None, ALU.is_ge, ALU.add, accum_out=count[:, 2:3]))

            def set_bias(qb):
                n = keys(qb)
                if qb >= 2:
                    dve.wait_ge(masked, masks[qb - 2, HEADS - 1, len(parts(qb - 2)) - 1] + 1)
                mark(nc.vector.scalar_tensor_tensor(lost[:], short[:], float(BEST), short[:], ALU.subtract, ALU.mult))
                mark(nc.vector.tensor_scalar(bias[:, qb % 2, 0:n], score[:, qb % 2, 0:n], cut[:, 0:1], FAR, ALU.is_lt, ALU.mult))
                last_step()
                nc.vector.tensor_scalar(report[:, 0:1], count[:, 2:3], float(TOP), None, ALU.not_equal).then_inc(selected, 1)
                nc.vector.tensor_scalar(report[:, 1:2], lost[:], 0.0, None, ALU.is_gt).then_inc(selected, 1)

            def search(qb):
                n = keys(qb)
                s, ge = score[:, qb % 2, 0:n], tied[:, 0:n]
                done = [SEARCH * place_of(qb)]

                def then(ins):
                    done[0] += 1
                    ins.then_inc(searched, 1)
                    dve.wait_ge(searched, done[0])

                then(nc.vector.tensor_scalar(ge, s, 0.0, None, ALU.is_ge, ALU.add, accum_out=count[:, 3:4]))
                then(nc.vector.tensor_scalar(flip[:], count[:, 3:4], float(TOP), -1.0, ALU.is_ge, ALU.add))
                then(nc.vector.memset(pref[:], 0))
                before = done[0]
                with dve.Fori(0, BITS) as i:
                    nc.vector.tensor_scalar(cand[:], pref[:], bit_i[:, bass.ds(i, 1)], flip[:, 0:1], ALU.bitwise_or, ALU.bitwise_xor).then_inc(searched, 1)
                    dve.wait_ge(searched, i * 4 + (before + 1))
                    nc.vector.tensor_scalar(ge, s, cand[:].bitcast(F32), None, ALU.is_ge, ALU.add, accum_out=count[:, 3:4]).then_inc(searched, 1)
                    dve.wait_ge(searched, i * 4 + (before + 2))
                    nc.vector.tensor_scalar(kept[:], count[:, 3:4], float(TOP), bit_f[:, bass.ds(i, 1)], ALU.is_ge, ALU.mult).then_inc(searched, 1)
                    dve.wait_ge(searched, i * 4 + (before + 3))
                    nc.vector.tensor_tensor(pref[:], pref[:], kept[:], ALU.bitwise_or).then_inc(searched, 1)
                    dve.wait_ge(searched, i * 4 + (before + 4))
                done[0] = before + 4 * BITS
                then(nc.vector.tensor_tensor(thr[:], pref[:], flip[:], ALU.bitwise_xor))
                assert done[0] == SEARCH * (place_of(qb) + 1)

            def break_ties(qb):
                n = keys(qb)
                s, eq, pl, b, t = score[:, qb % 2, 0:n], tied[:, 0:n], place[:, 0:n], bias[:, qb % 2, 0:n], thr[:].bitcast(F32)
                done = [TIES * place_of(qb) + 1]

                def then(ins):
                    done[0] += 1
                    ins.then_inc(repaired, 1)
                    dve.wait_ge(repaired, done[0])

                then(nc.vector.tensor_scalar(eq, s, t, None, ALU.is_gt, ALU.add, accum_out=count[:, 4:5]))
                then(nc.vector.tensor_scalar(count[:, 5:6], count[:, 4:5], -1.0, float(TOP), ALU.mult, ALU.add))
                then(nc.vector.tensor_scalar(eq, s, t, None, ALU.is_equal))
                then(nc.vector.tensor_tensor_scan(pl, eq, eq, 0.0, ALU.add, ALU.bypass))
                then(nc.vector.scalar_tensor_tensor(pl, pl, count[:, 5:6], eq, ALU.is_le, ALU.mult))
                then(nc.vector.scalar_tensor_tensor(pl, s, t, pl, ALU.is_gt, ALU.add))
                then(nc.vector.tensor_scalar(b, pl, -1.0, -FAR, ALU.add, ALU.mult))
                assert done[0] == TIES * (place_of(qb) + 1)

            def check_selection(qb):
                i = place_of(qb)
                dve.wait_ge(report_summed, i + 1)
                nc.vector.tensor_copy(reported[:], report_ps).then_inc(report_read, 1)
                dve.wait_ge(report_read, i + 1)
                unequal = dve.value_load(reported[0:1, 0:1], min_val=0, max_val=P)
                with dve.If(unequal != 0):
                    nc.vector.tensor_copy(thr[:].bitcast(F32), cut[:]).then_inc(repaired, 1)
                    dve.wait_ge(repaired, TIES * i + 1)
                    unfound = dve.value_load(reported[0:1, 1:2], min_val=0, max_val=P)
                    with dve.If(unfound != 0):
                        search(qb)
                    with dve.If(unfound == 0):
                        dve.sem_inc(searched, SEARCH)
                    dve.wait_ge(searched, SEARCH * (i + 1))
                    break_ties(qb)
                with dve.If(unequal == 0):
                    dve.sem_inc(searched, SEARCH)
                    dve.sem_inc(repaired, TIES)
                dve.wait_ge(repaired, TIES * (i + 1))

            def attend(qb, nxt, later):
                n, each = keys(qb), len(parts(qb))
                heads = qb * HEADS
                if qb not in selecting:
                    dve.wait_ge(causal, qb + 1)

                def mask(h, m):
                    j, (at, w) = (heads + h) % DEEP, parts(qb)[m]
                    if m == 0 and heads + h >= DEEP:
                        dve.wait_ge(turned, group_at[divmod(heads + h - DEEP + 1, HEADS)])
                    p = number["attend", qb, h, m]
                    dve.wait_ge(product, p + 1)
                    before = FAR
                    if m:
                        dve.wait_ge(masked, masks[qb, h, m - 1] + 1)
                        before = top[:, j, m - 1:m]
                    nc.vector.tensor_tensor_reduce(out=arg[:, j, at:at + w], in0=pr[p % 2][:, 0:w], in1=bias[:, qb % 2, at:at + w], scale=1.0,
                                                   scalar=before, op0=ALU.add, op1=ALU.max, accum_out=top[:, j, m:m + 1]).then_inc(masked, 1)

                def negate(h):
                    dve.wait_ge(masked, masks[qb, h, each - 1] + 1)
                    j = (heads + h) % DEEP
                    nc.vector.tensor_scalar(minus_top[:, j:j + 1], top[:, j, each - 1:each], -1.0, None, ALU.mult).then_inc(negated, 1)

                def mask_head(h):
                    for m in range(each):
                        mask(h, m)
                    negate(h)

                mask_head(0)
                for h in range(HEADS):
                    if h + 1 < HEADS:
                        mask_head(h + 1)
                    if nxt:
                        if 1 <= h <= STEPS // 2:
                            decide(nxt, 2 * h - 1)
                            move(2 * h - 1)
                        if h < STEPS // 2:
                            count_at_guess(nxt)
                            decide(nxt, 2 * h)
                            move(2 * h)
                    if later:
                        add_scores(later, h)
                    if nxt:
                        if h == HEADS - 3:
                            count_above(nxt)
                            drop_above(nxt)
                            find_short()
                            best_below(nxt)
                        if h == HEADS - 2:
                            pick()
                            find_cut()
                            count_selected(nxt)
                            set_bias(nxt)
            assert STEPS // 2 <= HEADS - 3 and STEPS % 2 == 0
            split_q_attend(0)
            for done, n in enumerate((1, 0, 2)):
                dve.wait_ge(key_hi, done + 1)
                nc.vector.tensor_tensor(key_rows[n][2], raw[:, n], key_rows[n][1].bitcast(F32), ALU.subtract).then_inc(key_lo, 1)
            split_q(first_selecting)
            dve.wait_ge(bits_in, 64)
            dve.wait_ge(wi_left, 1)
            dve.wait_ge(v_left, TILES // 4)
            for qb in blocks:
                if qb + 1 < TILES:
                    split_q_attend(qb + 1)
                if qb + 3 in selecting:
                    split_q(qb + 3)
                if qb in selecting:
                    check_selection(qb)
                attend(qb, qb + 1 if qb + 1 in selecting else None, qb + 2 if qb + 2 in selecting else None)
                if qb + 2 in selecting:
                    take_range(qb + 2)

        @block.tensor
        def _(pe):
            pe.wait_ge(vw_in, 32)
            for t in range(TILES):
                ins = nc.tensor.transpose(turn[0][:, t * IDX_HEADS:(t + 1) * IDX_HEADS], wi_raw[:, t * P:t * P + P], ident[0:IDX_HEADS, 0:IDX_HEADS])
            ins.then_inc(wi_turned, 1)
            for g in range(TILES // 4):
                if g == 1:
                    pe.wait_ge(wi_left, 1)
                if g >= 2:
                    pe.wait_ge(v_left, g - 1)
                for t in range(4):
                    ins = nc.tensor.transpose(turn[(g + 1) % 2][:, t * P:t * P + P], v_raw[:, (g * 4 + t) * P:(g * 4 + t + 1) * P], ident[:])
                ins.then_inc(v_turned, 1)
            pe.wait_ge(key_lo, len(key_rows))
            pe.wait_ge(v_left, TILES // 4)
            pe.wait_ge(ones_set, 1)

            def scores(n):
                kind, qb, h, m, at, width = products[n]
                if h == 0 and m == 0:
                    pe.wait_ge(*((qi_lo, place_of(qb) + 1) if kind == "index" else (q_lo, qb + 1)))
                if n >= 2:
                    left(pe, n - 2)
                q = (qi_two if kind == "index" else q_two)[:, qb % 2, h, :]
                kv = h // (HEADS // KV_HEADS)
                for g, w in quads(at, width):
                    hi, lo = (ki_hi[:, g:g + w], ki_lo[:, g:g + w]) if kind == "index" else (k_hi[:, kv, g:g + w], k_lo[:, kv, g:g + w])
                    nc.tensor.matmul(pr[n % 2][:, g - at:g - at + w], q, hi, start=True, stop=False)
                    ins = nc.tensor.matmul(pr[n % 2][:, g - at:g - at + w], q, lo, start=False, stop=True)
                ins.then_inc(product, 1)

            def weigh(qb, h, m):
                n = keys(qb)
                t = qb * HEADS + h
                at, w = quads(0, n)[m]
                g = group_at[qb, h] + m
                if m == 0 and t >= 2:
                    pe.wait_ge(o_ready, t - 1)
                if m == 0 and h == 0 and qb in selecting:
                    pe.wait_ge(report_read, place_of(qb) + 1)
                pe.wait_ge(p_ready, g + 1)
                for c in range(0, w, P):
                    ins = nc.tensor.matmul(o_ps[t % 2][:], v_one[:, (at + c) // P, h // (HEADS // KV_HEADS), :], prob[:, g % 2, c:c + P],
                                           start=at + c == 0, stop=at + c + P == n)
                ins.then_inc(weighed, 1)

            def turn_one(qb, h, m):
                at, w = quads(0, keys(qb))[m]
                g = group_at[qb, h] + m
                if m == 0:
                    pe.wait_ge(raised, qb * HEADS + h + 1)
                if g >= 2:
                    pe.wait_ge(p_ready, g - 1)
                for c in range(0, w, P):
                    ins = nc.tensor.transpose(turn[g % 2][:, c:c + P], arg[:, (qb * HEADS + h) % DEEP, at + c:at + c + P], ident[:])
                ins.then_inc(turned, 1)

            def scores_of(kind, qb, h):
                for m in range(len(parts(qb))):
                    scores(number[kind, qb, h, m])

            for qb in blocks:
                for h in range(DEEP - 1):
                    scores_of("attend", qb, h)
                groups = quads(0, keys(qb))
                index = len(parts(qb + 2)) if qb + 2 in selecting else 0
                for h in range(HEADS):
                    for m in range(max(len(groups), index)):
                        if m < len(groups):
                            turn_one(qb, h, m)
                        if m < index:
                            scores(number["index", qb + 2, h, m])
                        if 0 < m < len(groups):
                            weigh(qb, h, m - 1)
                    if h + DEEP - 1 < HEADS:
                        scores_of("attend", qb, h + DEEP - 1)
                    if h == HEADS - 1 and qb + 1 in selecting:
                        pe.wait_ge(selected, 2 * (place_of(qb + 1) + 1))
                        pe.wait_ge(o_ready, qb * HEADS + HEADS - 1)
                        nc.tensor.matmul(report_ps, v_one[:, 0, 0, HD:HD + 1], report[:], start=True, stop=True).then_inc(report_summed, 1)
                    weigh(qb, h, len(groups) - 1)


def phase_out_2(nc, sem, xf, mix_t, p_t, w_out, gate_row, out):
    with ExitStack() as ctx:
        al = Alloc(nc, ctx)
        w_raw = al.sb("oc_w_raw", [P, 2, DM])
        w_hi = al.sb("oc_w_hi", [P, KC, DM], F32R)
        w_lo = al.sb("oc_w_lo", [P, KC, DM], F32R)
        m_raw = al.sb("oc_m_raw", [P, 2, KC, P])
        g_raw = al.sb("oc_g_raw", [P, 2, KC, P])
        m_hi = al.sb("oc_m_hi", [P, 2, KC, P], F32R)
        m_lo = al.sb("oc_m_lo", [P, 2, KC, P], F32R)
        xin = al.sb("oc_x", [P, 2, DM])
        y = al.sb("oc_y", [P, 2, DM])
        gate = al.sb("oc_gate", [P, DM])
        acc = [al.ps(f"oc_acc{j}", [P, DM]) for j in range(2)]
        w_in = [sem(f"oc_w_in{j}") for j in range(2)]
        m_in = [sem(f"oc_m_in{j}") for j in range(2)]
        x_in = [sem(f"oc_x_in{j}") for j in range(2)]
        y_out = [sem(f"oc_y_out{j}") for j in range(2)]
        gate_in, w_hi_done, w_lo_done, gated = sem("oc_gate_in"), sem("oc_w_hi"), sem("oc_w_lo"), sem("oc_gated")
        m_hi_done, m_lo_done, product, scaled, added = sem("oc_m_hi"), sem("oc_m_lo"), sem("oc_product"), sem("oc_scaled"), sem("oc_added")
        w_v = w_out.rearrange("(k p) n -> k p n", p=P)
        m_v = mix_t.rearrange("(k p) (t n) -> t p k n", p=P, n=P)
        gp_v = p_t[ROW_GP:ROW_GP + 512, :].rearrange("(k p) (t n) -> t p k n", p=P, n=P)
        ga_v = p_t[ROW_GA:ROW_GA + 512, :].rearrange("(k p) (t n) -> t p k n", p=P, n=P)
        x_v = xf.rearrange("(t p) d -> t p d", p=P)
        o_v = out.rearrange("(t p) d -> t p d", p=P)
        PAIRS = TILES // 2
        HALF = KC // 2
        block = ctx.enter_context(nc.Block())

        @block.sync
        def _(sp):
            def load(tile, j):
                sp.dma_start(m_raw[:, j], tile(m_v, "a p k n -> (a p) k n")).then_inc(m_in[j], 16)
                sp.dma_start(g_raw[:, j, 0:HALF], tile(gp_v, "a p k n -> (a p) k n")).then_inc(m_in[j], 16)
                sp.dma_start(g_raw[:, j, HALF:], tile(ga_v, "a p k n -> (a p) k n")).then_inc(m_in[j], 16)

            def load_x(tile, j):
                sp.dma_start(xin[:, j], tile(x_v, "a p d -> (a p) d")).then_inc(x_in[j], 16)

            for j in range(2):
                load(lambda v, _: v[j], j)
            for k in range(KC):
                if k >= 2:
                    sp.wait_ge(w_lo_done, k - 1)
                sp.dma_start(w_raw[:, k % 2], w_v[k]).then_inc(w_in[k % 2], 16)
            sp.dma_start(gate[:], gate_row.partition_broadcast(P)).then_inc(gate_in, 16)
            for j in range(2):
                load_x(lambda v, _: v[j], j)
            with sp.Fori(0, PAIRS - 1) as i:
                for j in range(2):
                    sp.wait_ge(m_lo_done, i * 2 + (j + 1))
                    load(lambda v, r: v[bass.ds(i * 2 + (j + 2), 1)].rearrange(r), j)
                    sp.wait_ge(added, i * 2 + (j + 1))
                    sp.dma_start(o_v[bass.ds(i * 2 + j, 1)].rearrange("a p d -> (a p) d"), y[:, j]).then_inc(y_out[j], 16)
                    load_x(lambda v, r: v[bass.ds(i * 2 + (j + 2), 1)].rearrange(r), j)
            for j in range(2):
                sp.wait_ge(added, TILES - 1 + j)
                sp.dma_start(o_v[TILES - 2 + j], y[:, j]).then_inc(y_out[j], 16)
            for j in range(2):
                sp.wait_ge(y_out[j], 16 * PAIRS + 16)

        @block.scalar
        def _(act):
            for k in range(KC):
                act.wait_ge(w_in[k % 2], 16 * (k // 2 + 1))
                nc.scalar.activation(w_hi[:, k], w_raw[:, k % 2], ACT.Copy).then_inc(w_hi_done, 1)

            with act.Fori(0, PAIRS) as i:
                for j in range(2):
                    act.wait_ge(gated, i * 2 + (j + 1))
                    act.wait_ge(product, i * 2 + (j + 1))
                    nc.scalar.activation(m_hi[:, j], m_raw[:, j], ACT.Copy).then_inc(m_hi_done, 1)

        @block.vector
        def _(dve):
            for k in range(KC):
                dve.wait_ge(w_hi_done, k + 1)
                nc.vector.tensor_tensor(w_lo[:, k], w_raw[:, k % 2], w_hi[:, k].bitcast(F32), ALU.subtract).then_inc(w_lo_done, 1)

            def gates(t, j):
                dve.wait_ge(m_in[j], (t - j) * 24 + 48)
                nc.vector.tensor_tensor(m_raw[:, j], m_raw[:, j], g_raw[:, j], ALU.mult).then_inc(gated, 1)
                dve.wait_ge(gated, t + 1)
                dve.wait_ge(m_hi_done, t + 1)
                nc.vector.tensor_tensor(m_lo[:, j], m_raw[:, j], m_hi[:, j].bitcast(F32), ALU.subtract).then_inc(m_lo_done, 1)

            def finish(t, j):
                dve.wait_ge(product, t + 3)
                dve.wait_ge(y_out[j], (t - j) * 8 + 16)
                nc.vector.tensor_tensor(y[:, j], acc[j][:], gate[:], ALU.mult).then_inc(scaled, 1)
                dve.wait_ge(scaled, t + 3)
                dve.wait_ge(x_in[j], (t - j) * 8 + 16)
                nc.vector.tensor_tensor(y[:, j], y[:, j], xin[:, j], ALU.add).then_inc(added, 1)

            dve.wait_ge(gate_in, 16)
            for j in range(2):
                gates(j, j)
            with dve.Fori(0, PAIRS - 1) as i:
                for j in range(2):
                    finish(i * 2 + j, j)
                    gates(i * 2 + (j + 2), j)
            for j in range(2):
                finish(TILES - 2 + j, j)

        @block.tensor
        def _(pe):
            pe.sem_inc(product, 2)
            pe.sem_inc(scaled, 2)
            for j in range(2):
                pe.sem_inc(y_out[j], 16)
            pe.wait_ge(w_lo_done, KC)
            with pe.Fori(0, PAIRS) as i:
                for j in range(2):
                    pe.wait_ge(m_lo_done, i * 2 + (j + 1))
                    pe.wait_ge(scaled, i * 2 + (j + 1))
                    for half in range(2):
                        cols = slice(half * 512, half * 512 + 512)
                        for k in range(KC):
                            for n, (w, a) in enumerate(split_pass_list(w_hi, w_lo, m_hi, m_lo)):
                                ins = nc.tensor.matmul(acc[j][:, cols], a[:, j, k, :], w[:, k, cols],
                                                       start=(k == 0 and n == 0), stop=(k == KC - 1 and n == 2))
                    ins.then_inc(product, 1)


def program(nc, a):
    def dram(name, shape):
        return nc.dram_tensor(name, shape, F32, kind="Internal").ap()

    y_t, x1, xn_t, kvqg_t = dram("d_y_t", [DM, SEQ]), dram("d_x1", [SEQ, DM]), dram("d_xn_t", [DM, SEQ]), dram("d_kvqg_t", [4 * 512, SEQ])
    o_t, mod_row, xf = dram("d_o_t", [512, SEQ]), dram("d_mod_row", [3 * DM]), dram("d_xf", [SEQ, DM])
    p_t, rot_t, mix_t = dram("d_p_t", [D_PROJ, SEQ]), dram("d_rot_t", [ROT_ROWS, SEQ]), dram("d_mix_t", [DM, SEQ])
    @contextmanager
    def semaphores():
        taken = []

        def sem(name):
            taken.append(nc.alloc_semaphore(name=name))
            return taken[-1]

        yield sem
        nc.clear_and_free_semaphores(taken)
        nc.all_engine_barrier()

    def halves(ctx, name):
        al = Alloc(nc, ctx)
        return al.sb(name + "_hi", [P, KC, SEQ], F32R), al.sb(name + "_lo", [P, KC, SEQ], F32R)

    with ExitStack() as ctx:
        ident = Alloc(nc, ctx).sb("ident", [P, P])
        with ExitStack() as inner:
            xt = halves(inner, "h_a")
            with semaphores() as sem:
                phase_norm_x(nc, sem, a["x"][0], a["norm_a"][0], ident, *xt)
            with semaphores() as sem:
                phase_mixer(nc, sem, a["w_in_a"][0], a["conv_a"][0], *xt, y_t)
        with semaphores() as sem:
            phase_out_a(nc, sem, a["x"][0], a["w_out_a"][0], y_t, ident, x1, xn_t)
        with ExitStack() as inner, semaphores() as sem:
            w_q, w_g = a["w_in_b"][0][:, 0:512], a["w_in_b"][0][:, 512:]
            phase_project(nc, sem, "pb", [a["w_kv"], w_q, w_g], [a["norm_kv"], a["norm_b"][0], a["norm_b"][0]], *halves(inner, "h_b"),
                          kvqg_t, xn_t, a["c_2"][0], a["w_ada_2"][0], a["b_ada_2"][0], mod_row)
        with semaphores() as sem:
            phase_stick(nc, sem, kvqg_t, o_t, ident)
        with ExitStack() as inner:
            xt = halves(inner, "h_2")
            with semaphores() as sem:
                phase_out_b(nc, sem, x1, o_t, kvqg_t, a["w_out_b"][0], a["norm_f"], mod_row, a["norm_w_2"][0], ident, xf, *xt)
            with semaphores() as sem:
                phase_project_rotate(nc, sem, a["w_in_2"][0], *xt, a["w_pool_2"][0], a["pool_scale_2"][0], a["q_norm_w_2"][0], a["k_norm_w_2"][0],
                                     a["cos_t"], a["sin_t"], a["inv_count"], p_t, mix_t, rot_t)
        with semaphores() as sem:
            phase_select_attend(nc, sem, p_t, rot_t, a["bit_int"], a["bit_val"], a["half_powers"], a["rank_row"], mix_t, ident)
        with semaphores() as sem:
            phase_out_2(nc, sem, xf, mix_t, p_t, a["w_out_2"][0], mod_row[2 * DM:], a["out"][0])


INPUTS = ("x", "norm_a", "w_in_a", "conv_a", "w_out_a", "norm_kv", "w_kv", "norm_b", "w_in_b", "w_out_b", "norm_f", "c_2",
          "norm_w_2", "w_ada_2", "b_ada_2", "w_in_2", "q_norm_w_2", "k_norm_w_2", "w_pool_2", "pool_scale_2", "w_out_2")


def shape_constants():
    half = HD // 2
    freqs = np.float32(10000.0) ** (-np.arange(half, dtype=np.float32) / np.float32(half))
    angle = (np.arange(SEQ, dtype=np.float32)[:, None] * freqs[None, :]).astype(np.float32).T
    cos, sin = np.cos(angle), np.sin(angle)
    counts = np.minimum(np.arange(1, HALO + 1)[None, :], np.array(WINDOWS)[:, None]).astype(np.float32)
    bits = (1 << np.arange(30, -1, -1)).astype(np.int32)
    return {"cos_t": np.tile(cos, (4, 1)).astype(np.float32), "sin_t": np.concatenate([-sin, sin, -sin, sin]).astype(np.float32),
            "inv_count": (np.float32(1) / counts).astype(np.float32), "bit_int": bits, "bit_val": bits.astype(np.float32),
            "half_powers": (np.float32(0.5) ** np.arange(1, 11)).astype(np.float32), "rank_row": np.arange(17, dtype=np.float32)}


def kernel(**inputs):
    import concourse.bacc as bacc
    from concourse.bass_utils import run_bass_kernel_spmd

    nc = bacc.Bacc("TRN2", target_bir_lowering=False, num_devices=1)
    arrays = {name: np.ascontiguousarray(inputs[name]) for name in INPUTS}
    arrays.update(shape_constants())
    a = {name: nc.dram_tensor("in_" + name, v.shape, mybir.dt.from_np(v.dtype), kind="ExternalInput").ap() for name, v in arrays.items()}
    a["out"] = nc.dram_tensor("out", [1, SEQ, DM], F32, kind="ExternalOutput").ap()
    program(nc, a)
    r = run_bass_kernel_spmd(nc, [{"in_" + name: v for name, v in arrays.items()}], core_ids=[0])
    return r.results[0]["out"]
```
